# Optimizing a Trainium2 kernel written in Bass

```python
import functools
import jax, jax.numpy as jnp
from jax import lax
import numpy as np

D_MODEL = 1024
BATCH = 1
SEQ = 512
DEPTH = 2
DEC_BATCH = 8
DEC_SEQ = 1
PAST_LEN = 2048
PAGE_SIZE = 128

N_AB_LAYERS = (DEPTH + 1) // 2
N_C_LAYERS = DEPTH // 2
FOX_HEADS = 4
FOX_DIM = 128
FOX_W = FOX_HEADS * FOX_DIM
Q_BLOCK = 128
GDN_HEADS = 4
GDN_DK = 128
GDN_DV = 128
GDN_QK_W = GDN_HEADS * GDN_DK
GDN_V_W = GDN_HEADS * GDN_DV
GDN_CONV_DIM = 2 * GDN_QK_W + GDN_V_W
CONV_W = 4
GDN_CHUNK = 64
AB_SPLITS = (FOX_W, 2 * FOX_W, 3 * FOX_W, 3 * FOX_W + FOX_HEADS,
             3 * FOX_W + FOX_HEADS + GDN_CONV_DIM,
             3 * FOX_W + FOX_HEADS + GDN_CONV_DIM + GDN_V_W,
             3 * FOX_W + FOX_HEADS + GDN_CONV_DIM + GDN_V_W + GDN_HEADS)
AB_IN = 3 * FOX_W + FOX_HEADS + GDN_CONV_DIM + GDN_V_W + 2 * GDN_HEADS
AB_MIX_W = FOX_W + GDN_V_W
RET_HEADS = 8
RET_DK = 128
RET_DV = 256
RET_QK_W = RET_HEADS * RET_DK
RET_V_W = RET_HEADS * RET_DV
RET_CHUNK = 128
C_IN = 2 * RET_QK_W + 2 * RET_V_W
ROPE_BASE = 10000.0
D_FF = 2816
EPS = 1e-6
POOL_NUM = 5
POOL_DEN = 4

kernel_name = "fox_gdn_retention_macaron_step"

def rmsnorm(x, g):
    xf = x.astype(jnp.float32)
    y = xf * lax.rsqrt(jnp.mean(xf * xf, axis=-1, keepdims=True) + EPS)
    return (y * g.astype(jnp.float32)).astype(x.dtype)

def l2norm(x):
    xf = x.astype(jnp.float32)
    return xf * lax.rsqrt(jnp.sum(xf * xf, axis=-1, keepdims=True) + EPS)

def head_layernorm(x):
    xf = x.astype(jnp.float32)
    mu = jnp.mean(xf, axis=-1, keepdims=True)
    xc = xf - mu
    return xc * lax.rsqrt(jnp.mean(xc * xc, axis=-1, keepdims=True) + EPS)

def swiglu(x, w_gu, w_down):
    a, b = jnp.split(x @ w_gu, 2, axis=-1)
    return (jax.nn.silu(a) * b) @ w_down

def rope(x, pos):
    half = x.shape[-1] // 2
    freqs = ROPE_BASE ** (-jnp.arange(half, dtype=jnp.float32) / half)
    ang = pos[:, None] * freqs[None, :]
    cos = jnp.cos(ang)[None, :, None, :]
    sin = jnp.sin(ang)[None, :, None, :]
    xf = x.astype(jnp.float32)
    x1, x2 = xf[..., :half], xf[..., half:]
    return jnp.concatenate([x1 * cos - x2 * sin, x1 * sin + x2 * cos], axis=-1)

def causal_conv(u, prev, w):
    L = u.shape[1]
    full = jnp.concatenate([prev.astype(u.dtype), u], axis=1)
    out = full[:, 0:L] * w[0]
    for i in range(1, CONV_W):
        out = out + full[:, i:i + L] * w[i]
    return out, full[:, L:]

def run_chunks(step, S0, xs, chunk):
    L = xs[0].shape[1]
    C = chunk if L % chunk == 0 else L
    N = L // C
    split = lambda t: jnp.moveaxis(t.reshape(t.shape[0], N, C, *t.shape[2:]), 1, 0)
    S, o = lax.scan(step, S0, tuple(split(t) for t in xs))
    o = jnp.moveaxis(o, 0, 1)
    return o.reshape(o.shape[0], L, *o.shape[3:]), S

def fox_prompt(q, k, v, logf):
    Bn, L, H, Dh = q.shape
    nb = L // Q_BLOCK
    c = jnp.cumsum(logf, axis=1)
    cT = c.transpose(0, 2, 1)
    kpos = jnp.arange(L)
    qb = q.reshape(Bn, nb, Q_BLOCK, H, Dh).transpose(1, 0, 2, 3, 4)
    cb = c.reshape(Bn, nb, Q_BLOCK, H).transpose(1, 0, 3, 2)
    scale = FOX_DIM ** -0.5

    def block(args):
        qi, ci, bi = args
        s = jnp.einsum('bqhd,bkhd->bhqk', qi, k).astype(jnp.float32) * scale
        s = s + ci[..., :, None] - cT[:, :, None, :]
        qpos = bi * Q_BLOCK + jnp.arange(Q_BLOCK)
        s = jnp.where(kpos[None, :] <= qpos[:, None], s, -jnp.inf)
        p = jax.nn.softmax(s, axis=-1).astype(v.dtype)
        return jnp.einsum('bhqk,bkhd->bqhd', p, v)

    o = lax.map(block, (qb, cb, jnp.arange(nb)))
    return o.transpose(1, 0, 2, 3, 4).reshape(Bn, L, H, Dh)

def fox_sample(q, k, v, logf, k_cache, v_cache, lf_cache, layer, page_table):
    Bn, L, H, Dh = q.shape
    P = page_table.shape[1] * PAGE_SIZE
    kp = k_cache[layer, page_table].reshape(Bn, P, H, Dh)
    vp = v_cache[layer, page_table].reshape(Bn, P, H, Dh)
    lp = lf_cache[layer, page_table].reshape(Bn, P, H).astype(jnp.float32)
    rc = lax.cumsum(lp, axis=1, reverse=True) - lp
    cn = jnp.cumsum(logf, axis=1).transpose(0, 2, 1)
    scale = FOX_DIM ** -0.5
    s_past = (jnp.einsum('bqhd,bkhd->bhqk', q, kp).astype(jnp.float32) * scale
              + cn[..., :, None] + rc.transpose(0, 2, 1)[:, :, None, :])
    s_new = (jnp.einsum('bqhd,bkhd->bhqk', q, k).astype(jnp.float32) * scale
             + cn[..., :, None] - cn[..., None, :])
    i = jnp.arange(L)
    s_new = jnp.where(i[None, :] <= i[:, None], s_new, -jnp.inf)
    p = jax.nn.softmax(jnp.concatenate([s_past, s_new], axis=-1), axis=-1).astype(v.dtype)
    return (jnp.einsum('bhqk,bkhd->bqhd', p[..., :P], vp)
            + jnp.einsum('bhqk,bkhd->bqhd', p[..., P:], v))

def gdn_chunk(S, xs):
    q, k, v, g, beta = xs
    q, k, v = (t.transpose(0, 2, 1, 3) for t in (q, k, v))
    g, beta = g.transpose(0, 2, 1), beta.transpose(0, 2, 1)
    C = q.shape[2]
    i = jnp.arange(C)
    tril = i[:, None] >= i[None, :]
    strict = i[:, None] > i[None, :]
    gc = jnp.cumsum(g, axis=-1)
    gam = jnp.exp(jnp.where(tril, gc[..., :, None] - gc[..., None, :], -jnp.inf))
    kb = k * beta[..., None]
    A = jnp.where(strict, jnp.einsum('bhid,bhjd->bhij', kb, k) * gam, 0.0)
    M = A + jnp.eye(C, dtype=jnp.float32)
    rhs = jnp.concatenate([v * beta[..., None], kb * jnp.exp(gc)[..., None]], axis=-1)
    X = lax.linalg.triangular_solve(M, rhs, left_side=True, lower=True, unit_diagonal=True)
    u, w = X[..., :GDN_DV], X[..., GDN_DV:]
    v_new = u - jnp.einsum('bhck,bhkv->bhcv', w, S)
    attn = jnp.einsum('bhid,bhjd->bhij', q, k) * gam
    o = (jnp.einsum('bhck,bhkv->bhcv', q * jnp.exp(gc)[..., None], S)
         + jnp.einsum('bhij,bhjv->bhiv', attn, v_new))
    gl = gc[..., -1:]
    S_new = (S * jnp.exp(gl)[..., None]
             + jnp.einsum('bhck,bhcv->bhkv', k * jnp.exp(gl - gc)[..., None], v_new))
    return S_new, o.transpose(0, 2, 1, 3)

def gdn_mix(conv_in, z, a, b, conv_prev, S0, conv_w, A_log, dt_bias, norm_g):
    Bn, L, _ = conv_in.shape
    c, conv_new = causal_conv(conv_in, conv_prev, conv_w)
    c = jax.nn.silu(c)
    q, k, v = jnp.split(c, (GDN_QK_W, 2 * GDN_QK_W), axis=-1)
    q = l2norm(q.reshape(Bn, L, GDN_HEADS, GDN_DK)) * GDN_DK ** -0.5
    k = l2norm(k.reshape(Bn, L, GDN_HEADS, GDN_DK))
    v = v.reshape(Bn, L, GDN_HEADS, GDN_DV).astype(jnp.float32)
    g = -jnp.exp(A_log.astype(jnp.float32)) * jax.nn.softplus(a.astype(jnp.float32) + dt_bias.astype(jnp.float32))
    beta = jax.nn.sigmoid(b.astype(jnp.float32))
    o, S_new = run_chunks(gdn_chunk, S0.astype(jnp.float32), (q, k, v, g, beta), GDN_CHUNK)
    o = rmsnorm(o, norm_g) * jax.nn.silu(z.reshape(Bn, L, GDN_HEADS, GDN_DV).astype(jnp.float32))
    return o.reshape(Bn, L, GDN_V_W), conv_new, S_new

def ab_mixer(u, layer, past, w_in, w_out, b_f, conv_w, A_log, dt_bias, norm_g):
    Bn, L, _ = u.shape
    fq, fk, fv, ff, gconv, gz, ga, gb = jnp.split(u @ w_in, AB_SPLITS, axis=-1)
    heads = lambda t: t.reshape(Bn, L, FOX_HEADS, FOX_DIM)
    fq, fk, fv = heads(fq), heads(fk), heads(fv)
    logf = jax.nn.log_sigmoid((ff + b_f).astype(jnp.float32))
    if past is None:
        fo = fox_prompt(fq, fk, fv, logf)
        conv_prev = jnp.zeros((Bn, CONV_W - 1, GDN_CONV_DIM), u.dtype)
        S0 = jnp.zeros((Bn, GDN_HEADS, GDN_DK, GDN_DV), jnp.float32)
    else:
        k_cache, v_cache, lf_cache, page_table, conv_prev, S0 = past
        fo = fox_sample(fq, fk, fv, logf, k_cache, v_cache, lf_cache, layer, page_table)
    go, conv_new, S_new = gdn_mix(gconv, gz, ga, gb, conv_prev, S0, conv_w, A_log, dt_bias, norm_g)
    y = jnp.concatenate([fo.reshape(Bn, L, FOX_W), go.astype(fo.dtype)], axis=-1) @ w_out
    return y, (fk, fv, logf, conv_new, S_new)

def ret_chunk(S, xs, lg):
    q, k, v = (t.transpose(0, 2, 1, 3) for t in xs)
    C = q.shape[2]
    i = jnp.arange(C, dtype=jnp.float32)
    diff = i[:, None] - i[None, :]
    dmat = jnp.exp(jnp.where(diff[None] >= 0, diff[None] * lg[:, None, None], -jnp.inf))
    inner = jnp.einsum('bhij,bhjv->bhiv', jnp.einsum('bhid,bhjd->bhij', q, k) * dmat[None], v)
    cross = jnp.einsum('bhck,bhkv->bhcv', q * jnp.exp(lg[:, None] * (i[None, :] + 1.0))[None, :, :, None], S)
    S_new = (S * jnp.exp(lg * C)[None, :, None, None]
             + jnp.einsum('bhck,bhcv->bhkv', k * jnp.exp(lg[:, None] * (C - 1.0 - i[None, :]))[None, :, :, None], v))
    return S_new, (inner + cross).transpose(0, 2, 1, 3)

def ret_mixer(u, pos, S0, w_in, w_out, gnorm):
    Bn, L, _ = u.shape
    q, k, v, gate = jnp.split(u @ w_in, (RET_QK_W, 2 * RET_QK_W, 2 * RET_QK_W + RET_V_W), axis=-1)
    q = rope(q.reshape(Bn, L, RET_HEADS, RET_DK), pos)
    k = rope(k.reshape(Bn, L, RET_HEADS, RET_DK), pos) * RET_DK ** -0.5
    v = v.reshape(Bn, L, RET_HEADS, RET_DV).astype(jnp.float32)
    if S0 is None:
        S0 = jnp.zeros((Bn, RET_HEADS, RET_DK, RET_DV), jnp.float32)
    lg = jnp.log(1.0 - jnp.exp2(-5.0 - jnp.arange(RET_HEADS, dtype=jnp.float32)))
    o, S_new = run_chunks(functools.partial(ret_chunk, lg=lg), S0.astype(jnp.float32), (q, k, v), RET_CHUNK)
    o = head_layernorm(o).reshape(Bn, L, RET_V_W) * gnorm
    y = (jax.nn.silu(gate) * o.astype(gate.dtype)) @ w_out
    return y, S_new

def setup_inputs(seed: int = 0) -> dict:
    key = jax.random.key(seed)
    ks = iter(jax.random.split(key, 32))
    f32 = jnp.float32
    nrm = lambda shape, scale: jax.random.normal(next(ks), shape, f32) * scale
    n_pages = PAST_LEN // PAGE_SIZE
    n_pool = DEC_BATCH * n_pages * POOL_NUM // POOL_DEN
    x_prompt = nrm((BATCH, SEQ, D_MODEL), 1.0)
    x_sample = nrm((DEC_BATCH, DEC_SEQ, D_MODEL), 1.0)
    cache_fox_k = nrm((N_AB_LAYERS, n_pool, PAGE_SIZE, FOX_HEADS, FOX_DIM), 1.0)
    cache_fox_v = nrm((N_AB_LAYERS, n_pool, PAGE_SIZE, FOX_HEADS, FOX_DIM), 1.0)
    cache_fox_logf = jax.nn.log_sigmoid(nrm((N_AB_LAYERS, n_pool, PAGE_SIZE, FOX_HEADS), 1.0) + 9.0)
    page_table = jax.random.permutation(next(ks), n_pool)[:DEC_BATCH * n_pages].reshape(DEC_BATCH, n_pages).astype(jnp.int32)
    state_gdn_conv = nrm((N_AB_LAYERS, DEC_BATCH, CONV_W - 1, GDN_CONV_DIM), 1.0)
    state_gdn_S = nrm((N_AB_LAYERS, DEC_BATCH, GDN_HEADS, GDN_DK, GDN_DV), 0.1)
    state_ret_S = nrm((N_C_LAYERS, DEC_BATCH, RET_HEADS, RET_DK, RET_DV), 0.5)
    norm_g = 1.0 + nrm((DEPTH, 3, D_MODEL), 0.02)
    final_norm_g = 1.0 + nrm((D_MODEL,), 0.02)
    ffn_w_gu = nrm((DEPTH, 2, D_MODEL, 2 * D_FF), D_MODEL ** -0.5)
    ffn_w_down = nrm((DEPTH, 2, D_FF, D_MODEL), D_FF ** -0.5)
    ab_w_in = nrm((N_AB_LAYERS, D_MODEL, AB_IN), D_MODEL ** -0.5)
    ab_w_out = nrm((N_AB_LAYERS, AB_MIX_W, D_MODEL), AB_MIX_W ** -0.5)
    fox_b_f = 5.0 + nrm((N_AB_LAYERS, FOX_HEADS), 0.5)
    gdn_conv_w = nrm((N_AB_LAYERS, CONV_W, GDN_CONV_DIM), CONV_W ** -0.5)
    gdn_A_log = jnp.log(jax.random.uniform(next(ks), (N_AB_LAYERS, GDN_HEADS), f32, 1.0, 16.0))
    dt = jnp.exp(jax.random.uniform(next(ks), (N_AB_LAYERS, GDN_HEADS), f32, np.log(1e-3), np.log(1e-1)))
    gdn_dt_bias = dt + jnp.log(-jnp.expm1(-dt))
    gdn_norm_g = 1.0 + nrm((N_AB_LAYERS, GDN_DV), 0.02)
    c_w_in = nrm((N_C_LAYERS, D_MODEL, C_IN), D_MODEL ** -0.5)
    c_w_out = nrm((N_C_LAYERS, RET_V_W, D_MODEL), RET_V_W ** -0.5)
    ret_norm_g = 1.0 + nrm((N_C_LAYERS, RET_V_W), 0.02)
    return {"x_prompt": x_prompt, "x_sample": x_sample,
            "cache_fox_k": cache_fox_k, "cache_fox_v": cache_fox_v, "cache_fox_logf": cache_fox_logf,
            "page_table": page_table, "state_gdn_conv": state_gdn_conv, "state_gdn_S": state_gdn_S,
            "state_ret_S": state_ret_S, "norm_g": norm_g, "final_norm_g": final_norm_g,
            "ffn_w_gu": ffn_w_gu, "ffn_w_down": ffn_w_down, "ab_w_in": ab_w_in, "ab_w_out": ab_w_out,
            "fox_b_f": fox_b_f, "gdn_conv_w": gdn_conv_w, "gdn_A_log": gdn_A_log, "gdn_dt_bias": gdn_dt_bias,
            "gdn_norm_g": gdn_norm_g, "c_w_in": c_w_in, "c_w_out": c_w_out, "ret_norm_g": ret_norm_g}

def reference(x_prompt, x_sample, cache_fox_k, cache_fox_v, cache_fox_logf, page_table,
              state_gdn_conv, state_gdn_S, state_ret_S, norm_g, final_norm_g, ffn_w_gu, ffn_w_down,
              ab_w_in, ab_w_out, fox_b_f, gdn_conv_w, gdn_A_log, gdn_dt_bias, gdn_norm_g,
              c_w_in, c_w_out, ret_norm_g):
    xp, xs = x_prompt, x_sample
    past_len = page_table.shape[1] * PAGE_SIZE
    pos_p = jnp.arange(xp.shape[1], dtype=jnp.float32)
    pos_s = past_len + jnp.arange(xs.shape[1], dtype=jnp.float32)
    fkp, fvp, flp, fks, fvs, fls = [], [], [], [], [], []
    gcp, gsp, gcs, gss = [], [], [], []
    rsp, rss = [], []
    for li in range(DEPTH):
        g_ffa, g_mix, g_ffb = norm_g[li, 0], norm_g[li, 1], norm_g[li, 2]
        xp = xp + 0.5 * swiglu(rmsnorm(xp, g_ffa), ffn_w_gu[li, 0], ffn_w_down[li, 0])
        xs = xs + 0.5 * swiglu(rmsnorm(xs, g_ffa), ffn_w_gu[li, 0], ffn_w_down[li, 0])
        j = li // 2
        if li % 2 == 0:
            params = (ab_w_in[j], ab_w_out[j], fox_b_f[j], gdn_conv_w[j], gdn_A_log[j], gdn_dt_bias[j], gdn_norm_g[j])
            mp, (k_p, v_p, lf_p, conv_p, S_p) = ab_mixer(rmsnorm(xp, g_mix), j, None, *params)
            past = (cache_fox_k, cache_fox_v, cache_fox_logf, page_table, state_gdn_conv[j], state_gdn_S[j])
            ms, (k_s, v_s, lf_s, conv_s, S_s) = ab_mixer(rmsnorm(xs, g_mix), j, past, *params)
            fkp.append(k_p); fvp.append(v_p); flp.append(lf_p)
            fks.append(k_s); fvs.append(v_s); fls.append(lf_s)
            gcp.append(conv_p); gsp.append(S_p); gcs.append(conv_s); gss.append(S_s)
        else:
            mp, R_p = ret_mixer(rmsnorm(xp, g_mix), pos_p, None, c_w_in[j], c_w_out[j], ret_norm_g[j])
            ms, R_s = ret_mixer(rmsnorm(xs, g_mix), pos_s, state_ret_S[j], c_w_in[j], c_w_out[j], ret_norm_g[j])
            rsp.append(R_p); rss.append(R_s)
        xp = xp + mp.astype(xp.dtype)
        xs = xs + ms.astype(xs.dtype)
        xp = xp + 0.5 * swiglu(rmsnorm(xp, g_ffb), ffn_w_gu[li, 1], ffn_w_down[li, 1])
        xs = xs + 0.5 * swiglu(rmsnorm(xs, g_ffb), ffn_w_gu[li, 1], ffn_w_down[li, 1])
    y_prompt = rmsnorm(xp, final_norm_g)
    y_sample = rmsnorm(xs, final_norm_g)
    return (y_prompt, y_sample,
            jnp.stack(fkp), jnp.stack(fvp), jnp.stack(flp),
            jnp.stack(fks), jnp.stack(fvs), jnp.stack(fls),
            jnp.stack(gcp), jnp.stack(gsp), jnp.stack(gcs), jnp.stack(gss),
            jnp.stack(rsp), jnp.stack(rss))


_drawn_inputs = setup_inputs


def setup_inputs(seed=0):
    import zlib

    import numpy as np

    out = dict(_drawn_inputs(seed))
    spreads = {}
    factors = {'cache_fox_logf': 64.0,
     'final_norm_g': 8.348,
     'gdn_norm_g': 5.54,
     'ret_norm_g': 21.703,
     'cache_fox_k': 3.567,
     'cache_fox_v': 2.908}
    for name, (base, spread) in spreads.items():
        noise = np.random.default_rng([zlib.crc32(name.encode()), seed]).standard_normal(out[name].shape)
        drawn = base * np.exp(spread * noise) if base else spread * noise
        out[name] = __import__('jax').numpy.asarray(drawn.astype(out[name].dtype))
    for name, factor in factors.items():
        out[name] = (out[name] * factor).astype(out[name].dtype)
    return out
```

```python
from contextlib import ExitStack

import numpy as np

import concourse.bass as bass
from concourse import mybir

F32 = mybir.dt.float32
F32R = mybir.dt.float32r
I32 = mybir.dt.int32
ALU = mybir.AluOpType
ACT = mybir.ActivationFunctionType
AX = mybir.AxisListType.X

P = 128
D_MODEL, D_FF = 1024, 2816
SEQ, DEC = 512, 8
TOK = SEQ + DEC
HALF = TOK // 2
KD = D_MODEL // P
KF = D_FF // P
KH = KF // 2
NBLK = SEQ // P
FOX_HEADS = GDN_HEADS = 4
RET_HEADS, RET_DV = 8, 256
N_PAGES, N_POOL = 16, 160
CONV_W, CONV_CH = 4, 12
AB_CH = 28
EPS = 1e-6
LEVELS = 7
NEG = -1e30

CONST_PARTS = [("ident", P), ("maskneg", P), ("incl", P), ("later", P),
               ("levels", LEVELS * P), ("rope", 2 * TOK), ("dmat", RET_HEADS * P), ("qdec", RET_HEADS * P),
               ("kdec", RET_HEADS), ("chunkdec", RET_HEADS), ("stepdec", RET_HEADS)]
CONST_AT = {}
for _name, _n in CONST_PARTS:
    CONST_AT[_name] = (sum(n for _, n in CONST_PARTS[:len(CONST_AT)]), _n)
CONST_COLS = sum(n for _, n in CONST_PARTS)

PAR_NORM, PAR_FINAL, PAR_CONV, PAR_GDN, PAR_RET, PAR_ROWS = 0, 48, 56, 104, 105, 121
"""PAR_NORM + 8*n + d: norm n, chunk d; PAR_CONV + 12*tap + channel chunk; PAR_RET + 2*head + half."""

ROW_LOGF, ROW_GC, ROW_BETA, ROW_NEGC = 0, 32, 64, 96


def shape_constants():
    i = np.arange(P)
    f = np.float32
    c = np.zeros((P, CONST_COLS), f)

    def put(name, a):
        at, n = CONST_AT[name]
        c[:, at:at + n] = a.reshape(P, n)

    put("ident", np.eye(P, dtype=f))
    put("maskneg", np.where(i[None, :] > i[:, None], f(NEG), f(0)))
    put("incl", (i[None, :] >= i[:, None]).astype(f))
    put("later", (i[:, None] > i[None, :]).astype(f))
    lev = np.zeros((P, LEVELS, P), f)
    for n in range(LEVELS):
        s = 1 << n
        row, col = i[:, None], i[None, :]
        lev[:, n] = (row // (2 * s) == col // (2 * s)) & (row // s % 2 == 0) & (col // s % 2 == 1)
    put("levels", lev)
    half = P // 2
    freqs = f(10000.0) ** (-np.arange(half, dtype=f) / f(half))
    pos = np.concatenate([np.arange(SEQ, dtype=f), np.full(DEC, N_PAGES * P, f)])
    ang = (pos[:, None] * freqs[None, :].astype(f)).astype(f).T.astype(np.float64)
    cos, sin = np.cos(ang), np.sin(ang)
    cc, ss = np.concatenate([cos, cos]), np.concatenate([-sin, sin])
    put("rope", np.stack([cc, ss], 1).astype(f))
    lg = np.log(1.0 - 2.0 ** (-5.0 - np.arange(RET_HEADS)))
    diff = i[None, None, :] - i[:, None, None]
    put("dmat", np.where(diff >= 0, np.exp(np.maximum(diff, 0) * lg[None, :, None]), 0.0).astype(f))
    put("qdec", np.broadcast_to(np.exp(lg[None, :, None] * (i[None, None, :] + 1.0)), (P, RET_HEADS, P)).astype(f))
    put("kdec", np.exp(lg[None, :] * (P - 1.0 - i[:, None])).astype(f))
    put("chunkdec", np.broadcast_to(np.exp(lg * P), (P, RET_HEADS)).astype(f))
    put("stepdec", np.broadcast_to(np.exp(lg), (P, RET_HEADS)).astype(f))
    return c


class Steps:

    def __init__(self, sem, names):
        self.sem, self.names, self.next = sem, names, 0

    def done(self, instruction, name):
        assert self.names[self.next % len(self.names)] == name, (name, self.names[self.next % len(self.names)])
        self.next += 1
        instruction.then_inc(self.sem, 1)

    def value(self, name, turn=0):
        return turn * len(self.names) + (self.names.index(name) + 1)


def hold(engine, sem, value, least=1):
    if not isinstance(value, int):
        engine.wait_ge(sem, least)
    engine.wait_ge(sem, value)


def await_step(engine, steps, name, turn=0):
    hold(engine, steps.sem, steps.value(name, turn))


def trunk_program(nc, x_prompt, x_sample, cache_k, cache_v, cache_logf, page_table, state_conv, state_gdn, state_ret,
                  norm_g, final_g, w_gu, w_down, ab_in, ab_out, fox_b, conv_w, a_log, dt_bias, gdn_g, c_in, c_out,
                  ret_g, consts, y_prompt, y_sample, fk_prompt, fv_prompt, fl_prompt, fk_sample, fv_sample,
                  fl_sample, conv_prompt, gs_prompt, conv_sample, gs_sample, rs_prompt, rs_sample):
    ctx = ExitStack()
    base = nc.sbuf_base + (-nc.sbuf_base) % 32
    room = nc.sbuf_usable_end - base
    cursor = {"main": 0}

    def at(name, shape, offset, dt=F32):
        size = 4 * int(np.prod(shape[1:]))
        assert offset % 32 == 0 and offset + size <= room, (name, offset, size, room)
        return nc.alloc_sbuf_tensor_at(name, shape, dt, offset=base + offset)

    def new(name, shape, dt=F32, area="main"):
        offset = cursor[area]
        cursor[area] = offset + -(-4 * int(np.prod(shape[1:])) // 32) * 32
        return at(name, shape, offset, dt)

    with ctx:
        def sem(name):
            return ctx.enter_context(nc.semaphore(name))

        X = new("X", [P, KD, TOK])
        IDENT = new("IDENT", [P, P])
        ONES = new("ONES", [P, P])
        MASKNEG = new("MASKNEG", [P, P])
        INCL = new("INCL", [P, P])
        LATER = new("LATER", [P, P])
        PAR = new("PAR", [P, P])
        RSTD = new("RSTD", [P, TOK])
        SSQ = new("SSQ", [P, TOK])
        SQ = new("SQ", [P, TOK])
        EPSC = new("EPSC", [P, 4])
        ZERO = new("ZERO", [P, 1, 1])
        COLS = new("COLS", [P, 4])
        TA = new("TA", [P, TOK])
        TB = new("TB", [P, TOK])
        TH = new("TH", [P, TOK])
        ring_at = cursor["main"]
        RAW = new("RAW", [P, 2, KH, P])
        WHI = new("WHI", [P, 2, KH, P], F32R)
        WLO = new("WLO", [P, 2, KH, P], F32R)
        cursor["xs"] = cursor["main"]
        XH = new("XH", [P, KD, TOK], F32R, "xs")
        XL = new("XL", [P, KD, TOK], F32R, "xs")
        cursor["abwork"] = cursor["main"]
        cursor["h"] = cursor["xs"]
        cursor["load"] = cursor["proj"] = cursor["ret"] = cursor["fin"] = cursor["h"]
        HH = new("HH", [P, KF, TOK], F32R, "h")
        HL = new("HL", [P, KF, TOK], F32R, "h")
        cursor["ab"] = cursor["retc"] = cursor["h"]
        XTOK = new("XTOK", [P, NBLK, D_MODEL], area="load")
        XTOKS = new("XTOKS", [DEC, D_MODEL], area="load")
        PROWS = new("PROWS", [P, P], area="load")
        YF = new("YF", [P, KD, TOK], area="fin")
        YTOK = new("YTOK", [P, NBLK, D_MODEL], area="fin")
        YTOKS = new("YTOKS", [DEC, D_MODEL], area="fin")

        ACC = [ctx.enter_context(nc.psum_tensor(f"ACC{i}", [P, 2, 512], F32)) for i in range(4)]

        def bank(b, n=512):
            return ACC[b // 2][:, b % 2, 0:n]

        def halves(a):
            return a.rearrange("p (n t) -> p n t", n=2)

        consts_in = sem("consts_in")
        inputs_in = sem("inputs_in")
        cols_clear = sem("cols_clear")
        ones_set = sem("ones_set")
        raw_in = [sem("raw_in0"), sem("raw_in1")]
        zero_set = sem("zero_set")
        hi_split = sem("hi_split")
        split = sem("split")
        used = sem("used")
        tile_free = sem("tile_free")
        sq_ready = sem("sq_ready")
        ssq_ready = sem("ssq_ready")
        xh_ready = sem("xh_ready")
        xl_ready = sem("xl_ready")
        stat_done = sem("stat_done")
        std_ready = sem("std_ready")
        rstd_ready = sem("rstd_ready")
        act_ready = sem("act_ready")
        hfull_ready = sem("hfull_ready")
        hh_ready = sem("hh_ready")
        h_ready = sem("h_ready")
        stored = sem("stored")
        stores = [0]

        unit_at, tile_at = {}, {}
        u = 0
        t = KD
        for name, units, tiles in (("up0", 2 * KF, 2 * KF), ("down0", 2 * KD, KD), ("ab_in", AB_CH + 1, AB_CH + 1),
                                   ("ab_out", KD, KD), ("up1", 2 * KF, 2 * KF), ("down1", 2 * KD, KD),
                                   ("up2", 2 * KF, 2 * KF), ("down2", 2 * KD, KD), ("ret_in", 6 * RET_HEADS, 6 * RET_HEADS),
                                   ("ret_out", 2 * KD, KD), ("up3", 2 * KF, 2 * KF), ("down3", 2 * KD, KD)):
            unit_at[name], tile_at[name] = u, t
            u, t = u + units, t + tiles
        UPDATE = {"load": 0, "down0": 1, "ab_out": 2, "down1": 3, "down2": 4, "ret_out": 5, "down3": 6}
        NORM_OF = {"up0": 0, "ab_in": 1, "up1": 2, "up2": 3, "ret_in": 4, "up3": 5, "final": 6}
        SSQ_STEPS = KD + 1
        tile_at_update = [0] + [tile_at[n] for n in UPDATE if n != "load"]

        par_turned = sem("par_turned")
        par_ready = sem("par_ready")
        loaded_turned = sem("loaded_turned")
        x_part = sem("x_part")
        y_ready = sem("y_ready")
        final_turned = sem("final_turned")
        final_copied = Steps(sem("final_copied"), [f"tok{n}" for n in range(NBLK)] + ["sample"])
        LOOP_STORES = 0
        AB_Q, AB_K, AB_V, AB_CONV, AB_Z = 0, 4, 8, 12, 24
        PRJ = new("PRJ", [P, AB_CH, TOK], area="proj")
        MOH = new("MOH", [P, KD, TOK], F32R, "proj")
        MOL = new("MOL", [P, KD, TOK], F32R, "proj")
        LEV = new("LEV", [P, LEVELS, P], area="ab")
        R = new("R", [P, TOK], area="ab")
        RT = new("RT", [P, NBLK, P], area="ab")
        RTS = new("RTS", [DEC, P], area="ab")
        SC = new("SC", [P, DEC, N_PAGES, FOX_HEADS], area="ab")
        LF = new("LF", [P, DEC, N_PAGES, FOX_HEADS], area="ab")
        SUF = new("SUF", [P, DEC, N_PAGES, FOX_HEADS], area="ab")
        NDH = DEC * FOX_HEADS
        SN, MX, DEN, QKS = (new(n, [P, DEC, FOX_HEADS], area="ab") for n in ("SN", "MX", "DEN", "QKS"))
        OS = new("OS", [P, FOX_HEADS, DEC], area="ab")
        OT = new("OT", [P, FOX_HEADS, DEC], area="ab")
        MXC = new("MXC", [NDH, 1], area="ab")
        DG = new("DG", [NDH, NDH], area="ab")
        PT_SB = new("PT_SB", [1, DEC * N_PAGES], I32, "ab")
        cursor["fp"] = cursor["fs"] = cursor["gd"] = cursor["abwork"]
        QS, KS, VS = (new(n, [P, SEQ], area="fp") for n in ("QS", "KS", "VS"))
        SELH = new("SELH", [P, P], area="fp")
        KT, VT = (new(n, [P, NBLK, P], area="fp") for n in ("KT", "VT"))
        PROB = new("PROB", [P, 2, SEQ], area="fp")
        PTR = new("PTR", [P, 2, NBLK, P], area="fp")
        STAT = new("STAT", [P, 2, 4], area="fp")
        PAGES = new("PAGES", [P, 8, FOX_HEADS * P], area="fs")
        PROD = new("PROD", [P, 4, FOX_HEADS * P], area="fs")
        QTOK, KTOKS, VTOKS = (new(n, [DEC, FOX_HEADS * P], area="fs") for n in ("QTOK", "KTOKS", "VTOKS"))
        SELB = new("SELB", [DEC, P], area="fs")

        small_in = sem("small_in")
        cols_in = sem("cols_in")
        lev_in = sem("lev_in")
        pt_in = sem("pt_in")
        clear_r = sem("clear_r")
        gate_dve = Steps(sem("gate_dve"), ["z", "az", "t", "g", "logf", "c", "negc"] + [f"gc{n}" for n in range(NBLK)]
                         + ["gcs", "rt", "rts"])
        gate_act = Steps(sem("gate_act"), ["fac", "e", "l", "beta"])
        gate_pe = Steps(sem("gate_pe"), ["rt"])
        fp_pe = Steps(sem("fp_pe"), ["ktok", "vtok", "score0", "score1", "turn0", "pv0", "score2", "turn1", "pv1",
                                     "score3", "turn2", "pv2", "turn3", "pv3"])
        fp_act = Steps(sem("fp_act"), ["q", "k", "v", "sel", "ktok", "exp0", "exp1", "pt0", "exp2", "pt1", "exp3",
                                       "pt2", "pt3", "hi"])
        fp_dve = Steps(sem("fp_dve"), ["vtok", "max0", "neg0", "max1", "neg1", "rinv0", "norm0", "max2", "neg2",
                                       "rinv1", "norm1", "max3", "neg3", "rinv2", "norm2", "rinv3", "norm3", "lo"])
        fk_stored = sem("fk_stored")
        fv_stored = sem("fv_stored")
        kpage_in = [sem("kpage_in0"), sem("kpage_in1")]
        vpage_in = [sem("vpage_in0"), sem("vpage_in1")]
        lf_in = sem("lf_in")
        prod_done = sem("prod_done")
        sum_done = sem("sum_done")
        vbatch_done = sem("vbatch_done")
        selb_ready = sem("selb_ready")
        qb_ready = sem("qb_ready")
        vo_done = sem("vo_done")
        vo_copied = sem("vo_copied")
        fs_pe = Steps(sem("fs_pe"), ["tok", "later", "total", "cn", "snew", "turn", "max", "den"])
        fs_act = Steps(sem("fs_act"), ["qtok", "ktok", "vtok", "exp", "expn", "hi"])
        fs_dve = Steps(sem("fs_dve"), ["qk", "suf15"] + [f"suf{g}" for g in range(14, -1, -1)]
                       + ["scale", "addsuf", "addcn", "sn", "mx", "mxc", "dg", "m", "sub", "subn", "dn", "den", "rinv",
                          "norm", "normn", "vn", "add", "lo"])
        AB_UNIT, AB_TILE = unit_at["ab_in"], tile_at["ab_in"]
        AB_FREE = AB_TILE + AB_CH + 1 + 4
        SCALE = float(P) ** -0.5
        GQ, GK, GV = AB_CONV, AB_CONV + 4, AB_CONV + 8
        NJ = GDN_HEADS * DEC
        GCH = [P, GDN_HEADS, P]
        (KTS, VTS, GAM, EG, KBT, QET, AT, ATS, ATTN, XI, XIT, T1, VB, KBE, KDE, WT, VNEW, STATE) = (
            new(n, GCH, area="gd") for n in ("KTS", "VTS", "GAM", "EG", "KBT", "QET", "AT", "ATS", "ATTN", "XI", "XIT",
                                             "T1", "VB", "KBE", "KDE", "WT", "VNEW", "STATE"))
        SS = new("SS", [P, NJ, P], area="gd")
        assert cursor["gd"] <= cursor["abwork"] + 4 * (2 * KD + AB_CONV) * TOK
        CONVROWS = at("CONVROWS", [DEC * (CONV_W - 1), CONV_CH * P], cursor["abwork"])
        TAILS = at("TAILS", [DEC + CONV_W - 1, CONV_CH * P], cursor["abwork"] + 6144)
        PREV = at("PREV", [P, CONV_CH, DEC, CONV_W - 1], cursor["abwork"] + 2 * 6144)
        cursor["gs"] = cursor["abwork"]
        KQ = new("KQ", [P, NJ, 2], area="gs")
        KC, QKP, EGS, VN2, W1, W2 = (new(n, [P, GDN_HEADS, DEC], area="gs") for n in ("KC", "QKP", "EGS", "VN2", "W1", "W2"))
        BEQ = new("BEQ", [P, 3, NJ], area="gs")
        KTK, VTK = (new(n, [NJ, P], area="gs") for n in ("KTK", "VTK"))
        VBD = new("VBD", [NJ, 2, DEC, P], area="gs")
        KDC, EGC, BEGE = (new(n, [P, GDN_HEADS], area="ab") for n in ("KDC", "EGC", "BEGE"))

        tails_stored = sem("tails_stored")
        gdn_stored = sem("gdn_stored")
        convrows_in = sem("convrows_in")
        ss_in = sem("ss_in")
        gp_pe = Steps(sem("gp_pe"), ["prev", "tails"])
        gp_act = Steps(sem("gp_act"), ["prev", "tail0", "tail1", "tail2"])
        cv_dve = Steps(sem("cv_dve"), ["w3", "p1", "s0", "p2", "s1", "p3", "s2"])
        cv_act = sem("cv_act")
        ln_act = Steps(sem("ln_act"), ["sq0", "sq1", "std0", "std1"])
        ln_pe = Steps(sem("ln_pe"), ["sum0", "sum1"])
        ln_dve = Steps(sem("ln_dve"), ["inv0", "mul0", "inv1", "mul1"])
        gl_pe = Steps(sem("gl_pe"), ["gcb", "bb", "ktok", "vtok", "a", "qk"]
                      + [f"{w}{n}" for n in range(LEVELS) for w in (("t", "x", "xt") if n < LEVELS - 1 else ("t", "xt"))]
                      + ["u", "wt", "ws", "o", "s"])
        gl_act = Steps(sem("gl_act"), ["kts", "vts", "gam", "eg", "kdc", "egc"] + [f"t{n}" for n in range(LEVELS)]
                       + ["u", "wt", "o"])
        gl_dve = Steps(sem("gl_dve"), ["xi", "xit", "dt", "gd", "gamm", "kbt", "qet", "at", "attn", "bege", "vb", "kbe", "kd"]
                       + [f"{w}{n}" for n in range(LEVELS) for w in (("ats", "x", "xt") if n < LEVELS - 1 else ("ats", "xt"))]
                       + ["vn", "s"])
        state_clear = sem("state_clear")
        gs_pe = Steps(sem("gs_pe"), ["r", "bc", "kt", "vt"] + [f"up{h}" for h in range(GDN_HEADS)])
        gs_act = Steps(sem("gs_act"), ["egs", "beq", "kt", "vt"])
        gs_dve = Steps(sem("gs_dve"), ["kq0", "kq1", "kc", "qkp", "a1", "a2", "a3", "o1", "o2", "o3"]
                       + [f"{w}{h}" for h in range(GDN_HEADS) for w in ("bd", "s")])
        go_act = Steps(sem("go_act"), ["sq", "std", "hi"])
        go_pe = Steps(sem("go_pe"), ["sum"])
        go_dve = Steps(sem("go_dve"), ["inv", "norm", "gate", "lo"])
        FOX_END = fs_dve.value("lo")
        RCH = 2 * RET_HEADS
        RMOH = new("RMOH", [P, RCH, TOK], F32R, "ret")
        RMOL = new("RMOL", [P, RCH, TOK], F32R, "ret")
        QB = [new(f"QB{i}", [P, TOK], area="ret") for i in range(2)]
        KB = [new(f"KB{i}", [P, TOK], area="ret") for i in range(2)]
        VBH = [new(f"VBH{i}", [P, 2, TOK], area="ret") for i in range(2)]
        VTK_R = new("VTK_R", [P, NBLK, RET_DV], area="ret")
        cursor["retc"] = max(cursor["retc"], cursor["ret"])
        ROPE = new("ROPE", [P, 2, TOK], area="retc")
        DMAT = new("DMAT", [P, RET_HEADS, P], area="retc")
        QDEC = new("QDEC", [P, RET_HEADS, P], area="retc")
        DECS = new("DECS", [P, 3, RET_HEADS], area="retc")
        KD_ = SQ[:, 0:SEQ].rearrange("p (n d) -> p n d", n=NBLK)

        def ring_tail(name, n, shape):
            assert 4 * int(np.prod(shape[1:])) <= 4 * (KH - KD) * P
            return at(name, shape, ring_at + 4 * (n * KH + KD) * P)

        SALL = [ring_tail(f"SALL{n}", n + 2, [P, RET_DV]) for n in range(NBLK)]
        SSR = new("SSR", [P, DEC, RET_DV], area="retc")
        VSC = new("VSC", [P, 2, DEC], area="retc")
        WSC = new("WSC", [P, 2, DEC], area="retc")
        QSD, QKR = (new(n, [P, DEC], area="retc") for n in ("QSD", "QKR"))
        KVT = ring_tail("KVT", 0, [DEC, 3 * P])
        VBR = TH[0:DEC, 0:2 * RET_DV].rearrange("j (b v) -> j b v", b=2)
        ATT = TH

        ret_consts_in = sem("ret_consts_in")
        rp_act = Steps(sem("rp_act"), ["q", "k"])
        rp_dve = Steps(sem("rp_dve"), ["qc", "qs", "q", "kc", "ks", "k"])
        rm_pe = Steps(sem("rm_pe"), ["ktok", "v0", "v1", "a", "kv", "o", "cross", "mean", "tok", "r0", "r1", "var", "r2", "r3"])
        rm_act = Steps(sem("rm_act"), ["vt0", "vt1", "o0", "o1", "tk", "sq0", "sq1", "std", "si0", "hi0", "si1", "hi1"])
        rm_dve = Steps(sem("rm_dve"), ["kd", "att", "qd", "qsd", "qkp", "vsc", "s0", "s1", "s2", "s3", "ov", "os", "c0", "c1",
                                       "bd0", "bd1", "u0", "u1", "inv", "n0", "n1", "bd2", "bd3", "u2", "u3",
                                       "g0", "lo0", "g1", "lo1"])
        rss_in = sem("rss_in")
        rss_stored = sem("rss_stored")
        rsp_stored = sem("rsp_stored")
        RU, RTILE = unit_at["ret_in"], tile_at["ret_in"]

        def ret_first(turn):
            return 0 if isinstance(turn, int) and turn == 0 else 6 * turn - 2

        def ret_turns(engine, turn):
            turn(0, 0)
            with engine.Fori(0, RET_HEADS // 2 - 1) as i:
                turn(2 * i + 1, 1)
                turn(2 * i + 2, 0)
            turn(RET_HEADS - 1, 1)
            turn(RET_HEADS, 0)

        block = ctx.enter_context(nc.Block())

        @block.sync
        def _(sp):
            def store(to, of):
                stores[0] += 1
                sp.dma_start(to, of).then_inc(stored, 16)

            def load_unit(unit, slot, nk, source):
                hold(sp, split, unit + 1)
                sp.dma_start(RAW[:, slot, 0:nk, :], source).then_inc(raw_in[slot], 16)

            def load_up(f):
                w = w_gu[f // 2, f % 2].rearrange("(k p) c -> p k c", p=P)
                u0 = unit_at[f"up{f}"]
                with sp.Fori(0, KF // 2) as i:
                    for s in range(4):
                        col = (s % 2) * D_FF + P * (s // 2) + 2 * P * i
                        load_unit(u0 + 4 * i + s, (u0 + s) % 2, KD, w[:, :, bass.ds(col, P)])

            def load_down(f):
                w = w_down[f // 2, f % 2].rearrange("(s k p) c -> p s k c", p=P, k=KH)
                u0 = unit_at[f"down{f}"]
                with sp.Fori(0, KD // 2) as i:
                    for s in range(4):
                        load_unit(u0 + 4 * i + s, (u0 + s) % 2, KH,
                                  w[:, s % 2, :, bass.ds(2 * P * i + P * (s // 2), P)])

            sp.dma_start(PROWS[PAR_NORM:PAR_FINAL, :], norm_g.rearrange("l s (c p) -> (l s c) p", p=P)).then_inc(inputs_in, 16)
            sp.dma_start(PROWS[PAR_FINAL:PAR_CONV, :], final_g.rearrange("(c p) -> c p", p=P)).then_inc(inputs_in, 16)
            sp.dma_start(PROWS[PAR_CONV:PAR_GDN, :], conv_w[0].rearrange("w (c p) -> (w c) p", p=P)).then_inc(inputs_in, 16)
            sp.dma_start(PROWS[PAR_GDN:PAR_RET, :], gdn_g).then_inc(inputs_in, 16)
            sp.dma_start(PROWS[PAR_RET:PAR_ROWS, :], ret_g[0].rearrange("(c p) -> c p", p=P)).then_inc(inputs_in, 16)
            sp.dma_start(XTOKS[:, :], x_sample.rearrange("b o d -> (b o) d")).then_inc(inputs_in, 16)
            sp.dma_start(XTOK[:, :, :], x_prompt[0].rearrange("(n p) d -> p n d", p=P)).then_inc(inputs_in, 16)
            for tile, name in ((IDENT, "ident"), (MASKNEG, "maskneg"), (INCL, "incl"), (LATER, "later")):
                c0, n = CONST_AT[name]
                sp.dma_start(tile[:, :], consts[:, c0:c0 + n]).then_inc(consts_in, 16)
            for tile, src in ((COLS[ROW_LOGF:ROW_LOGF + 4, 0:1], fox_b), (COLS[ROW_GC:ROW_GC + 4, 0:1], dt_bias),
                              (COLS[ROW_GC:ROW_GC + 4, 1:2], a_log)):
                sp.wait_ge(cols_clear, 5)
                sp.dma_start(tile, src.rearrange("a h -> h a")).then_inc(cols_in, 16)
            c0, n = CONST_AT["levels"]
            sp.dma_start(LEV[:, :, :], consts[:, c0:c0 + n].rearrange("p (l c) -> p l c", l=LEVELS)).then_inc(lev_in, 16)
            sp.dma_start(PT_SB[:, :], page_table.rearrange("b (o g) -> o (b g)", o=1)).then_inc(pt_in, 16)
            load_up(0)
            load_down(0)
            abw = ab_in[0].rearrange("(k p) c -> p k c", p=P)
            for f0, turns, shift in ((AB_Q, 3, 0), (AB_CONV, 4, FOX_HEADS)):
                with sp.Fori(0, turns) as i:
                    for s in range(4):
                        load_unit(AB_UNIT + f0 + 4 * i + s, (AB_UNIT + s) % 2, KD,
                                  abw[:, :, bass.ds(P * (f0 + s) + shift + 4 * P * i, P)])
            slot = (AB_UNIT + AB_CH) % 2
            hold(sp, split, AB_UNIT + AB_CH + 1)
            for at_col, c0, dst_sem in ((ROW_LOGF, 3 * 512, raw_in[slot]), (ROW_GC, 3588, small_in), (ROW_BETA, 3592, small_in)):
                sp.dma_start(RAW[:, slot, 0:KD, at_col:at_col + 4], abw[:, :, c0:c0 + 4]).then_inc(dst_sem, 16)
            sp.wait_ge(gate_dve.sem, gate_dve.value("rt"))
            store(fl_prompt[0, 0].rearrange("(n p) h -> p n h", p=P), RT[:, :, ROW_LOGF:ROW_LOGF + 4])
            sp.wait_ge(gate_dve.sem, gate_dve.value("rts"))
            store(fl_sample.rearrange("a b o h -> (a b o) h"), RTS[:, ROW_LOGF:ROW_LOGF + 4])
            with sp.Fori(0, FOX_HEADS) as h:
                await_step(sp, fp_act, "ktok", h)
                sp.dma_start(fk_prompt[0, 0].rearrange("(n p) h d -> p n h d", p=P)[:, :, bass.ds(h, 1), :]
                             .rearrange("p n a d -> p n (a d)"), KT[:, :, :]).then_inc(fk_stored, 16)
                await_step(sp, fp_dve, "vtok", h)
                sp.dma_start(fv_prompt[0, 0].rearrange("(n p) h d -> p n h d", p=P)[:, :, bass.ds(h, 1), :]
                             .rearrange("p n a d -> p n (a d)"), VT[:, :, :]).then_inc(fv_stored, 16)
            sp.wait_ge(fk_stored, 16 * FOX_HEADS)
            sp.wait_ge(fv_stored, 16 * FOX_HEADS)
            sp.wait_ge(fs_act.sem, fs_act.value("ktok"))
            store(fk_sample[0].rearrange("b o h d -> (b o) (h d)"), KTOKS[:, :])
            sp.wait_ge(fs_act.sem, fs_act.value("vtok"))
            store(fv_sample[0].rearrange("b o h d -> (b o) (h d)"), VTOKS[:, :])
            sp.wait_ge(pt_in, 16)
            with sp.Fori(0, DEC) as b:
                for m in range(4):
                    hold(sp, prod_done, 4 * b + m + 1)
                    for g in range(4 * m, 4 * m + 4):
                        page = sp.value_load(PT_SB[0:1, bass.ds(N_PAGES * b + g, 1)], min_val=0, max_val=N_POOL - 1)
                        sp.dma_start(PAGES[:, g % 8, :], cache_k[0, bass.ds(page, 1)].rearrange("a t h d -> (a t) (h d)"))\
                          .then_inc(kpage_in[m % 2], 16)
                        sp.dma_start(LF[:, bass.ds(b, 1), g, :].rearrange("p a h -> p (a h)"),
                                     cache_logf[0, bass.ds(page, 1)].rearrange("a t h -> (a t) h")).then_inc(lf_in, 16)
            sp.wait_ge(prod_done, 4 * DEC + 2)
            with sp.Fori(0, DEC) as b:
                for m in range(4):
                    hold(sp, vbatch_done, 4 * b + m + 1)
                    for g in range(4 * m, 4 * m + 4):
                        page = sp.value_load(PT_SB[0:1, bass.ds(N_PAGES * b + g, 1)], min_val=0, max_val=N_POOL - 1)
                        sp.dma_start(PAGES[:, g % 8, :], cache_v[0, bass.ds(page, 1)].rearrange("a t h d -> (a t) (h d)"))\
                          .then_inc(vpage_in[m % 2], 16)
            sp.wait_ge(fs_dve.sem, FOX_END)
            sp.dma_start(CONVROWS[:, :], state_conv[0].rearrange("b w c -> (b w) c")).then_inc(convrows_in, 16)
            for h in range(GDN_HEADS):
                sp.dma_start(SS[:, h * DEC:(h + 1) * DEC, :], state_gdn[0][:, h].rearrange("b k v -> k b v")).then_inc(ss_in, 16)
            store(conv_sample[0][:, 0:CONV_W - 2, :], state_conv[0][:, 1:CONV_W - 1, :])
            sp.wait_ge(gp_act.sem, gp_act.value("tail2"))
            sp.dma_start(conv_prompt[0, 0], TAILS[0:CONV_W - 1, :]).then_inc(tails_stored, 16)
            sp.dma_start(conv_sample[0][:, CONV_W - 2, :], TAILS[CONV_W - 1:, :]).then_inc(tails_stored, 16)
            sp.wait_ge(tails_stored, 32)
            sp.wait_ge(gl_dve.sem, gl_dve.value("s", NBLK - 1))
            store(gs_prompt[0, 0].rearrange("h k v -> k h v"), STATE[:, :, :])
            for h in range(GDN_HEADS):
                sp.wait_ge(gs_dve.sem, gs_dve.value(f"s{h}"))
                store(gs_sample[0][:, h].rearrange("b k v -> k b v"), SS[:, h * DEC:(h + 1) * DEC, :])
            gdn_stores = stores[0]
            sp.wait_ge(stored, 16 * gdn_stores)
            sp.sem_inc(gdn_stored, 1)
            abo = ab_out[0].rearrange("(k p) c -> p k c", p=P)
            with sp.Fori(0, KD // 2) as i:
                for s in range(2):
                    load_unit(unit_at["ab_out"] + 2 * i + s, (unit_at["ab_out"] + s) % 2, KD,
                              abo[:, :, bass.ds(2 * P * i + P * s, P)])
            load_up(1)
            load_down(1)
            load_up(2)
            load_down(2)
            for tile, name in ((ROPE, "rope"), (DMAT, "dmat"), (QDEC, "qdec")):
                c0, n = CONST_AT[name]
                n = int(np.prod(tile.shape[1:]))
                sp.wait_ge(used, RU + 2)
                sp.dma_start(tile[:, :, :], consts[:, c0:c0 + n].rearrange("p (a c) -> p a c", a=tile.shape[1])).then_inc(ret_consts_in, 16)
            c0, _ = CONST_AT["kdec"]
            sp.dma_start(DECS[:, :, :], consts[:, c0:c0 + 3 * RET_HEADS].rearrange("p (a c) -> p a c", a=3)).then_inc(ret_consts_in, 16)
            cw = c_in[0].rearrange("(k p) c -> p k c", p=P)
            V0, G0 = 2 * RET_HEADS * P, 2 * RET_HEADS * P + RET_HEADS * RET_DV

            def load_turn(h, parity):
                first = ret_first(h)
                n = 0
                if parity is not None and not (isinstance(h, int) and h == RET_HEADS):
                    for col in (h * P, h * P + RET_HEADS * P, h * RET_DV + V0, h * RET_DV + V0 + P):
                        load_unit(RU + first + n, (RU + n) % 2, KD, cw[:, :, bass.ds(col, P)])
                        n += 1
                if not (isinstance(h, int) and h == 0):
                    for col in ((h - 1) * RET_DV + G0, (h - 1) * RET_DV + G0 + P):
                        load_unit(RU + first + n, (RU + n) % 2, KD, cw[:, :, bass.ds(col, P)])
                        n += 1

            ret_turns(sp, load_turn)
            sp.wait_ge(rsp_stored, 16 * RET_HEADS)
            sp.wait_ge(rss_stored, 16 * RET_HEADS)
            co = c_out[0].rearrange("(s k p) c -> p s k c", p=P, k=KD)
            with sp.Fori(0, KD // 2) as i:
                for s in range(4):
                    load_unit(unit_at["ret_out"] + 4 * i + s, (unit_at["ret_out"] + s) % 2, KD,
                              co[:, s % 2, :, bass.ds(2 * P * i + P * (s // 2), P)])
            load_up(3)
            load_down(3)
            sp.wait_ge(final_copied.sem, final_copied.value("tok3"))
            store(y_prompt[0].rearrange("(n p) d -> p n d", p=P), YTOK[:, :, :])
            sp.wait_ge(final_copied.sem, final_copied.value("sample"))
            store(y_sample.rearrange("b o d -> (b o) d"), YTOKS[:, :])
            sp.wait_ge(stored, 16 * stores[0] + 16 * LOOP_STORES)

        @block.gpsimd
        def _(pool):
            def split_unit(unit, slot, nk, raw_count):
                hold(pool, raw_in[slot], 16 * raw_count, 16)
                hold(pool, used, unit + 1)
                pool.tensor_tensor(WHI[:, slot, 0:nk, :], RAW[:, slot, 0:nk, :], ZERO[:, :].broadcast_to([P, nk, P]),
                                   ALU.add).then_inc(hi_split, 1)
                hold(pool, hi_split, unit + 1)
                pool.tensor_tensor(WLO[:, slot, 0:nk, :], RAW[:, slot, 0:nk, :], WHI[:, slot, 0:nk, :].bitcast(F32),
                                   ALU.subtract).then_inc(split, 1)

            def split_phase(name, nk, turns, body):
                u0 = unit_at[name]
                with pool.Fori(0, turns) as i:
                    for s in range(body):
                        split_unit(u0 + body * i + s, (u0 + s) % 2, nk, (body // 2) * i + (u0 + s) // 2 + 1)

            pool.sem_inc(split, 2)
            pool.memset(ZERO[:, :], 0.0).then_inc(zero_set, 1)
            pool.wait_ge(zero_set, 1)
            split_phase("up0", KD, KF // 2, 4)
            split_phase("down0", KH, KD // 2, 4)
            split_phase("ab_in", KD, AB_CH // 4, 4)
            pool.wait_ge(small_in, 32)
            split_unit(AB_UNIT + AB_CH, (AB_UNIT + AB_CH) % 2, KD, (AB_UNIT + AB_CH) // 2 + 1)
            split_phase("ab_out", KD, KD // 2, 2)
            split_phase("up1", KD, KF // 2, 4)
            split_phase("down1", KH, KD // 2, 4)
            split_phase("up2", KD, KF // 2, 4)
            split_phase("down2", KH, KD // 2, 4)
            def split_turn(h, parity):
                first = ret_first(h)
                units = 4 if isinstance(h, int) and h == 0 else 2 if isinstance(h, int) and h == RET_HEADS else 6
                for n in range(units):
                    half_count = (RU + first + n) // 2 if isinstance(h, int) else 3 * h - 1 + (RU + n) // 2
                    split_unit(RU + first + n, (RU + n) % 2, KD, half_count + 1)

            ret_turns(pool, split_turn)
            split_phase("ret_out", KD, KD // 2, 4)
            split_phase("up3", KD, KF // 2, 4)
            split_phase("down3", KH, KD // 2, 4)

        @block.tensor
        def _(pe):
            def project(unit, slot, nk, acc, hi, lo, k0=0, last=True, ready=None):
                hold(pe, split, unit + 3)
                for k in range(nk):
                    if ready is not None:
                        pe.wait_ge(ready[0], ready[1] + k0 + k)
                    first = k == 0 and k0 == 0
                    final = last and k == nk - 1
                    for w, a, opens, closes in ((WHI, hi, True, False), (WHI, lo, False, False), (WLO, hi, False, True)):
                        for n in range(2):
                            ins = pe.matmul(ACC[acc][:, n, 0:HALF], w[:, slot, k, :],
                                            a[:, k0 + k, n * HALF:(n + 1) * HALF],
                                            start=first and opens, stop=final and closes)
                ins.then_inc(used, 1)

            def statistics(r):
                pe.wait_ge(ssq_ready, SSQ_STEPS * (r + 1))
                for n in range(2):
                    ins = pe.matmul(ACC[3][:, n, 0:HALF], ONES[:, :], SSQ[:, n * HALF:(n + 1) * HALF], start=True, stop=True)
                ins.then_inc(stat_done, 1)

            def up(f):
                u0, t0, r = unit_at[f"up{f}"], tile_at[f"up{f}"], NORM_OF[f"up{f}"]
                with pe.Fori(0, KF // 2) as i:
                    for s in range(4):
                        hold(pe, tile_free, t0 + 4 * i + s + 1)
                        if s == 2:
                            pe.wait_ge(std_ready, r + 1)
                        project(u0 + 4 * i + s, (u0 + s) % 2, KD, s, XH, XL, ready=(xl_ready, KD * r + 1))

            def down(name, hi, lo, nk, per_chunk, ready):
                u0, t0 = unit_at[name], tile_at[name]
                with pe.Fori(0, KD // 2) as i:
                    for s in range(2):
                        hold(pe, tile_free, t0 + 2 * i + s + 3)
                        for m in range(per_chunk):
                            n = per_chunk * s + m
                            project(u0 + 2 * per_chunk * i + n, (u0 + n) % 2, nk, s, hi, lo, k0=nk * m,
                                    last=m == per_chunk - 1, ready=ready)

            pe.sem_inc(used, 2)
            pe.sem_inc(vbatch_done, 2)
            pe.wait_ge(consts_in, 64)
            pe.wait_ge(inputs_in, 7 * 16)
            pe.transpose(bank(7, PAR_ROWS), PROWS[0:PAR_ROWS, :], IDENT[0:PAR_ROWS, 0:PAR_ROWS]).then_inc(par_turned, 1)
            for d in range(KD):
                if d >= 4:
                    pe.wait_ge(tile_free, d + 1)
                elif d == 3:
                    pe.wait_ge(par_ready, 1)
                for n in range(NBLK):
                    pe.transpose(ACC[d % 4][:, 0, n * P:(n + 1) * P], XTOK[:, n, d * P:(d + 1) * P], IDENT[:, :])
                pe.transpose(ACC[d % 4][:, 1, 0:DEC], XTOKS[:, d * P:(d + 1) * P], IDENT[0:DEC, 0:DEC]).then_inc(loaded_turned, 1)
            pe.wait_ge(tile_free, KD + 4)
            statistics(0)
            up(0)
            down("down0", HH, HL, KH, 2, (h_ready, 1))
            statistics(1)
            with pe.Fori(0, AB_CH // 4) as i:
                for s in range(4):
                    hold(pe, tile_free, AB_TILE + 4 * i + s + 1)
                    if s == 3:
                        pe.wait_ge(std_ready, 2)
                    project(AB_UNIT + 4 * i + s, (AB_UNIT + s) % 2, KD, s, XH, XL, ready=(xl_ready, KD + 1))
            pe.wait_ge(tile_free, AB_TILE + AB_CH + 1)
            project(AB_UNIT + AB_CH, (AB_UNIT + AB_CH) % 2, KD, 0, XH, XL)

            pe.wait_ge(tile_free, AB_FREE)
            pe.wait_ge(gate_dve.sem, gate_dve.value("gcs"))
            pe.wait_ge(gate_act.sem, gate_act.value("beta"))
            for n in range(NBLK):
                pe.transpose(bank(2)[:, n * P:(n + 1) * P], R[:, n * P:(n + 1) * P], IDENT[:, :])
            gate_pe.done(pe.transpose(bank(3)[0:DEC, 0:P], R[:, SEQ:TOK], IDENT[:, :]), "rt")

            pe.wait_ge(gate_dve.sem, gate_dve.value("rts"))
            with pe.Fori(0, FOX_HEADS) as h:
                def score(q):
                    if q >= 2:
                        await_step(pe, fp_act, f"exp{q - 2}", h)
                    w = (q + 1) * P
                    pe.matmul(bank(q % 2, w), QS[:, q * P:w], PRJ[:, bass.ds(h + AB_K, 1), 0:w].rearrange("p a t -> p (a t)"),
                              start=True, stop=False)
                    pe.matmul(bank(q % 2, w), SELH[:, :], R[:, 0:w], start=False, stop=False)
                    fp_pe.done(pe.matmul(bank(q % 2)[:, q * P:w], IDENT[:, :], MASKNEG[:, :], start=False, stop=True), f"score{q}")

                def turn(q):
                    await_step(pe, fp_dve, f"norm{q}", h)
                    for k in range(q + 1):
                        ins = pe.transpose(bank(2 + q % 2)[:, k * P:(k + 1) * P], PROB[:, q % 2, k * P:(k + 1) * P], IDENT[:, :])
                    fp_pe.done(ins, f"turn{q}")

                def values(q):
                    await_step(pe, fp_act, f"pt{q}", h)
                    for k in range(q + 1):
                        ins = pe.matmul(bank(4)[:, q * P:(q + 1) * P], VT[:, k, :], PTR[:, q % 2, k, :], start=k == 0, stop=k == q)
                    fp_pe.done(ins, f"pv{q}")

                await_step(pe, fp_act, "sel", h)
                for n in range(NBLK):
                    ins = pe.transpose(bank(5)[:, n * P:(n + 1) * P], KS[:, n * P:(n + 1) * P], IDENT[:, :])
                fp_pe.done(ins, "ktok")
                for n in range(NBLK):
                    ins = pe.transpose(bank(6)[:, n * P:(n + 1) * P], VS[:, n * P:(n + 1) * P], IDENT[:, :])
                fp_pe.done(ins, "vtok")
                score(0)
                score(1)
                turn(0)
                values(0)
                score(2)
                turn(1)
                values(1)
                score(3)
                turn(2)
                values(2)
                turn(3)
                values(3)

            pe.wait_ge(fp_dve.sem, fp_dve.value("lo", FOX_HEADS - 1))
            for j, ch in enumerate((AB_Q, AB_K, AB_V)):
                for h in range(FOX_HEADS):
                    ins = pe.transpose(bank(j)[0:DEC, h * P:(h + 1) * P], PRJ[:, ch + h, SEQ:TOK], IDENT[:, :])
            fs_pe.done(ins, "tok")
            with pe.Fori(0, DEC) as b:
                hold(pe, selb_ready, b + 1)
                hold(pe, prod_done, 4 * b + 2)
                pe.matmul(bank(3), SELB[:, :], QTOK[:, :], start=True, stop=True).then_inc(qb_ready, 1)
            pe.wait_ge(lf_in, 16 * DEC * N_PAGES)
            lf = LF[:, :, :, :].rearrange("p b g h -> p (b g h)")
            fs_pe.done(pe.matmul(bank(0), LATER[:, :], lf, start=True, stop=True), "later")
            fs_pe.done(pe.matmul(bank(1), ONES[:, :], lf, start=True, stop=True), "total")
            for h in range(FOX_HEADS):
                ins = pe.matmul(bank(2)[:, h * DEC:(h + 1) * DEC], IDENT[:, ROW_LOGF + h:ROW_LOGF + h + 1].broadcast_to([P, P]), R[:, SEQ:TOK], start=True, stop=True)
            fs_pe.done(ins, "cn")
            pe.wait_ge(fs_dve.sem, fs_dve.value("qk"))
            fs_pe.done(pe.matmul(bank(4, NDH), ONES[:, :], QKS[:, :, :].rearrange("p b h -> p (b h)"), start=True, stop=True), "snew")
            pe.wait_ge(fs_dve.sem, fs_dve.value("mx"))
            fs_pe.done(pe.transpose(bank(3)[0:NDH, 0:P], MX[:, :, :].rearrange("p b h -> p (b h)"), IDENT[:, :]), "turn")
            pe.wait_ge(fs_dve.sem, fs_dve.value("dg"))
            fs_pe.done(pe.matmul(bank(5, NDH), ONES[0:NDH, :], DG[:, :], start=True, stop=True), "max")
            pe.wait_ge(fs_dve.sem, fs_dve.value("dn"))
            fs_pe.done(pe.matmul(bank(6, NDH), ONES[:, :], DEN[:, :, :].rearrange("p b h -> p (b h)"), start=True, stop=True), "den")
            pe.wait_ge(fs_dve.sem, fs_dve.value("norm"))
            with pe.Fori(0, DEC) as b:
                hold(pe, vo_copied, b, 0)
                for m in range(4):
                    hold(pe, vpage_in[m % 2], 64 * (2 * b + m // 2 + 1), 64)
                    for g in range(4 * m, 4 * m + 4):
                        for h in range(FOX_HEADS):
                            ins = pe.matmul(bank(7)[:, h:h + 1], PAGES[:, g % 8, h * P:(h + 1) * P],
                                            SC[:, bass.ds(b, 1), g, h:h + 1].rearrange("p a c -> p (a c)"),
                                            start=g == 0 and h == 0, stop=g == N_PAGES - 1, skip_group_check=True)
                    ins.then_inc(vbatch_done, 1)
            pe.wait_ge(fs_dve.sem, FOX_END)
            pe.wait_ge(convrows_in, 16)
            for c in range(CONV_CH):
                rows = DEC * (CONV_W - 1)
                ins = pe.transpose(bank(0)[:, c * rows:(c + 1) * rows], CONVROWS[:, c * P:(c + 1) * P], IDENT[0:rows, 0:rows])
            gp_pe.done(ins, "prev")
            for c in range(CONV_CH):
                ins = pe.transpose(bank(1 + c // 4)[0:DEC + CONV_W - 1, (c % 4) * P:(c % 4 + 1) * P],
                                   PRJ[:, AB_CONV + c, SEQ - CONV_W + 1:TOK], IDENT[:, :])
            gp_pe.done(ins, "tails")
            pe.wait_ge(gp_act.sem, gp_act.value("tail2"))
            with pe.Fori(0, GDN_HEADS) as h:
                for m, tile in enumerate((SQ, SSQ)):
                    await_step(pe, ln_act, f"sq{m}", h)
                    for n in range(2):
                        ins = pe.matmul(ACC[2 + m][:, n, 0:HALF], ONES[:, :], tile[:, n * HALF:(n + 1) * HALF], start=True, stop=True)
                    ln_pe.done(ins, f"sum{m}")
            def per_head(b, left, right, start=True, stop=True):
                for h in range(GDN_HEADS):
                    ins = pe.matmul(bank(b)[:, h * P:(h + 1) * P], left(h), right(h), start=start, stop=stop)
                return ins

            with pe.Fori(0, NBLK) as c:
                def rows_of(c=c):
                    return R[:, bass.ds(c * P, P)]

                hold(pe, gl_dve.sem, len(gl_dve.names) * c, 0)
                hold(pe, gl_act.sem, len(gl_act.names) * c, 0)
                gl_pe.done(per_head(0, lambda h: IDENT[:, ROW_GC + h:ROW_GC + h + 1].broadcast_to([P, P]), lambda h: rows_of()), "gcb")
                gl_pe.done(per_head(1, lambda h: IDENT[:, ROW_BETA + h:ROW_BETA + h + 1].broadcast_to([P, P]), lambda h: rows_of()), "bb")
                await_step(pe, gl_act, "vts", c)
                for b, tile, name in ((2, KTS, "ktok"), (3, VTS, "vtok")):
                    for h in range(GDN_HEADS):
                        ins = pe.transpose(bank(b)[:, h * P:(h + 1) * P], tile[:, h, :], IDENT[:, :])
                    gl_pe.done(ins, name)
                await_step(pe, gl_dve, "kbt", c)
                gl_pe.done(per_head(4, lambda h: KTS[:, h, :], lambda h: KBT[:, h, :]), "a")
                gl_pe.done(per_head(5, lambda h: KTS[:, h, :], lambda h: PRJ[:, GQ + h, bass.ds(c * P, P)]), "qk")
                for n in range(LEVELS):
                    await_step(pe, gl_dve, f"ats{n}", c)
                    gl_pe.done(per_head(6, lambda h: ATS[:, h, :], lambda h: XI[:, h, :]), f"t{n}")
                    await_step(pe, gl_act, f"t{n}", c)
                    if n < LEVELS - 1:
                        gl_pe.done(per_head(7, lambda h: XIT[:, h, :], lambda h: T1[:, h, :]), f"x{n}")
                    gl_pe.done(per_head(0, lambda h: T1[:, h, :], lambda h: XIT[:, h, :]), f"xt{n}")
                await_step(pe, gl_dve, f"xt{LEVELS - 1}", c)
                gl_pe.done(per_head(1, lambda h: XIT[:, h, :], lambda h: VB[:, h, :]), "u")
                gl_pe.done(per_head(2, lambda h: KBE[:, h, :], lambda h: XIT[:, h, :]), "wt")
                await_step(pe, gl_act, "wt", c)
                gl_pe.done(per_head(3, lambda h: WT[:, h, :], lambda h: STATE[:, h, :]), "ws")
                await_step(pe, gl_dve, "vn", c)
                for h in range(GDN_HEADS):
                    pe.matmul(bank(4)[:, h * P:(h + 1) * P], STATE[:, h, :], QET[:, h, :], start=True, stop=False)
                    ins = pe.matmul(bank(4)[:, h * P:(h + 1) * P], VNEW[:, h, :], ATTN[:, h, :], start=False, stop=True)
                gl_pe.done(ins, "o")
                gl_pe.done(per_head(5, lambda h: KDE[:, h, :], lambda h: VNEW[:, h, :]), "s")
            pe.wait_ge(gl_dve.sem, gl_dve.value("s", NBLK - 1))
            pe.wait_ge(gl_act.sem, gl_act.value("o", NBLK - 1))
            pe.wait_ge(ss_in, 16 * GDN_HEADS)
            pe.wait_ge(gs_dve.sem, gs_dve.value("qkp"))
            for j in range(NJ):
                ins = pe.matmul(bank(0)[:, 2 * j:2 * j + 2], SS[:, j, :], KQ[:, j, :], start=True, stop=True)
            gs_pe.done(ins, "r")
            for k, row in ((0, ROW_BETA), (1, ROW_GC)):
                for h in range(GDN_HEADS):
                    pe.matmul(bank(1)[:, k * NJ + h * DEC:k * NJ + (h + 1) * DEC], IDENT[:, row + h:row + h + 1].broadcast_to([P, P]),
                              R[:, SEQ:TOK], start=True, stop=True)
            gs_pe.done(pe.matmul(bank(1)[:, 2 * NJ:3 * NJ], ONES[:, :], QKP[:, :, :].rearrange("p h b -> p (h b)"), start=True, stop=True), "bc")
            gs_pe.done(pe.transpose(bank(2)[0:NJ, 0:P], KC[:, :, :].rearrange("p h b -> p (h b)"), IDENT[:, :]), "kt")
            pe.wait_ge(gs_dve.sem, gs_dve.value("a3"))
            gs_pe.done(pe.transpose(bank(3)[0:NJ, 0:P], VN2[:, :, :].rearrange("p h b -> p (h b)"), IDENT[:, :]), "vt")
            pe.wait_ge(gs_act.sem, gs_act.value("vt"))
            for h in range(GDN_HEADS):
                pe.wait_ge(gs_dve.sem, gs_dve.value(f"bd{h}"))
                for n in range(2):
                    ins = pe.matmul(ACC[2 + h % 2][:, n, :], KTK[:, :], VBD[:, h % 2, 4 * n:4 * n + 4, :].rearrange("j b d -> j (b d)"),
                                    start=True, stop=True)
                gs_pe.done(ins, f"up{h}")
            pe.wait_ge(gs_dve.sem, gs_dve.value(f"s{GDN_HEADS - 1}"))
            with pe.Fori(0, GDN_HEADS) as h:
                await_step(pe, go_act, "sq", h)
                for n in range(2):
                    ins = pe.matmul(ACC[0][:, n, 0:HALF], ONES[:, :], SQ[:, n * HALF:(n + 1) * HALF], start=True, stop=True)
                go_pe.done(ins, "sum")
            pe.wait_ge(go_dve.sem, go_dve.value("lo", GDN_HEADS - 1))
            with pe.Fori(0, KD // 2) as i:
                for s in range(2):
                    hold(pe, tile_free, tile_at["ab_out"] + 2 * i + s + 3)
                    project(unit_at["ab_out"] + 2 * i + s, (unit_at["ab_out"] + s) % 2, KD, s, MOH, MOL)
            statistics(2)
            up(1)
            down("down1", HH, HL, KH, 2, (h_ready, KF + 1))
            statistics(3)
            up(2)
            down("down2", HH, HL, KH, 2, (h_ready, 2 * KF + 1))
            statistics(4)
            pe.wait_ge(ret_consts_in, 64)

            def ret_turn(h, p):
                first, is_first, is_last = ret_first(h), isinstance(h, int) and h == 0, isinstance(h, int) and h == RET_HEADS
                g, o = h - 1, 1 - p
                count = [0]

                def tile():
                    n = count[0]
                    count[0] += 1
                    hold(pe, tile_free, RTILE + first + n + 3)
                    project(RU + first + n, (RU + n) % 2, KD, n % 2, XH, XL, ready=(xl_ready, KD * 4 + 1))

                def turned(b, source, name):
                    for n in range(NBLK):
                        ins = pe.transpose(bank(b)[:, n * P:(n + 1) * P], source(n), IDENT[:, :])
                    rm_pe.done(ins, name)

                def update(n):
                    await_step(pe, rm_dve, f"bd{n}", g)
                    if n >= 2:
                        await_step(pe, rm_dve, f"u{n - 2}", g)
                    rm_pe.done(pe.matmul(bank(6 + n % 2), KVT[:, 0:P], VBR[:, :, :].rearrange("j b v -> j (b v)"),
                                         start=True, stop=True), f"r{n}")

                if not is_last:
                    tile()
                if not is_first:
                    hold(pe, tile_free, RTILE + first + 4)
                    await_step(pe, rp_dve, "k", g)
                    hold(pe, rm_dve.sem, len(rm_dve.names) * g, 0)
                    hold(pe, rm_act.sem, len(rm_act.names) * g, 0)
                    turned(4, lambda n: KB[o][:, n * P:(n + 1) * P], "ktok")
                    turned(5, lambda n: VBH[o][:, 0, n * P:(n + 1) * P], "v0")
                    turned(6, lambda n: VBH[o][:, 1, n * P:(n + 1) * P], "v1")
                    for n in range(NBLK):
                        ins = pe.matmul(bank(7)[:, n * P:(n + 1) * P], KB[o][:, n * P:(n + 1) * P], QB[o][:, n * P:(n + 1) * P],
                                        start=True, stop=True)
                    rm_pe.done(ins, "a")
                if not is_last:
                    tile()
                if not is_first:
                    await_step(pe, rm_dve, "att", g)
                    await_step(pe, rm_act, "vt1", g)
                    for n in range(NBLK):
                        ins = pe.matmul(bank(6 + n // 2)[:, (n % 2) * RET_DV:(n % 2 + 1) * RET_DV], KD_[:, n, :], VTK_R[:, n, :],
                                        start=True, stop=True)
                    rm_pe.done(ins, "kv")
                if not is_last:
                    tile()
                if not is_first:
                    await_step(pe, rm_dve, "s3", g)
                    for v in range(2):
                        for n in range(NBLK):
                            out = bank(4 + v)[:, n * P:(n + 1) * P]
                            ins = pe.matmul(out, VTK_R[:, n, v * P:(v + 1) * P], ATT[:, n * P:(n + 1) * P], start=True, stop=n == 0)
                            if n > 0:
                                ins = pe.matmul(out, SALL[n - 1][:, v * P:(v + 1) * P], QB[o][:, n * P:(n + 1) * P],
                                                start=False, stop=True)
                    rm_pe.done(ins, "o")
                    hold(pe, rss_in, 16 * g + 16, 16)
                    for b in range(DEC):
                        for v in range(2):
                            pe.matmul(bank(6)[:, v * DEC + b:v * DEC + b + 1], SSR[:, b, v * P:(v + 1) * P], QSD[:, b:b + 1],
                                      start=True, stop=True)
                    rm_pe.done(pe.matmul(bank(6)[:, 2 * DEC:3 * DEC], ONES[:, :], QKR[:, :], start=True, stop=True), "cross")
                if not is_last:
                    tile()
                if not is_first:
                    await_step(pe, rm_act, "o1", g)
                    await_step(pe, rm_dve, "os", g)
                    for n in range(2):
                        for v in range(2):
                            ins = pe.matmul(ACC[2][:, n, 0:HALF], ONES[:, :], VBH[o][:, v, n * HALF:(n + 1) * HALF],
                                            start=v == 0, stop=v == 1)
                    rm_pe.done(ins, "mean")
                    pe.transpose(bank(7)[0:DEC, 0:P], KB[o][:, SEQ:TOK], IDENT[:, :])
                    for v in range(2):
                        ins = pe.transpose(bank(7)[0:DEC, (v + 1) * P:(v + 2) * P], VSC[:, v, :], IDENT[:, :])
                    rm_pe.done(ins, "tok")
                    await_step(pe, rm_act, "tk", g)
                    update(0)
                    update(1)
                    tile()
                    await_step(pe, rm_act, "sq1", g)
                    for n in range(2):
                        for v, squares in enumerate((SQ, SSQ)):
                            ins = pe.matmul(ACC[2][:, n, 0:HALF], ONES[:, :], squares[:, n * HALF:(n + 1) * HALF],
                                            start=v == 0, stop=v == 1)
                    rm_pe.done(ins, "var")
                    update(2)
                    update(3)
                    tile()

            ret_turns(pe, ret_turn)
            pe.wait_ge(rm_dve.sem, rm_dve.value("lo1", RET_HEADS - 1))
            down("ret_out", RMOH, RMOL, KD, 2, None)
            statistics(5)
            up(3)
            down("down3", HH, HL, KH, 2, (h_ready, 3 * KF + 1))
            statistics(6)
            for n in range(NBLK):
                for d in range(KD):
                    pe.wait_ge(y_ready, d + 1)
                    if n >= 2 and d == 0:
                        pe.wait_ge(final_copied.sem, n - 1)
                    ins = pe.transpose(ACC[n % 2][:, d // 4, (d % 4) * P:(d % 4 + 1) * P], YF[:, d, n * P:(n + 1) * P], IDENT[:, :])
                ins.then_inc(final_turned, 1)
            for d in range(KD):
                ins = pe.transpose(ACC[2][0:DEC, d // 4, (d % 4) * P:(d % 4 + 1) * P], YF[:, d, SEQ:TOK], IDENT[:, :])
            ins.then_inc(final_turned, 1)

        @block.scalar
        def _(act):
            def norm_chunk(r, d):
                n = KD * r + d
                hold(act, tile_free, tile_at_update[r] + d + 5)
                hold(act, ssq_ready, SSQ_STEPS * r + d + 1)
                act.activation(SQ[:, :], X[:, bass.ds(d, 1), :].rearrange("p a t -> p (a t)"), ACT.Square).then_inc(sq_ready, 1)
                act.activation(XH[:, bass.ds(d, 1), :].rearrange("p a t -> p (a t)"),
                               X[:, bass.ds(d, 1), :].rearrange("p a t -> p (a t)"), ACT.Identity,
                               scale=PAR[:, bass.ds(PAR_NORM + KD * r + d, 1)]).then_inc(xh_ready, 1)

            def norm_chunks(r):
                with act.Fori(0, KD) as d:
                    norm_chunk(r, d)

            def deviation(r):
                act.wait_ge(stat_done, r + 1)
                act.activation(halves(RSTD[:, :]), ACC[3][:, :, 0:HALF], ACT.Sqrt, bias=EPSC[:, 0:1],
                               scale=1.0 / D_MODEL).then_inc(std_ready, 1)

            def up(f):
                t0 = tile_at[f"up{f}"]
                with act.Fori(0, KF) as j:
                    hold(act, tile_free, t0 + 2 * j + 5)
                    act.activation(TA[:, :], TA[:, :], ACT.Silu).then_inc(act_ready, 1)
                    hold(act, hfull_ready, KF * f + j + 1)
                    act.activation(HH[:, bass.ds(j, 1), :].rearrange("p a t -> p (a t)"), TH[:, :], ACT.Copy).then_inc(hh_ready, 1)

            act.wait_ge(par_turned, 1)
            act.activation(PAR[:, 0:PAR_ROWS], bank(7, PAR_ROWS), ACT.Copy).then_inc(par_ready, 1)
            act.wait_ge(par_ready, 1)
            act.wait_ge(ones_set, 4)
            norm_chunks(0)
            deviation(0)
            up(0)
            norm_chunks(1)
            deviation(1)
            act.wait_ge(cols_in, 48)
            gate_act.done(act.activation(COLS[ROW_GC:ROW_GC + 4, 3:4], COLS[ROW_GC:ROW_GC + 4, 1:2], ACT.Exp), "fac")
            act.wait_ge(gate_dve.sem, gate_dve.value("az"))
            gate_act.done(act.activation(TB[:, :], TB[:, :], ACT.Exp, scale=-1.0), "e")
            act.wait_ge(gate_act.sem, gate_act.value("e"))
            gate_act.done(act.activation(TB[:, :], TB[:, :], ACT.Ln, bias=EPSC[:, 2:3]), "l")
            act.wait_ge(gate_dve.sem, gate_dve.value("t"))
            gate_act.done(act.activation(R[ROW_BETA:ROW_BETA + 4, :], TH[ROW_BETA:ROW_BETA + 4, :], ACT.Exp), "beta")

            with act.Fori(0, FOX_HEADS) as h:
                def chunk(first):
                    return PRJ[:, bass.ds(h + first, 1), 0:SEQ].rearrange("p a t -> p (a t)")

                def exponent(q):
                    await_step(act, fp_dve, f"neg{q}", h)
                    fp_act.done(act.activation(PROB[:, q % 2, 0:(q + 1) * P], bank(q % 2, (q + 1) * P), ACT.Exp,
                                               bias=STAT[:, q % 2, 1:2], accum_out=STAT[:, q % 2, 2:3]), f"exp{q}")

                def turned(q):
                    await_step(act, fp_pe, f"turn{q}", h)
                    fp_act.done(act.activation(PTR[:, q % 2, 0:q + 1, :].rearrange("p k q -> p (k q)"),
                                               bank(2 + q % 2, (q + 1) * P), ACT.Copy), f"pt{q}")

                fp_act.done(act.activation(QS[:, :], chunk(AB_Q), ACT.Copy, scale=SCALE), "q")
                fp_act.done(act.activation(KS[:, :], chunk(AB_K), ACT.Copy), "k")
                fp_act.done(act.activation(VS[:, :], chunk(AB_V), ACT.Copy), "v")
                fp_act.done(act.activation(SELH[:, :], IDENT[:, bass.ds(h + ROW_NEGC, 1)].broadcast_to([P, P]), ACT.Copy), "sel")
                await_step(act, fp_pe, "ktok", h)
                hold(act, fk_stored, 16 * h, 0)
                fp_act.done(act.activation(KT[:, :, :].rearrange("p n d -> p (n d)"), bank(5), ACT.Copy), "ktok")
                exponent(0)
                exponent(1)
                turned(0)
                exponent(2)
                turned(1)
                exponent(3)
                turned(2)
                turned(3)
                await_step(act, fp_pe, "pv3", h)
                fp_act.done(act.activation(MOH[:, bass.ds(h, 1), 0:SEQ].rearrange("p a t -> p (a t)"), bank(4), ACT.Copy), "hi")

            act.wait_ge(fk_stored, 16 * FOX_HEADS)
            act.wait_ge(fv_stored, 16 * FOX_HEADS)
            act.wait_ge(fs_pe.sem, fs_pe.value("tok"))
            for j, (tile, name) in enumerate(((QTOK, "qtok"), (KTOKS, "ktok"), (VTOKS, "vtok"))):
                fs_act.done(act.activation(tile[:, :], bank(j)[0:DEC, :], ACT.Copy), name)
            with act.Fori(0, DEC) as b:
                hold(act, qb_ready, b, 0)
                act.activation(SELB[:, :], IDENT[0:DEC, bass.ds(b, 1)].broadcast_to([DEC, P]), ACT.Copy).then_inc(selb_ready, 1)
            act.wait_ge(fs_dve.sem, fs_dve.value("sub"))
            sc = SC[:, :, :, :].rearrange("p b g h -> p (b g h)")
            fs_act.done(act.activation(sc, sc, ACT.Exp), "exp")
            act.wait_ge(fs_dve.sem, fs_dve.value("subn"))
            sn = SN[:, :, :].rearrange("p b h -> p (b h)")
            fs_act.done(act.activation(sn, sn, ACT.Exp), "expn")
            with act.Fori(0, DEC) as b:
                hold(act, vbatch_done, 4 * b + 6)
                act.activation(OS[:, :, bass.ds(b, 1)].rearrange("p h a -> p (h a)"), bank(7, FOX_HEADS), ACT.Copy).then_inc(vo_copied, 1)
            act.wait_ge(fs_dve.sem, fs_dve.value("add"))
            fs_act.done(act.activation(MOH[:, 0:FOX_HEADS, SEQ:TOK], OS[:, :, :], ACT.Copy), "hi")
            act.wait_ge(fs_dve.sem, FOX_END)
            act.wait_ge(gp_pe.sem, gp_pe.value("prev"))
            gp_act.done(act.activation(PREV[:, :, :, :].rearrange("p c b w -> p (c b w)"), bank(0, CONV_CH * DEC * (CONV_W - 1)), ACT.Copy), "prev")
            act.wait_ge(gp_pe.sem, gp_pe.value("tails"))
            for n in range(3):
                gp_act.done(act.activation(TAILS[:, n * 512:(n + 1) * 512], bank(1 + n)[0:DEC + CONV_W - 1, :], ACT.Copy), f"tail{n}")

            def whole(chunk):
                return PRJ[:, bass.ds(chunk, 1), :].rearrange("p a t -> p (a t)")

            with act.Fori(0, CONV_CH // 2) as i:
                for m, tile in enumerate((TA, TB)):
                    await_step(act, cv_dve, "s2", 2 * i + m)
                    act.activation(whole(2 * i + m + AB_CONV), tile[:, :], ACT.Silu).then_inc(cv_act, 1)
            with act.Fori(0, GDN_HEADS) as h:
                act.activation(whole(h + AB_Z), whole(h + AB_Z), ACT.Silu).then_inc(cv_act, 1)
            act.wait_ge(cv_act, CONV_CH + GDN_HEADS)
            act.wait_ge(cv_dve.sem, cv_dve.value("s2", CONV_CH - 1))
            with act.Fori(0, GDN_HEADS) as h:
                for m, (tile, chunk) in enumerate(((SQ, GQ), (SSQ, GK))):
                    hold(act, ln_dve.sem, len(ln_dve.names) * h, 0)
                    ln_act.done(act.activation(tile[:, :], whole(h + chunk), ACT.Square), f"sq{m}")
                for m, (tile, chunk) in enumerate(((TA, GQ), (TB, GK))):
                    await_step(act, ln_pe, f"sum{m}", h)
                    ln_act.done(act.activation(halves(tile[:, :]), ACC[2 + m][:, :, 0:HALF], ACT.Sqrt,
                                               bias=EPSC[:, 1 - m:2 - m], scale=float(P) if m == 0 else 1.0), f"std{m}")
            act.wait_ge(ln_dve.sem, ln_dve.value("mul1", GDN_HEADS - 1))
            act.wait_ge(tails_stored, 32)
            with act.Fori(0, NBLK) as c:
                def chunk_of(first):
                    return PRJ[:, first:first + GDN_HEADS, bass.ds(c * P, P)]

                hold(act, gl_dve.sem, len(gl_dve.names) * c, 0)
                gl_act.done(act.activation(KTS[:, :, :], chunk_of(GK), ACT.Copy), "kts")
                gl_act.done(act.activation(VTS[:, :, :], chunk_of(GV), ACT.Copy), "vts")
                await_step(act, gl_dve, "gd", c)
                gl_act.done(act.activation(GAM[:, :, :], GAM[:, :, :], ACT.Exp), "gam")
                gl_act.done(act.activation(EG[:, :, :].rearrange("p h i -> p (h i)"), bank(0), ACT.Exp), "eg")
                gl_act.done(act.activation(KDC[:, :], KDC[:, :], ACT.Exp), "kdc")
                gl_act.done(act.activation(EGC[:, :], RT[:, bass.ds(c, 1), ROW_GC:ROW_GC + 4].rearrange("p a h -> p (a h)"), ACT.Exp), "egc")
                for n in range(LEVELS):
                    await_step(act, gl_pe, f"t{n}", c)
                    gl_act.done(act.activation(T1[:, :, :].rearrange("p h i -> p (h i)"), bank(6), ACT.Copy), f"t{n}")
                await_step(act, gl_pe, "u", c)
                gl_act.done(act.activation(VNEW[:, :, :].rearrange("p h i -> p (h i)"), bank(1), ACT.Copy), "u")
                await_step(act, gl_pe, "wt", c)
                gl_act.done(act.activation(WT[:, :, :].rearrange("p h i -> p (h i)"), bank(2), ACT.Copy), "wt")
                await_step(act, gl_pe, "o", c)
                gl_act.done(act.activation(chunk_of(GQ), bank(4).rearrange("p (h i) -> p h i", h=GDN_HEADS), ACT.Copy), "o")
            act.wait_ge(gs_pe.sem, gs_pe.value("bc"))
            gs_act.done(act.activation(EGS[:, :, :].rearrange("p h b -> p (h b)"), bank(1)[:, NJ:2 * NJ], ACT.Exp), "egs")
            gs_act.done(act.activation(BEQ[:, :, :].rearrange("p n j -> p (n j)"), bank(1, 3 * NJ), ACT.Copy), "beq")
            act.wait_ge(gs_pe.sem, gs_pe.value("kt"))
            gs_act.done(act.activation(KTK[:, :], bank(2)[0:NJ, 0:P], ACT.Copy), "kt")
            act.wait_ge(gs_pe.sem, gs_pe.value("vt"))
            gs_act.done(act.activation(VTK[:, :], bank(3)[0:NJ, 0:P], ACT.Copy), "vt")
            act.wait_ge(gs_dve.sem, gs_dve.value("o3"))
            with act.Fori(0, GDN_HEADS) as h:
                hold(act, go_dve.sem, len(go_dve.names) * h, 0)
                go_act.done(act.activation(SQ[:, :], whole(h + GQ), ACT.Square), "sq")
                await_step(act, go_pe, "sum", h)
                go_act.done(act.activation(halves(TA[:, :]), ACC[0][:, :, 0:HALF], ACT.Sqrt, bias=EPSC[:, 0:1], scale=1.0 / P), "std")
                await_step(act, go_dve, "gate", h)
                go_act.done(act.activation(MOH[:, bass.ds(h + FOX_HEADS, 1), :].rearrange("p a t -> p (a t)"), TH[:, :], ACT.Copy), "hi")
            act.wait_ge(gdn_stored, 1)
            norm_chunks(2)
            deviation(2)
            up(1)
            norm_chunks(3)
            deviation(3)
            up(2)
            norm_chunks(4)
            deviation(4)
            act.wait_ge(ret_consts_in, 64)

            def ret_turn(h, p):
                first, is_first, is_last = ret_first(h), isinstance(h, int) and h == 0, isinstance(h, int) and h == RET_HEADS
                g, o = h - 1, 1 - p

                def swap(n, name):
                    hold(act, tile_free, RTILE + first + n + 5)
                    act.activation(TB[0:64, :], TA[64:P, :], ACT.Copy)
                    rp_act.done(act.activation(TB[64:P, :], TA[0:64, :], ACT.Copy), name)

                def gate(v, n):
                    hold(act, tile_free, RTILE + first + n + 5)
                    rm_act.done(act.activation(TA[:, :], TA[:, :], ACT.Silu), f"si{v}")
                    await_step(act, rm_dve, f"g{v}", g)
                    rm_act.done(act.activation(RMOH[:, bass.ds(2 * g + v, 1), :].rearrange("p a t -> p (a t)"), TH[:, :], ACT.Copy), f"hi{v}")

                if not is_first:
                    hold(act, rss_stored, 16 * g, 0)
                    act.dma_start(SSR[:, :, :], state_ret[0][:, bass.ds(g, 1)].rearrange("b a k v -> k b (a v)")).then_inc(rss_in, 16)
                if not is_last:
                    swap(0, "q")
                if not is_first:
                    await_step(act, rm_pe, "v1", g)
                    for v in range(2):
                        rm_act.done(act.activation(VTK_R[:, :, v * P:(v + 1) * P], bank(5 + v).rearrange("p (n d) -> p n d", n=NBLK),
                                                   ACT.Copy), f"vt{v}")
                if not is_last:
                    swap(1, "k")
                if not is_first:
                    await_step(act, rm_dve, "s3", g)
                    act.dma_start(rs_prompt[0, 0, bass.ds(g, 1)].rearrange("a k v -> (a k) v"), SALL[NBLK - 1][:, :]).then_inc(rsp_stored, 16)
                    await_step(act, rm_pe, "o", g)
                    await_step(act, rm_dve, "vsc", g)
                    for v in range(2):
                        rm_act.done(act.activation(VBH[o][:, v, 0:SEQ], bank(4 + v), ACT.Copy), f"o{v}")
                    await_step(act, rm_pe, "tok", g)
                    rm_act.done(act.activation(KVT[:, :], bank(7)[0:DEC, 0:3 * P], ACT.Copy), "tk")
                    for v, (squares, name) in enumerate(((SQ, "c0"), (SSQ, "c1"))):
                        await_step(act, rm_dve, name, g)
                        rm_act.done(act.activation(squares[:, :], VBH[o][:, v, :], ACT.Square), f"sq{v}")
                    await_step(act, rm_pe, "var", g)
                    rm_act.done(act.activation(halves(TB[:, :]), ACC[2][:, :, 0:HALF], ACT.Sqrt, bias=EPSC[:, 0:1],
                                               scale=1.0 / RET_DV), "std")
                    await_step(act, rm_dve, "u3", g)
                    act.dma_start(rs_sample[0][:, bass.ds(g, 1)].rearrange("b a k v -> k b (a v)"), SSR[:, :, :]).then_inc(rss_stored, 16)
                    gate(0, 0 if is_last else 4)
                    gate(1, 1 if is_last else 5)

            ret_turns(act, ret_turn)
            norm_chunks(5)
            deviation(5)
            up(3)
            norm_chunks(6)
            deviation(6)
            for n in range(NBLK):
                act.wait_ge(final_turned, n + 1)
                final_copied.done(act.activation(YTOK[:, n, :].rearrange("p (h c) -> p h c", h=2), ACC[n % 2][:, :, :], ACT.Copy), f"tok{n}")
            act.wait_ge(final_turned, NBLK + 1)
            final_copied.done(act.activation(YTOKS[:, :].rearrange("p (h c) -> p h c", h=2), ACC[2][0:DEC, :, :], ACT.Copy), "sample")

        @block.vector
        def _(dve):
            def clear_squares(r):
                if r >= 1:
                    dve.wait_ge(stat_done, r)
                dve.memset(SSQ[:, :], 0.0).then_inc(ssq_ready, 1)

            def norm_chunk(r, d):
                n = KD * r + d
                hold(dve, sq_ready, n + 1)
                hold(dve, ssq_ready, SSQ_STEPS * r + d + 1)
                dve.tensor_tensor(SSQ[:, :], SSQ[:, :], SQ[:, :], ALU.add).then_inc(ssq_ready, 1)
                hold(dve, xh_ready, n + 1)
                dve.scalar_tensor_tensor(out=XL[:, bass.ds(d, 1), :].rearrange("p a t -> p (a t)"),
                                         in0=X[:, bass.ds(d, 1), :].rearrange("p a t -> p (a t)"),
                                         scalar=PAR[:, bass.ds(PAR_NORM + KD * r + d, 1)],
                                         in1=XH[:, bass.ds(d, 1), :].rearrange("p a t -> p (a t)").bitcast(F32),
                                         op0=ALU.mult, op1=ALU.subtract).then_inc(xl_ready, 1)

            def update(name, scale, per_chunk=2):
                u0, r = unit_at[name], UPDATE[name]
                clear_squares(r)
                with dve.Fori(0, KD // 2) as i:
                    for s in range(2):
                        d = 2 * i + s
                        hold(dve, used, u0 + per_chunk * d + per_chunk + 2)
                        xd = X[:, bass.ds(d, 1), :].rearrange("p a (n t) -> p (a n) t", n=2)
                        dve.scalar_tensor_tensor(out=xd, in0=ACC[s][:, :, 0:HALF], scalar=scale, in1=xd,
                                                 op0=ALU.mult, op1=ALU.add).then_inc(tile_free, 1)
                        norm_chunk(r, d)

            def reciprocal(r):
                dve.wait_ge(std_ready, r + 1)
                dve.reciprocal(RSTD[:, :], RSTD[:, :]).then_inc(rstd_ready, 1)
                dve.wait_ge(rstd_ready, r + 1)

            def up(f):
                t0, u0 = tile_at[f"up{f}"], unit_at[f"up{f}"]
                with dve.Fori(0, KF // 2) as i:
                    for s in range(2):
                        t = t0 + 4 * i + 2 * s
                        n = KF * f + 2 * i + s
                        hold(dve, used, u0 + 4 * i + 2 * s + 3)
                        dve.tensor_tensor(halves(TA[:, :]), ACC[2 * s][:, :, 0:HALF], halves(RSTD[:, :]),
                                          ALU.mult).then_inc(tile_free, 1)
                        hold(dve, used, u0 + 4 * i + 2 * s + 4)
                        dve.tensor_tensor(halves(TB[:, :]), ACC[2 * s + 1][:, :, 0:HALF], halves(RSTD[:, :]),
                                          ALU.mult).then_inc(tile_free, 1)
                        hold(dve, act_ready, n + 1)
                        hold(dve, tile_free, t + 6)
                        dve.tensor_tensor(TH[:, :], TA[:, :], TB[:, :], ALU.mult).then_inc(hfull_ready, 1)
                        hold(dve, hh_ready, n + 1)
                        dve.tensor_tensor(HL[:, bass.ds(2 * i + s, 1), :].rearrange("p a t -> p (a t)"), TH[:, :],
                                          HH[:, bass.ds(2 * i + s, 1), :].rearrange("p a t -> p (a t)").bitcast(F32),
                                          ALU.subtract).then_inc(h_ready, 1)

            dve.sem_inc(tile_free, 4)
            dve.memset(ONES[:, :], 1.0).then_inc(ones_set, 1)
            dve.memset(EPSC[:, 0:1], EPS).then_inc(ones_set, 1)
            dve.memset(EPSC[:, 1:2], P * EPS).then_inc(ones_set, 1)
            dve.memset(EPSC[:, 2:3], 1.0).then_inc(ones_set, 1)
            dve.memset(COLS[:, 0:2], 0.0).then_inc(cols_clear, 1)
            dve.memset(COLS[:, 2:3], 1.0).then_inc(cols_clear, 1)
            dve.memset(COLS[:, 3:4], 0.0).then_inc(cols_clear, 1)
            dve.wait_ge(cols_clear, 3)
            dve.memset(COLS[ROW_GC:ROW_GC + 4, 2:3], -1.0).then_inc(cols_clear, 1)
            dve.memset(COLS[ROW_LOGF:ROW_LOGF + 4, 3:4], 1.0).then_inc(cols_clear, 1)
            dve.sem_inc(prod_done, 2)
            dve.wait_ge(par_ready, 1)
            clear_squares(0)
            for d in range(KD):
                dve.wait_ge(loaded_turned, d + 1)
                dve.tensor_copy(X[:, d, 0:SEQ], ACC[d % 4][:, 0, 0:SEQ]).then_inc(x_part, 1)
                dve.wait_ge(x_part, d + 1)
                dve.tensor_copy(X[:, d, SEQ:TOK], ACC[d % 4][:, 1, 0:DEC]).then_inc(tile_free, 1)
                dve.wait_ge(tile_free, d + 5)
                norm_chunk(0, d)
            reciprocal(0)
            up(0)
            update("down0", 0.5)
            reciprocal(1)
            with dve.Fori(0, AB_CH // 4) as i:
                for s in range(4):
                    hold(dve, used, AB_UNIT + 4 * i + s + 3)
                    dve.tensor_tensor(PRJ[:, bass.ds(4 * i + s, 1), :].rearrange("p a (n t) -> p (a n) t", n=2),
                                      ACC[s][:, :, 0:HALF], halves(RSTD[:, :]), ALU.mult).then_inc(tile_free, 1)
            dve.memset(R[:, :], 0.0).then_inc(clear_r, 1)
            dve.wait_ge(clear_r, 1)
            dve.wait_ge(cols_in, 48)
            dve.wait_ge(cols_clear, 5)
            dve.wait_ge(used, AB_UNIT + AB_CH + 3)
            dve.tensor_tensor(halves(TA[:, :]), ACC[0][:, :, 0:HALF], halves(RSTD[:, :]), ALU.mult).then_inc(tile_free, 1)

            dve.wait_ge(tile_free, AB_FREE)
            gate_dve.done(dve.tensor_scalar(TA[:, :], TA[:, :], COLS[:, 0:1], None, ALU.add), "z")
            dve.wait_ge(gate_dve.sem, gate_dve.value("z"))
            gate_dve.done(dve.scalar_tensor_tensor(out=TB[:, :], in0=TA[:, :], scalar=-1.0, in1=TA[:, :], op0=ALU.mult, op1=ALU.max), "az")
            dve.wait_ge(gate_act.sem, gate_act.value("l"))
            dve.tensor_scalar(TH[:, :], TA[:, :], COLS[:, 2:3], 0.0, ALU.mult, ALU.min).then_inc(clear_r, 1)
            dve.wait_ge(clear_r, 2)
            gate_dve.done(dve.tensor_tensor(TH[:, :], TH[:, :], TB[:, :], ALU.subtract), "t")
            dve.wait_ge(gate_dve.sem, gate_dve.value("t"))
            gate_dve.done(dve.tensor_scalar(TA[:, :], TH[:, :], COLS[:, 3:4], None, ALU.mult), "g")
            dve.wait_ge(gate_dve.sem, gate_dve.value("g"))
            lo, hi = ROW_LOGF, ROW_LOGF + 4
            gate_dve.done(dve.tensor_copy(R[lo:hi, :], TA[lo:hi, :]), "logf")
            gate_dve.done(dve.tensor_tensor_scan(SQ[lo:hi, 0:SEQ], ONES[lo:hi, 0:1].broadcast_to([4, SEQ]), TA[lo:hi, 0:SEQ],
                                                 0.0, ALU.mult, ALU.add), "c")
            dve.wait_ge(gate_dve.sem, gate_dve.value("c"))
            gate_dve.done(dve.tensor_scalar(R[ROW_NEGC:ROW_NEGC + 4, 0:SEQ], SQ[lo:hi, 0:SEQ], -1.0, None, ALU.mult), "negc")
            lo, hi = ROW_GC, ROW_GC + 4
            for n in range(NBLK):
                gate_dve.done(dve.tensor_tensor_scan(R[lo:hi, n * P:(n + 1) * P], ONES[lo:hi, :], TA[lo:hi, n * P:(n + 1) * P],
                                                     0.0, ALU.mult, ALU.add), f"gc{n}")
            gate_dve.done(dve.tensor_copy(R[lo:hi, SEQ:TOK], TA[lo:hi, SEQ:TOK]), "gcs")
            dve.wait_ge(gate_pe.sem, gate_pe.value("rt"))
            gate_dve.done(dve.tensor_copy(RT[:, :, :].rearrange("p n c -> p (n c)"), bank(2)), "rt")
            gate_dve.done(dve.tensor_copy(RTS[:, :], bank(3)[0:DEC, 0:P]), "rts")

            with dve.Fori(0, FOX_HEADS) as h:
                def row_max(q):
                    await_step(dve, fp_pe, f"score{q}", h)
                    fp_dve.done(dve.tensor_reduce(STAT[:, q % 2, 0:1], bank(q % 2, (q + 1) * P), AX, ALU.max), f"max{q}")
                    await_step(dve, fp_dve, f"max{q}", h)
                    fp_dve.done(dve.tensor_scalar(STAT[:, q % 2, 1:2], STAT[:, q % 2, 0:1], -1.0, None, ALU.mult), f"neg{q}")

                def normalize(q):
                    await_step(dve, fp_act, f"exp{q}", h)
                    fp_dve.done(dve.reciprocal(STAT[:, q % 2, 3:4], STAT[:, q % 2, 2:3]), f"rinv{q}")
                    await_step(dve, fp_dve, f"rinv{q}", h)
                    p = PROB[:, q % 2, 0:(q + 1) * P]
                    fp_dve.done(dve.tensor_scalar(p, p, STAT[:, q % 2, 3:4], None, ALU.mult), f"norm{q}")

                await_step(dve, fp_pe, "vtok", h)
                hold(dve, fv_stored, 16 * h, 0)
                fp_dve.done(dve.tensor_copy(VT[:, :, :].rearrange("p n d -> p (n d)"), bank(6)), "vtok")
                row_max(0)
                row_max(1)
                normalize(0)
                row_max(2)
                normalize(1)
                row_max(3)
                normalize(2)
                normalize(3)
                await_step(dve, fp_act, "hi", h)
                fp_dve.done(dve.tensor_tensor(MOL[:, bass.ds(h, 1), 0:SEQ].rearrange("p a t -> p (a t)"), bank(4),
                                              MOH[:, bass.ds(h, 1), 0:SEQ].rearrange("p a t -> p (a t)").bitcast(F32),
                                              ALU.subtract), "lo")

            dve.wait_ge(fk_stored, 16 * FOX_HEADS)
            dve.wait_ge(fv_stored, 16 * FOX_HEADS)
            with dve.Fori(0, DEC) as b:
                for m in range(4):
                    hold(dve, kpage_in[m % 2], 64 * (2 * b + m // 2 + 1), 64)
                    if m == 0:
                        hold(dve, qb_ready, b + 1)
                    hold(dve, sum_done, 4 * b + m, 0)
                    k0 = 4 * (m % 2)
                    dve.tensor_tensor(PROD[:, :, :], PAGES[:, k0:k0 + 4, :],
                                      ACC[1][:, 1:2, :].broadcast_to([P, 4, 512]), ALU.mult).then_inc(prod_done, 1)
                    hold(dve, prod_done, 4 * b + m + 3)
                    dve.tensor_reduce(SC[:, bass.ds(b, 1), 4 * m:4 * m + 4, :].rearrange("p a g h -> p (a g) h"),
                                      PROD[:, :, :].rearrange("p g (h d) -> p g h d", h=FOX_HEADS), AX, ALU.add).then_inc(sum_done, 1)

            def chain(ins, name):
                fs_dve.done(ins, name)
                dve.wait_ge(fs_dve.sem, fs_dve.value(name))

            def by_head(chunk):
                return PRJ[:, chunk:chunk + FOX_HEADS, SEQ:TOK].rearrange("p h b -> p b h")

            def over_pages(tile):
                return tile[:, :, None, :].broadcast_to([P, DEC, N_PAGES, FOX_HEADS])

            chain(dve.tensor_tensor(QKS[:, :, :], by_head(AB_Q), by_head(AB_K), ALU.mult), "qk")
            dve.wait_ge(fs_pe.sem, fs_pe.value("total"))
            chain(dve.memset(SUF[:, :, 15, :], 0.0), "suf15")
            total = bank(1).rearrange("p (b g h) -> p b g h", g=N_PAGES, h=FOX_HEADS)
            for g in range(14, -1, -1):
                chain(dve.tensor_tensor(SUF[:, :, g, :], total[:, :, g + 1, :], SUF[:, :, g + 1, :], ALU.add), f"suf{g}")
            dve.wait_ge(sum_done, 4 * DEC)
            chain(dve.scalar_tensor_tensor(out=SC[:, :, :, :].rearrange("p b g h -> p (b g h)"),
                                           in0=SC[:, :, :, :].rearrange("p b g h -> p (b g h)"), scalar=SCALE, in1=bank(0),
                                           op0=ALU.mult, op1=ALU.add), "scale")
            chain(dve.tensor_tensor(SC[:, :, :, :], SC[:, :, :, :], SUF[:, :, :, :], ALU.add), "addsuf")
            dve.wait_ge(fs_pe.sem, fs_pe.value("cn"))
            cn = bank(2, NDH).rearrange("p (h b) -> p b h", b=DEC)[:, :, None, :].broadcast_to([P, DEC, N_PAGES, FOX_HEADS])
            chain(dve.tensor_tensor(SC[:, :, :, :], cn, SC[:, :, :, :], ALU.add), "addcn")
            dve.wait_ge(fs_pe.sem, fs_pe.value("snew"))
            chain(dve.tensor_scalar(SN[:, :, :].rearrange("p b h -> p (b h)"), bank(4, NDH), SCALE, None, ALU.mult), "sn")
            chain(dve.tensor_reduce(MX[:, :, :], SC[:, :, :, :].rearrange("p b g h -> p b h g"), AX, ALU.max), "mx")
            dve.wait_ge(fs_pe.sem, fs_pe.value("turn"))
            chain(dve.tensor_reduce(MXC[:, :], bank(3)[0:NDH, 0:P], AX, ALU.max), "mxc")
            chain(dve.tensor_scalar(DG[:, :], IDENT[0:NDH, 0:NDH], MXC[:, 0:1], None, ALU.mult), "dg")
            dve.wait_ge(fs_pe.sem, fs_pe.value("max"))
            chain(dve.tensor_tensor(MX[:, :, :], bank(5, NDH).rearrange("p (b h) -> p b h", h=FOX_HEADS), SN[:, :, :], ALU.max), "m")
            chain(dve.tensor_tensor(SC[:, :, :, :], SC[:, :, :, :], over_pages(MX), ALU.subtract), "sub")
            chain(dve.tensor_tensor(SN[:, :, :], SN[:, :, :], MX[:, :, :], ALU.subtract), "subn")
            dve.wait_ge(fs_act.sem, fs_act.value("expn"))
            chain(dve.tensor_reduce(DEN[:, :, :], SC[:, :, :, :].rearrange("p b g h -> p b h g"), AX, ALU.add), "dn")
            dve.wait_ge(fs_pe.sem, fs_pe.value("den"))
            chain(dve.tensor_tensor(DEN[:, :, :], bank(6, NDH).rearrange("p (b h) -> p b h", h=FOX_HEADS), SN[:, :, :], ALU.add), "den")
            chain(dve.reciprocal(DEN[:, :, :], DEN[:, :, :]), "rinv")
            chain(dve.tensor_tensor(SC[:, :, :, :], SC[:, :, :, :], over_pages(DEN), ALU.mult), "norm")
            chain(dve.tensor_tensor(SN[:, :, :], SN[:, :, :], DEN[:, :, :], ALU.mult), "normn")
            chain(dve.tensor_tensor(OT[:, :, :].rearrange("p h b -> p b h"), by_head(AB_V), SN[:, :, :], ALU.mult), "vn")
            dve.wait_ge(vo_copied, DEC)
            chain(dve.tensor_tensor(OS[:, :, :], OS[:, :, :], OT[:, :, :], ALU.add), "add")
            dve.wait_ge(fs_act.sem, fs_act.value("hi"))
            chain(dve.tensor_tensor(MOL[:, 0:FOX_HEADS, SEQ:TOK], OS[:, :, :],
                                    MOH[:, 0:FOX_HEADS, SEQ:TOK].bitcast(F32), ALU.subtract), "lo")
            dve.wait_ge(gp_act.sem, gp_act.value("prev"))
            dve.wait_ge(gp_pe.sem, gp_pe.value("tails"))
            with dve.Fori(0, CONV_CH // 2) as i:
                for m, tile in enumerate((TA, TB)):
                    c = 2 * i + m

                    def source(a, b):
                        return PRJ[:, bass.ds(c + AB_CONV, 1), a:b].rearrange("p a t -> p (a t)")

                    def tap(w):
                        return PAR[:, bass.ds(c + PAR_CONV + CONV_CH * w, 1)]

                    hold(dve, cv_act, 2 * i, 0)
                    cv_dve.done(dve.tensor_scalar(tile[:, :], source(0, TOK), tap(3), None, ALU.mult), "w3")
                    for s in range(1, CONV_W):
                        await_step(dve, cv_dve, "w3" if s == 1 else f"s{s - 2}", c)
                        cv_dve.done(dve.scalar_tensor_tensor(out=tile[:, s:SEQ], in0=source(0, SEQ - s), scalar=tap(CONV_W - 1 - s),
                                                             in1=tile[:, s:SEQ], op0=ALU.mult, op1=ALU.add), f"p{s}")
                        prev = PREV[:, bass.ds(c, 1), :, s - 1:s].rearrange("p a b w -> p (a b w)")
                        cv_dve.done(dve.scalar_tensor_tensor(out=tile[:, SEQ:TOK], in0=prev, scalar=tap(s - 1),
                                                             in1=tile[:, SEQ:TOK], op0=ALU.mult, op1=ALU.add), f"s{s - 1}")
            dve.wait_ge(cv_act, CONV_CH + GDN_HEADS)
            with dve.Fori(0, GDN_HEADS) as h:
                for m, (tile, chunk) in enumerate(((TA, GQ), (TB, GK))):
                    await_step(dve, ln_act, f"std{m}", h)
                    ln_dve.done(dve.reciprocal(tile[:, :], tile[:, :]), f"inv{m}")
                    await_step(dve, ln_dve, f"inv{m}", h)
                    x = PRJ[:, bass.ds(h + chunk, 1), :].rearrange("p a t -> p (a t)")
                    ln_dve.done(dve.tensor_tensor(x, x, tile[:, :], ALU.mult), f"mul{m}")
            dve.wait_ge(tails_stored, 32)
            dve.wait_ge(ln_dve.sem, ln_dve.value("mul1", GDN_HEADS - 1))
            dve.wait_ge(lev_in, 16)
            dve.memset(STATE[:, :, :], 0.0).then_inc(state_clear, 1)
            dve.wait_ge(state_clear, 1)
            with dve.Fori(0, NBLK) as c:
                def flat(tile):
                    return tile[:, :, :].rearrange("p h i -> p (h i)")

                def heads_of(b):
                    return bank(b).rearrange("p (h i) -> p h i", h=GDN_HEADS)

                def column(row, h):
                    return RT[:, bass.ds(c, 1), row + h:row + h + 1].rearrange("p a h -> p (a h)")

                def same(a):
                    return a[:, None, :].broadcast_to(GCH)

                await_step(dve, gl_pe, "gcb", c)
                gl_dve.done(dve.tensor_copy(XI[:, :, :], same(IDENT)), "xi")
                gl_dve.done(dve.tensor_copy(XIT[:, :, :], same(IDENT)), "xit")
                for h in range(GDN_HEADS):
                    ins = dve.tensor_scalar(GAM[:, h, :], bank(0)[:, h * P:(h + 1) * P], column(ROW_GC, h), 0.0, ALU.subtract, ALU.min)
                gl_dve.done(ins, "dt")
                gl_dve.done(dve.tensor_tensor(KDC[:, :], heads_of(0)[:, :, P - 1:P].rearrange("p h a -> p (h a)"),
                                              RT[:, bass.ds(c, 1), ROW_GC:ROW_GC + 4].rearrange("p a h -> p (a h)"), ALU.subtract), "gd")
                await_step(dve, gl_act, "gam", c)
                gl_dve.done(dve.tensor_tensor(GAM[:, :, :], GAM[:, :, :], same(INCL), ALU.mult), "gamm")
                await_step(dve, gl_pe, "bb", c)
                await_step(dve, gl_act, "kts", c)
                gl_dve.done(dve.tensor_tensor(KBT[:, :, :], heads_of(1), KTS[:, :, :], ALU.mult), "kbt")
                await_step(dve, gl_act, "eg", c)
                gl_dve.done(dve.tensor_tensor(QET[:, :, :], PRJ[:, GQ:GQ + GDN_HEADS, bass.ds(c * P, P)], EG[:, :, :], ALU.mult), "qet")
                await_step(dve, gl_pe, "a", c)
                await_step(dve, gl_dve, "gamm", c)
                gl_dve.done(dve.tensor_tensor(AT[:, :, :], heads_of(4), GAM[:, :, :], ALU.mult), "at")
                await_step(dve, gl_pe, "qk", c)
                gl_dve.done(dve.tensor_tensor(ATTN[:, :, :], heads_of(5), GAM[:, :, :], ALU.mult), "attn")
                await_step(dve, gl_act, "egc", c)
                gl_dve.done(dve.tensor_tensor(BEGE[:, :], RT[:, bass.ds(c, 1), ROW_BETA:ROW_BETA + 4].rearrange("p a h -> p (a h)"),
                                              EGC[:, :], ALU.mult), "bege")
                for h in range(GDN_HEADS):
                    ins = dve.tensor_scalar(VB[:, h, :], bank(3)[:, h * P:(h + 1) * P], column(ROW_BETA, h), None, ALU.mult)
                gl_dve.done(ins, "vb")
                await_step(dve, gl_dve, "bege", c)
                for h in range(GDN_HEADS):
                    ins = dve.tensor_scalar(KBE[:, h, :], bank(2)[:, h * P:(h + 1) * P], BEGE[:, h:h + 1], None, ALU.mult)
                gl_dve.done(ins, "kbe")
                for h in range(GDN_HEADS):
                    ins = dve.tensor_scalar(KDE[:, h, :], bank(2)[:, h * P:(h + 1) * P], KDC[:, h:h + 1], None, ALU.mult)
                gl_dve.done(ins, "kd")
                for n in range(LEVELS):
                    if n >= 1:
                        await_step(dve, gl_pe, f"t{n - 1}", c)
                    gl_dve.done(dve.tensor_tensor(ATS[:, :, :], AT[:, :, :], same(LEV[:, n, :]), ALU.mult), f"ats{n}")
                    if n < LEVELS - 1:
                        await_step(dve, gl_pe, f"xt{n}", c)
                        gl_dve.done(dve.tensor_tensor(flat(XI), flat(XI), bank(7), ALU.subtract), f"x{n}")
                    await_step(dve, gl_pe, f"xt{n}", c)
                    gl_dve.done(dve.tensor_tensor(flat(XIT), flat(XIT), bank(0), ALU.subtract), f"xt{n}")
                await_step(dve, gl_pe, "ws", c)
                await_step(dve, gl_act, "u", c)
                gl_dve.done(dve.tensor_tensor(flat(VNEW), flat(VNEW), bank(3), ALU.subtract), "vn")
                await_step(dve, gl_pe, "s", c)
                for h in range(GDN_HEADS):
                    ins = dve.scalar_tensor_tensor(out=STATE[:, h, :], in0=STATE[:, h, :], scalar=EG[:, h, P - 1:P],
                                                   in1=bank(5)[:, h * P:(h + 1) * P], op0=ALU.mult, op1=ALU.add)
                gl_dve.done(ins, "s")

            dve.wait_ge(gl_act.sem, gl_act.value("o", NBLK - 1))
            dve.wait_ge(gl_dve.sem, gl_dve.value("s", NBLK - 1))

            def new_tokens(chunk):
                return PRJ[:, chunk:chunk + GDN_HEADS, SEQ:TOK]

            def grid(a):
                return a.rearrange("p (h b) -> p h b", h=GDN_HEADS)

            def chain_g(ins, name):
                gs_dve.done(ins, name)
                dve.wait_ge(gs_dve.sem, gs_dve.value(name))

            kq = KQ[:, :, :].rearrange("p (h b) n -> p h b n", h=GDN_HEADS)
            chain_g(dve.tensor_copy(kq[:, :, :, 0], new_tokens(GK)), "kq0")
            chain_g(dve.tensor_copy(kq[:, :, :, 1], new_tokens(GQ)), "kq1")
            chain_g(dve.tensor_copy(KC[:, :, :], new_tokens(GK)), "kc")
            chain_g(dve.tensor_tensor(QKP[:, :, :], new_tokens(GK), new_tokens(GQ), ALU.mult), "qkp")
            dve.wait_ge(gs_act.sem, gs_act.value("beq"))
            read = bank(0, 2 * NJ).rearrange("p (h b n) -> p h b n", h=GDN_HEADS, n=2)
            chain_g(dve.tensor_tensor(W1[:, :, :], read[:, :, :, 0], EGS[:, :, :], ALU.mult), "a1")
            chain_g(dve.tensor_tensor(W1[:, :, :], new_tokens(GV), W1[:, :, :], ALU.subtract), "a2")
            chain_g(dve.tensor_tensor(VN2[:, :, :], W1[:, :, :], grid(BEQ[:, 0, :]), ALU.mult), "a3")
            chain_g(dve.tensor_tensor(W1[:, :, :], read[:, :, :, 1], EGS[:, :, :], ALU.mult), "o1")
            chain_g(dve.tensor_tensor(W2[:, :, :], VN2[:, :, :], grid(BEQ[:, 2, :]), ALU.mult), "o2")
            chain_g(dve.tensor_tensor(new_tokens(GQ), W1[:, :, :], W2[:, :, :], ALU.add), "o3")
            dve.wait_ge(gs_act.sem, gs_act.value("vt"))
            for h in range(GDN_HEADS):
                if h >= 2:
                    dve.wait_ge(gs_pe.sem, gs_pe.value(f"up{h - 2}"))
                gs_dve.done(dve.tensor_tensor(VBD[:, h % 2, :, :], VTK[:, None, :].broadcast_to([NJ, DEC, P]),
                                              IDENT[0:NJ, h * DEC:(h + 1) * DEC][:, :, None].broadcast_to([NJ, DEC, P]), ALU.mult), f"bd{h}")
                dve.wait_ge(gs_pe.sem, gs_pe.value(f"up{h}"))
                for b in range(DEC):
                    ins = dve.scalar_tensor_tensor(out=SS[:, h * DEC + b, :], in0=SS[:, h * DEC + b, :], scalar=EGS[:, h, b:b + 1],
                                                   in1=ACC[2 + h % 2][:, b // 4, (b % 4) * P:(b % 4 + 1) * P], op0=ALU.mult, op1=ALU.add)
                gs_dve.done(ins, f"s{h}")

            with dve.Fori(0, GDN_HEADS) as h:
                def whole(chunk):
                    return PRJ[:, bass.ds(h + chunk, 1), :].rearrange("p a t -> p (a t)")

                await_step(dve, go_act, "std", h)
                go_dve.done(dve.reciprocal(TA[:, :], TA[:, :]), "inv")
                await_step(dve, go_dve, "inv", h)
                go_dve.done(dve.scalar_tensor_tensor(out=TB[:, :], in0=whole(GQ), scalar=PAR[:, PAR_GDN:PAR_GDN + 1], in1=TA[:, :],
                                                     op0=ALU.mult, op1=ALU.mult), "norm")
                await_step(dve, go_dve, "norm", h)
                go_dve.done(dve.tensor_tensor(TH[:, :], TB[:, :], whole(AB_Z), ALU.mult), "gate")
                await_step(dve, go_act, "hi", h)
                go_dve.done(dve.tensor_tensor(MOL[:, bass.ds(h + FOX_HEADS, 1), :].rearrange("p a t -> p (a t)"), TH[:, :],
                                              MOH[:, bass.ds(h + FOX_HEADS, 1), :].rearrange("p a t -> p (a t)").bitcast(F32), ALU.subtract), "lo")
            dve.wait_ge(gdn_stored, 1)
            update("ab_out", 1.0, 1)
            reciprocal(2)
            up(1)
            update("down1", 0.5)
            reciprocal(3)
            up(2)
            update("down2", 0.5)
            reciprocal(4)
            dve.wait_ge(ret_consts_in, 64)

            def ret_turn(h, p):
                first, is_first, is_last = ret_first(h), isinstance(h, int) and h == 0, isinstance(h, int) and h == RET_HEADS
                g, o = h - 1, 1 - p
                K_SCALE = float(P) ** -0.5

                def scaled(n, out):
                    hold(dve, used, RU + first + n + 3)
                    dve.tensor_tensor(halves(out), ACC[n % 2][:, :, 0:HALF], halves(RSTD[:, :]), ALU.mult).then_inc(tile_free, 1)

                def rotate(out, factor, name):
                    rp_dve.done(dve.scalar_tensor_tensor(out=out[:, :], in0=TA[:, :], scalar=factor, in1=ROPE[:, 0, :],
                                                         op0=ALU.mult, op1=ALU.mult), f"{name}c")
                    await_step(dve, rp_act, name, h)
                    rp_dve.done(dve.scalar_tensor_tensor(out=TB[:, :], in0=TB[:, :], scalar=factor, in1=ROPE[:, 1, :],
                                                         op0=ALU.mult, op1=ALU.mult), f"{name}s")
                    await_step(dve, rp_dve, f"{name}s", h)
                    rp_dve.done(dve.tensor_tensor(out[:, :], out[:, :], TB[:, :], ALU.add), name)

                def decay(kind):
                    return DECS[:, kind, bass.ds(g, 1)]

                def by_chunk(tile):
                    return tile[:, 0:SEQ].rearrange("p (n i) -> p n i", n=NBLK)

                def of_head(table):
                    return table[:, bass.ds(g, 1), :].broadcast_to([P, NBLK, P])

                def block_rows(n):
                    if n == 0:
                        await_step(dve, rm_act, "tk", g)
                    else:
                        await_step(dve, rm_pe, f"r{n - 1}", g)
                    rm_dve.done(dve.tensor_tensor(VBR[:, :, :], KVT[:, None, P:3 * P].broadcast_to([DEC, 2, RET_DV]),
                                                  IDENT[0:DEC, 2 * n:2 * n + 2][:, :, None].broadcast_to([DEC, 2, RET_DV]),
                                                  ALU.mult), f"bd{n}")

                def state_update(n):
                    await_step(dve, rm_pe, f"r{n}", g)
                    s = SSR[:, 2 * n:2 * n + 2, :].rearrange("p b v -> p (b v)")
                    rm_dve.done(dve.scalar_tensor_tensor(out=s, in0=s, scalar=decay(2), in1=bank(6 + n % 2), op0=ALU.mult, op1=ALU.add), f"u{n}")

                def gate(v, n):
                    hold(dve, used, RU + first + n + 3)
                    scaled(n, TA[:, :])
                    await_step(dve, rm_act, f"si{v}", g)
                    rm_dve.done(dve.tensor_tensor(TH[:, :], TA[:, :], VBH[o][:, v, :], ALU.mult), f"g{v}")
                    await_step(dve, rm_act, f"hi{v}", g)
                    rm_dve.done(dve.tensor_tensor(RMOL[:, bass.ds(2 * g + v, 1), :].rearrange("p a t -> p (a t)"), TH[:, :],
                                                  RMOH[:, bass.ds(2 * g + v, 1), :].rearrange("p a t -> p (a t)").bitcast(F32),
                                                  ALU.subtract), f"lo{v}")

                if not is_last:
                    scaled(0, TA[:, :])
                    hold(dve, tile_free, RTILE + first + 5)
                    rotate(QB[p], 1.0, "q")
                if not is_first:
                    await_step(dve, rm_pe, "a", g)
                    rm_dve.done(dve.tensor_scalar(KD_[:, :, :].rearrange("p n d -> p (n d)"), bank(4), decay(0), None, ALU.mult), "kd")
                    rm_dve.done(dve.tensor_tensor(by_chunk(ATT), bank(7).rearrange("p (n i) -> p n i", n=NBLK), of_head(DMAT), ALU.mult), "att")
                    rm_dve.done(dve.tensor_tensor(by_chunk(QB[o]), by_chunk(QB[o]), of_head(QDEC), ALU.mult), "qd")
                    rm_dve.done(dve.tensor_scalar(QSD[:, :], QB[o][:, SEQ:TOK], decay(2), None, ALU.mult), "qsd")
                    rm_dve.done(dve.tensor_tensor(QKR[:, :], QB[o][:, SEQ:TOK], KB[o][:, SEQ:TOK], ALU.mult), "qkp")
                    rm_dve.done(dve.tensor_copy(VSC[:, :, :], VBH[o][:, :, SEQ:TOK]), "vsc")
                if not is_last:
                    scaled(1, TA[:, :])
                    hold(dve, tile_free, RTILE + first + 6)
                    rotate(KB[p], K_SCALE, "k")
                if not is_first:
                    await_step(dve, rm_pe, "kv", g)
                    for n in range(NBLK):
                        kv = bank(6 + n // 2)[:, (n % 2) * RET_DV:(n % 2 + 1) * RET_DV]
                        if n == 0:
                            rm_dve.done(dve.tensor_copy(SALL[0][:, :], kv), "s0")
                            continue
                        await_step(dve, rm_dve, f"s{n - 1}", g)
                        if n == NBLK - 1:
                            hold(dve, rsp_stored, 16 * g, 0)
                        rm_dve.done(dve.scalar_tensor_tensor(out=SALL[n][:, :], in0=SALL[n - 1][:, :], scalar=decay(1), in1=kv,
                                                             op0=ALU.mult, op1=ALU.add), f"s{n}")
                if not is_last:
                    scaled(2, VBH[p][:, 0, :])
                if not is_first:
                    await_step(dve, rm_pe, "cross", g)
                    read = bank(6)[:, 0:2 * DEC].rearrange("p (v b) -> p v b", v=2)
                    qk = bank(6)[:, 2 * DEC:3 * DEC][:, None, :].broadcast_to([P, 2, DEC])
                    rm_dve.done(dve.tensor_tensor(WSC[:, :, :], qk, VSC[:, :, :], ALU.mult), "ov")
                    await_step(dve, rm_dve, "ov", g)
                    rm_dve.done(dve.tensor_tensor(VBH[o][:, :, SEQ:TOK], read, WSC[:, :, :], ALU.add), "os")
                if not is_last:
                    scaled(3, VBH[p][:, 1, :])
                if not is_first:
                    await_step(dve, rm_pe, "mean", g)
                    for v in range(2):
                        out = halves(VBH[o][:, v, :])
                        rm_dve.done(dve.scalar_tensor_tensor(out=out, in0=ACC[2][:, :, 0:HALF], scalar=-1.0 / RET_DV, in1=out,
                                                             op0=ALU.mult, op1=ALU.add), f"c{v}")
                    block_rows(0)
                    block_rows(1)
                    state_update(0)
                    state_update(1)
                    await_step(dve, rm_act, "std", g)
                    rm_dve.done(dve.reciprocal(TB[:, :], TB[:, :]), "inv")
                    await_step(dve, rm_dve, "inv", g)
                    for v in range(2):
                        rm_dve.done(dve.scalar_tensor_tensor(out=VBH[o][:, v, :], in0=VBH[o][:, v, :],
                                                             scalar=PAR[:, bass.ds(2 * g + PAR_RET + v, 1)], in1=TB[:, :],
                                                             op0=ALU.mult, op1=ALU.mult), f"n{v}")
                    block_rows(2)
                    block_rows(3)
                    state_update(2)
                    state_update(3)
                    gate(0, 0 if is_last else 4)
                    gate(1, 1 if is_last else 5)

            ret_turns(dve, ret_turn)
            update("ret_out", 1.0)
            reciprocal(5)
            up(3)
            update("down3", 0.5)
            reciprocal(6)
            for d in range(KD):
                dve.scalar_tensor_tensor(out=YF[:, d, :], in0=X[:, d, :], scalar=PAR[:, PAR_FINAL + d:PAR_FINAL + d + 1],
                                         in1=RSTD[:, :], op0=ALU.mult, op1=ALU.mult).then_inc(y_ready, 1)


_INS = ["x_prompt", "x_sample", "cache_fox_k", "cache_fox_v", "cache_fox_logf", "page_table", "state_gdn_conv",
        "state_gdn_S", "state_ret_S", "norm_g", "final_norm_g", "ffn_w_gu", "ffn_w_down", "ab_w_in", "ab_w_out",
        "fox_b_f", "gdn_conv_w", "gdn_A_log", "gdn_dt_bias", "gdn_norm_g", "c_w_in", "c_w_out", "ret_norm_g"]
_OUTS = [(1, 512, 1024), (8, 1, 1024), (1, 1, 512, 4, 128), (1, 1, 512, 4, 128), (1, 1, 512, 4), (1, 8, 1, 4, 128),
         (1, 8, 1, 4, 128), (1, 8, 1, 4), (1, 1, 3, 1536), (1, 1, 4, 128, 128), (1, 8, 3, 1536), (1, 8, 4, 128, 128),
         (1, 1, 8, 128, 256), (1, 8, 8, 128, 256)]


def kernel(**inputs):
    import concourse.bacc as _bacc
    from concourse.bass_utils import run_bass_kernel_spmd as _run

    nc = _bacc.Bacc("TRN2", target_bir_lowering=False, num_devices=1)
    arrays, args = {}, []
    for name in _INS + ["shape_constants"]:
        a = shape_constants() if name == "shape_constants" else np.ascontiguousarray(inputs[name])
        arrays[f"in_{name}"] = a
        args.append(nc.dram_tensor(f"in_{name}", a.shape, mybir.dt.from_np(a.dtype), kind="ExternalInput").ap())
    for i, shape in enumerate(_OUTS):
        args.append(nc.dram_tensor(f"out_{i}", shape, F32, kind="ExternalOutput").ap())
    trunk_program(nc, *args)
    r = _run(nc, [arrays], core_ids=[0])
    return tuple(r.results[0][f"out_{i}"] for i in range(len(_OUTS)))
```

```python
from contextlib import ExitStack

import numpy as np

import concourse.bass as bass
from concourse import mybir

F32 = mybir.dt.float32
F32R = mybir.dt.float32r
I32 = mybir.dt.int32
ALU = mybir.AluOpType
ACT = mybir.ActivationFunctionType
AX = mybir.AxisListType.X

P = 128
D_MODEL, D_FF = 1024, 2816
SEQ, DEC = 512, 8
TOK = SEQ + DEC
HALF = TOK // 2
KD = D_MODEL // P
KF = D_FF // P
KH = KF // 2
NBLK = SEQ // P
FOX_HEADS = GDN_HEADS = 4
RET_HEADS, RET_DV = 8, 256
N_PAGES, N_POOL = 16, 160
CONV_W, CONV_CH = 4, 12
AB_CH = 28
EPS = 1e-6
LEVELS = 7
NEG = -1e30

CONST_PARTS = [("ident", P), ("maskneg", P), ("incl", P), ("later", P),
               ("levels", LEVELS * P), ("rope", 2 * TOK), ("dmat", RET_HEADS * P), ("qdec", RET_HEADS * P),
               ("kdec", RET_HEADS), ("chunkdec", RET_HEADS), ("stepdec", RET_HEADS)]
CONST_AT = {}
for _name, _n in CONST_PARTS:
    CONST_AT[_name] = (sum(n for _, n in CONST_PARTS[:len(CONST_AT)]), _n)
CONST_COLS = sum(n for _, n in CONST_PARTS)

PAR_NORM, PAR_FINAL, PAR_CONV, PAR_GDN, PAR_RET, PAR_ROWS = 0, 48, 56, 104, 105, 121
"""PAR_NORM + 8*n + d: norm n, chunk d; PAR_CONV + 12*tap + channel chunk; PAR_RET + 2*head + half."""

ROW_LOGF, ROW_GC, ROW_BETA, ROW_NEGC = 0, 32, 64, 96


def shape_constants():
    i = np.arange(P)
    f = np.float32
    c = np.zeros((P, CONST_COLS), f)

    def put(name, a):
        at, n = CONST_AT[name]
        c[:, at:at + n] = a.reshape(P, n)

    put("ident", np.eye(P, dtype=f))
    put("maskneg", np.where(i[None, :] > i[:, None], f(NEG), f(0)))
    put("incl", (i[None, :] >= i[:, None]).astype(f))
    put("later", (i[:, None] > i[None, :]).astype(f))
    lev = np.zeros((P, LEVELS, P), f)
    for n in range(LEVELS):
        s = 1 << n
        row, col = i[:, None], i[None, :]
        lev[:, n] = (row // (2 * s) == col // (2 * s)) & (row // s % 2 == 0) & (col // s % 2 == 1)
    put("levels", lev)
    half = P // 2
    freqs = f(10000.0) ** (-np.arange(half, dtype=f) / f(half))
    pos = np.concatenate([np.arange(SEQ, dtype=f), np.full(DEC, N_PAGES * P, f)])
    ang = (pos[:, None] * freqs[None, :].astype(f)).astype(f).T.astype(np.float64)
    cos, sin = np.cos(ang), np.sin(ang)
    cc, ss = np.concatenate([cos, cos]), np.concatenate([-sin, sin])
    put("rope", np.stack([cc, ss], 1).astype(f))
    lg = np.log(1.0 - 2.0 ** (-5.0 - np.arange(RET_HEADS)))
    diff = i[None, None, :] - i[:, None, None]
    put("dmat", np.where(diff >= 0, np.exp(np.maximum(diff, 0) * lg[None, :, None]), 0.0).astype(f))
    put("qdec", np.broadcast_to(np.exp(lg[None, :, None] * (i[None, None, :] + 1.0)), (P, RET_HEADS, P)).astype(f))
    put("kdec", np.exp(lg[None, :] * (P - 1.0 - i[:, None])).astype(f))
    put("chunkdec", np.broadcast_to(np.exp(lg * P), (P, RET_HEADS)).astype(f))
    put("stepdec", np.broadcast_to(np.exp(lg), (P, RET_HEADS)).astype(f))
    return c


class Steps:

    def __init__(self, sem, names):
        self.sem, self.names, self.next = sem, names, 0
        self.opened = 0


    def done(self, instruction, name):
        assert self.names[self.next % len(self.names)] == name, (name, self.names[self.next % len(self.names)])
        self.next += 1
        instruction.then_inc(self.sem, 1)

    def value(self, name, turn=0):
        return turn * len(self.names) + (self.names.index(name) + 1) + self.opened

    def turns(self, n):
        return len(self.names) * n + self.opened


def hold(engine, sem, value, least=1):
    if not isinstance(value, int):
        engine.wait_ge(sem, least)
    engine.wait_ge(sem, value)


def await_turns(engine, steps, n):
    hold(engine, steps.sem, steps.turns(n))


def await_step(engine, steps, name, turn=0):
    hold(engine, steps.sem, steps.value(name, turn))


def trunk_program(nc, x_prompt, x_sample, cache_k, cache_v, cache_logf, page_table, state_conv, state_gdn, state_ret,
                  norm_g, final_g, w_gu, w_down, ab_in, ab_out, fox_b, conv_w, a_log, dt_bias, gdn_g, c_in, c_out,
                  ret_g, consts, y_prompt, y_sample, fk_prompt, fv_prompt, fl_prompt, fk_sample, fv_sample,
                  fl_sample, conv_prompt, gs_prompt, conv_sample, gs_sample, rs_prompt, rs_sample):
    ctx = ExitStack()
    base = nc.sbuf_base + (-nc.sbuf_base) % 32
    room = nc.sbuf_usable_end - base
    cursor = {"main": 0}

    def at(name, shape, offset, dt=F32):
        size = 4 * int(np.prod(shape[1:]))
        assert offset % 32 == 0 and offset + size <= room, (name, offset, size, room)
        return nc.alloc_sbuf_tensor_at(name, shape, dt, offset=base + offset)

    def new(name, shape, dt=F32, area="main"):
        offset = cursor[area]
        cursor[area] = offset + -(-4 * int(np.prod(shape[1:])) // 32) * 32
        return at(name, shape, offset, dt)

    with ctx:
        def sem(name):
            return ctx.enter_context(nc.semaphore(name))

        X = new("X", [P, KD, TOK])
        IDENT = new("IDENT", [P, P])
        ONES = new("ONES", [P, P])
        MASKNEG = new("MASKNEG", [P, P])
        INCL = new("INCL", [P, P])
        LATER = new("LATER", [P, P])
        PAR = new("PAR", [P, P])
        RSTD = new("RSTD", [P, TOK])
        SSQ = new("SSQ", [P, TOK])
        SQ = new("SQ", [P, TOK])
        EPSC = new("EPSC", [P, 4])
        ZERO = new("ZERO", [P, 1, 1])
        COLS = new("COLS", [P, 4])
        TA = new("TA", [P, TOK])
        TB = new("TB", [P, TOK])
        TH = new("TH", [P, TOK])
        ring_at = cursor["main"]
        RAW = new("RAW", [P, 2, KH, P])
        WHI = new("WHI", [P, 2, KH, P], F32R)
        WLO = new("WLO", [P, 2, KH, P], F32R)
        cursor["xs"] = cursor["main"]
        XH = new("XH", [P, KD, TOK], F32R, "xs")
        XL = new("XL", [P, KD, TOK], F32R, "xs")
        cursor["abwork"] = cursor["main"]
        cursor["h"] = cursor["xs"]
        cursor["load"] = cursor["proj"] = cursor["ret"] = cursor["fin"] = cursor["h"]
        HH = new("HH", [P, KF, TOK], F32R, "h")
        HL = new("HL", [P, KF, TOK], F32R, "h")
        cursor["ab"] = cursor["retc"] = cursor["h"]
        XTOK = new("XTOK", [P, NBLK, D_MODEL], area="load")
        XTOKS = new("XTOKS", [DEC, D_MODEL], area="load")
        PROWS = new("PROWS", [P, P], area="load")
        YF = new("YF", [P, KD, TOK], area="fin")
        YTOK = new("YTOK", [P, NBLK, D_MODEL], area="fin")
        YTOKS = new("YTOKS", [DEC, D_MODEL], area="fin")

        ACC = [ctx.enter_context(nc.psum_tensor(f"ACC{i}", [P, 2, 512], F32)) for i in range(4)]

        def bank(b, n=512):
            return ACC[b // 2][:, b % 2, 0:n]

        def halves(a):
            return a.rearrange("p (n t) -> p n t", n=2)

        consts_in = sem("consts_in")
        inputs_in = sem("inputs_in")
        cols_clear = sem("cols_clear")
        ones_set = sem("ones_set")
        raw_in = [sem("raw_in0"), sem("raw_in1")]
        zero_set = sem("zero_set")
        hi_split = sem("hi_split")
        split = sem("split")
        used = sem("used")
        tile_free = sem("tile_free")
        sq_ready = sem("sq_ready")
        ssq_ready = sem("ssq_ready")
        xh_ready = sem("xh_ready")
        xl_ready = sem("xl_ready")
        stat_done = sem("stat_done")
        std_ready = sem("std_ready")
        rstd_ready = sem("rstd_ready")
        act_ready = sem("act_ready")
        hfull_ready = sem("hfull_ready")
        hh_ready = sem("hh_ready")
        h_ready = sem("h_ready")
        stored = sem("stored")
        stores = [0]

        unit_at, tile_at = {}, {}
        u = 0
        t = KD
        for name, units, tiles in (("up0", 2 * KF, 2 * KF), ("down0", 2 * KD, KD), ("ab_in", AB_CH + 1, AB_CH + 1),
                                   ("ab_out", KD, KD), ("up1", 2 * KF, 2 * KF), ("down1", 2 * KD, KD),
                                   ("up2", 2 * KF, 2 * KF), ("down2", 2 * KD, KD), ("ret_in", 6 * RET_HEADS, 6 * RET_HEADS),
                                   ("ret_out", 2 * KD, KD), ("up3", 2 * KF, 2 * KF), ("down3", 2 * KD, KD)):
            unit_at[name], tile_at[name] = u, t
            u, t = u + units, t + tiles
        UPDATE = {"load": 0, "down0": 1, "ab_out": 2, "down1": 3, "down2": 4, "ret_out": 5, "down3": 6}
        NORM_OF = {"up0": 0, "ab_in": 1, "up1": 2, "up2": 3, "ret_in": 4, "up3": 5, "final": 6}
        SSQ_STEPS = KD + 1
        tile_at_update = [0] + [tile_at[n] for n in UPDATE if n != "load"]

        par_turned = sem("par_turned")
        par_ready = sem("par_ready")
        loaded_turned = sem("loaded_turned")
        x_part = sem("x_part")
        y_ready = sem("y_ready")
        final_turned = sem("final_turned")
        final_copied = Steps(sem("final_copied"), [f"tok{n}" for n in range(NBLK)] + ["sample"])
        AB_Q, AB_K, AB_V, AB_CONV, AB_Z = 0, 4, 8, 12, 24
        PRJ = new("PRJ", [P, AB_CH, TOK], area="proj")
        MOH = new("MOH", [P, KD, TOK], F32R, "proj")
        MOL = new("MOL", [P, KD, TOK], F32R, "proj")
        LEV = new("LEV", [P, LEVELS, P], area="ab")
        R = new("R", [P, TOK], area="ab")
        RT = new("RT", [P, NBLK, P], area="ab")
        RTS = new("RTS", [DEC, P], area="ab")
        SC = new("SC", [P, DEC, N_PAGES, FOX_HEADS], area="ab")
        LF = new("LF", [P, DEC, N_PAGES, FOX_HEADS], area="ab")
        SUF = new("SUF", [P, DEC, N_PAGES, FOX_HEADS], area="ab")
        NDH = DEC * FOX_HEADS
        SN, MX, DEN, QKS = (new(n, [P, DEC, FOX_HEADS], area="ab") for n in ("SN", "MX", "DEN", "QKS"))
        OS = new("OS", [P, FOX_HEADS, DEC], area="ab")
        OT = new("OT", [P, FOX_HEADS, DEC], area="ab")
        MXC = new("MXC", [NDH, 1], area="ab")
        DG = new("DG", [NDH, NDH], area="ab")
        PT_SB = new("PT_SB", [1, DEC * N_PAGES], I32, "ab")
        cursor["fp"] = cursor["fs"] = cursor["gd"] = cursor["abwork"]
        QS, KS, VS = (new(n, [P, SEQ], area="fp") for n in ("QS", "KS", "VS"))
        SELH = new("SELH", [P, P], area="fp")
        KT, VT = (t[:, 0:SEQ].rearrange("p (n d) -> p n d", n=NBLK) for t in (TA, TB))
        PROB = new("PROB", [P, 2, SEQ], area="fp")
        PTR = new("PTR", [P, 2, NBLK, P], area="fp")
        STAT = new("STAT", [P, 2, 4], area="fp")
        KTOKS = new("KTOKS", [DEC, FOX_HEADS * P], area="fp")
        VTOKS, QTOK = RSTD[0:DEC, 0:FOX_HEADS * P], TH[0:DEC, 0:FOX_HEADS * P]
        QBR = new("QBR", [P, 2, FOX_HEADS * P], area="ab")
        SELB = SQ[0:DEC, 0:P]
        KBATCH = 4
        EARLY = 6
        mo_at = cursor["proj"] - 2 * 4 * KD * TOK
        PAGES_BYTES = 4 * 2 * KBATCH * FOX_HEADS * P
        KPAGES = [at(f"KPAGES{n}", [P, 2, KBATCH, FOX_HEADS * P], a) for n, a in enumerate((mo_at, ring_at))]
        PROD = [at(f"PROD{n}", [P, KBATCH, FOX_HEADS * P], a + PAGES_BYTES) for n, a in enumerate((mo_at, ring_at))]
        CONVROWS = at("CONVROWS", [DEC * (CONV_W - 1), CONV_CH * P], mo_at + PAGES_BYTES * 3 // 2)
        TAILS = new("TAILS", [DEC + CONV_W - 1, CONV_CH * P], area="fp")
        PREV = new("PREV", [P, CONV_CH, DEC, CONV_W - 1], area="fp")
        VPAGES = at("VPAGES", [P, N_PAGES, FOX_HEADS * P], ring_at)

        small_in = sem("small_in")
        cols_in = sem("cols_in")
        lev_in = sem("lev_in")
        pt_in = sem("pt_in")
        clear_r = sem("clear_r")
        gate_dve = Steps(sem("gate_dve"), ["z", "az", "t", "g", "logf", "c", "negc"] + [f"gc{n}" for n in range(NBLK)]
                         + ["gcs", "rt", "rts"])
        gate_act = Steps(sem("gate_act"), ["fac", "e", "l", "beta"])
        gate_pe = Steps(sem("gate_pe"), ["rt"])
        fp_pe = Steps(sem("fp_pe"), ["ktok", "vtok", "score0", "score1", "turn0", "pv0", "score2", "turn1", "pv1",
                                     "score3", "turn2", "pv2", "turn3", "pv3"])
        fp_act = Steps(sem("fp_act"), ["q", "k", "v", "sel", "ktok", "exp0", "exp1", "pt0", "exp2", "pt1", "exp3",
                                       "pt2", "pt3", "hi"])
        fp_dve = Steps(sem("fp_dve"), ["vtok", "max0", "neg0", "max1", "neg1", "rinv0", "norm0", "max2", "neg2",
                                       "rinv1", "norm1", "max3", "neg3", "rinv2", "norm2", "rinv3", "norm3", "lo"])
        fk_stored = sem("fk_stored")
        fv_stored = sem("fv_stored")
        kpage_in = [sem("kpage_in0"), sem("kpage_in1")]
        vpage_in = [sem(f"vpage_in{m}") for m in range(4)]
        lf_in = sem("lf_in")
        prod_done = sem("prod_done")
        sum_done = sem("sum_done")
        vbatch_done = sem("vbatch_done")
        qtok_ready = sem("qtok_ready")
        qtok_turned = sem("qtok_turned")
        selb_ready = sem("selb_ready")
        qb_ready = sem("qb_ready")
        qbr_ready = sem("qbr_ready")
        vo_copied = sem("vo_copied")
        fs_pe = Steps(sem("fs_pe"), ["tok", "later", "total", "snew", "turn", "max", "den"])
        fs_act = Steps(sem("fs_act"), ["ktok", "vtok", "exp", "expn", "hi"])
        fs_dve = Steps(sem("fs_dve"), ["suf15"] + [f"suf{g}" for g in range(14, -1, -1)]
                       + ["addlater", "qk", "scale", "addcn", "sn", "mx", "mxc", "dg", "m", "sub", "subn", "dn", "den", "rinv",
                          "norm", "normn", "vn", "add", "lo"])
        AB_UNIT, AB_TILE = unit_at["ab_in"], tile_at["ab_in"]
        AB_FREE = AB_TILE + AB_CH + 1 + 4
        SCALE = float(P) ** -0.5
        GQ, GK, GV = AB_CONV, AB_CONV + 4, AB_CONV + 8
        NJ = GDN_HEADS * DEC
        GCH = [P, GDN_HEADS, P]
        (KTS, VTS, GAM, EG, KBT, QET, AT, ATS, ATTN, XI, XIT, T1, VB, KBE, KDE, WT, VNEW, STATE) = (
            new(n, GCH, area="gd") for n in ("KTS", "VTS", "GAM", "EG", "KBT", "QET", "AT", "ATS", "ATTN", "XI", "XIT",
                                             "T1", "VB", "KBE", "KDE", "WT", "VNEW", "STATE"))
        SS = new("SS", [P, NJ, P], area="gd")
        assert cursor["gd"] <= cursor["abwork"] + 4 * (2 * KD + AB_CONV) * TOK
        cursor["gs"] = cursor["abwork"]
        KQ = new("KQ", [P, NJ, 2], area="gs")
        KC, QKP, EGS, VN2, W1, W2 = (new(n, [P, GDN_HEADS, DEC], area="gs") for n in ("KC", "QKP", "EGS", "VN2", "W1", "W2"))
        BEQ = new("BEQ", [P, 3, NJ], area="gs")
        KTK, VTK = (new(n, [NJ, P], area="gs") for n in ("KTK", "VTK"))
        VBD = new("VBD", [NJ, 2, DEC, P], area="gs")
        KDC, EGC, BEGE = (new(n, [P, GDN_HEADS], area="ab") for n in ("KDC", "EGC", "BEGE"))

        tails_stored = sem("tails_stored")
        gdn_stored = sem("gdn_stored")
        convrows_in = sem("convrows_in")
        ss_in = sem("ss_in")
        gp_pe = Steps(sem("gp_pe"), ["prev", "tails"])
        gp_act = Steps(sem("gp_act"), ["prev", "tail0", "tail1", "tail2"])
        cv_dve = Steps(sem("cv_dve"), ["z", "p3", "s0", "p2", "s1", "p1", "s2", "w3"])
        cv_act = sem("cv_act")
        ln_act = Steps(sem("ln_act"), ["sq0", "sq1", "std0", "std1"])
        ln_pe = Steps(sem("ln_pe"), ["sum0", "sum1"])
        ln_dve = Steps(sem("ln_dve"), ["inv0", "mul0", "inv1", "mul1"])
        gl_pe = Steps(sem("gl_pe"), ["gcb", "bb", "ktok", "vtok", "a", "qk"]
                      + ["t0"] + [f"{w}{n}" for n in range(1, LEVELS) for w in (("t", "x", "xt") if n < LEVELS - 1 else ("t", "xt"))]
                      + ["u", "wt", "ws", "o", "s"])
        gl_act = Steps(sem("gl_act"), ["kts", "vts", "gam", "eg", "kdc", "egc"] + [f"t{n}" for n in range(1, LEVELS)]
                       + ["u", "wt", "o"])
        gl_dve = Steps(sem("gl_dve"), ["xi", "xit", "dt", "gd", "gamm", "kbt", "qet", "at", "attn", "bege", "vb", "kbe", "kd"]
                       + ["ats0", "xt0", "ats1", "x0"] + [w for n in range(1, LEVELS) for w in ([f"ats{n + 1}", f"x{n}", f"xt{n}"] if n < LEVELS - 1 else [f"xt{n}"])]
                       + ["vn", "s"])
        state_clear = sem("state_clear")
        gs_pe = Steps(sem("gs_pe"), ["r", "bc", "kt", "vt"] + [f"up{h}" for h in range(GDN_HEADS)])
        gs_act = Steps(sem("gs_act"), ["egs", "beq", "kt", "vt"])
        gs_dve = Steps(sem("gs_dve"), ["kq0", "kq1", "kc", "qkp", "a1", "a2", "a3", "o1", "o2", "o3"]
                       + [f"{w}{h}" for h in range(GDN_HEADS) for w in ("bd", "s")])
        go_act = Steps(sem("go_act"), ["sq", "std", "hi"])
        go_pe = Steps(sem("go_pe"), ["sum"])
        go_dve = Steps(sem("go_dve"), ["inv", "norm", "gate", "lo"])
        FOX_PROBS = fs_dve.value("vn")
        FOX_END = fs_dve.value("lo")
        RCH = 2 * RET_HEADS
        RMOH = new("RMOH", [P, RCH, TOK], F32R, "ret")
        RGATE = at("RGATE", [P, RCH, TOK], cursor["ret"])
        RMOL = new("RMOL", [P, RCH, TOK], F32R, "ret")
        QB = [new(f"QB{i}", [P, TOK], area="ret") for i in range(2)]
        KB = [new(f"KB{i}", [P, TOK], area="ret") for i in range(2)]
        VBH = [new(f"VBH{i}", [P, 2, TOK], area="ret") for i in range(2)]
        VTK_R = new("VTK_R", [P, NBLK, RET_DV], area="ret")
        cursor["retc"] = max(cursor["retc"], cursor["ret"])
        ROPE = new("ROPE", [P, 2, TOK], area="retc")
        DMAT = new("DMAT", [P, RET_HEADS, P], area="retc")
        QDEC = new("QDEC", [P, RET_HEADS, P], area="retc")
        DECS = new("DECS", [P, 3, RET_HEADS], area="retc")
        KD_ = SQ[:, 0:SEQ].rearrange("p (n d) -> p n d", n=NBLK)

        def ring_tail(name, n, shape):
            assert 4 * int(np.prod(shape[1:])) <= 4 * (KH - KD) * P
            return at(name, shape, ring_at + 4 * (n * KH + KD) * P)

        SALL = [ring_tail(f"SALL{n}", n + 2, [P, RET_DV]) for n in range(NBLK)]
        SSR = new("SSR", [P, DEC, RET_DV], area="retc")
        VSC = new("VSC", [P, 2, DEC], area="retc")
        WSC = new("WSC", [P, 2, DEC], area="retc")
        QSD, QKR = (new(n, [P, DEC], area="retc") for n in ("QSD", "QKR"))
        KVT = ring_tail("KVT", 0, [DEC, 3 * P])
        ATT = TH
        KBLK = TH[0:DEC, 0:DEC // 2 * P].rearrange("j (b d) -> j b d", b=DEC // 2)

        ret_consts_in = sem("ret_consts_in")
        rp_act = Steps(sem("rp_act"), ["q", "k"])
        rp_dve = Steps(sem("rp_dve"), ["qc", "qs", "q", "kc", "ks", "k"])
        rm_pe = Steps(sem("rm_pe"), ["ktok", "v0", "v1", "a", "kv", "o", "cross", "mean", "tok", "var", "r0", "r1", "r2", "r3"])
        rm_act = Steps(sem("rm_act"), ["vt0", "vt1", "o0", "o1", "tk", "sq0", "sq1", "std", "si0", "hi0", "si1", "hi1"])
        rm_dve = Steps(sem("rm_dve"), ["kd", "att", "qd", "qsd", "qkp", "vsc", "s0", "s1", "s2", "s3", "ov", "os", "c0", "c1",
                                       "kb0", "ga0", "inv", "n0", "n1", "u0", "u1", "kb1", "g0", "lo0", "ga1", "u2", "u3", "g1", "lo1"])
        states_stepped = sem("states_stepped")
        rss_in = sem("rss_in")
        rss_stored = sem("rss_stored")
        rsp_stored = sem("rsp_stored")
        RU, RTILE = unit_at["ret_in"], tile_at["ret_in"]

        def ret_first(turn):
            return 0 if isinstance(turn, int) and turn == 0 else 6 * turn - 2

        def ret_turns(engine, turn):
            turn(0, 0)
            with engine.Fori(0, RET_HEADS // 2 - 1) as i:
                turn(2 * i + 1, 1)
                turn(2 * i + 2, 0)
            turn(RET_HEADS - 1, 1)
            turn(RET_HEADS, 0)

        OPENED = {"act": (gl_act,), "dve": (gl_dve, ln_dve, go_dve)}
        for group in OPENED.values():
            for steps in group:
                steps.opened = 1

        def load_keys(engine, store, slot, first, n):
            hold(engine, prod_done, n + 1)
            for g in range(KBATCH):
                page = engine.value_load(PT_SB[0:1, bass.ds(first + g, 1)], min_val=0, max_val=N_POOL - 1)
                engine.dma_start(KPAGES[store][:, slot, g, :], cache_k[0, bass.ds(page, 1)].rearrange("a t h d -> (a t) (h d)"))\
                      .then_inc(kpage_in[slot], 16)

        block = ctx.enter_context(nc.Block())

        @block.sync
        def _(sp):
            def store(to, of):
                stores[0] += 1
                sp.dma_start(to, of).then_inc(stored, 16)

            for s in (fk_stored, fv_stored, rss_stored, rsp_stored):
                sp.sem_inc(s, 16)

            def load_unit(unit, slot, nk, source):
                hold(sp, split, unit + 1)
                sp.dma_start(RAW[:, slot, 0:nk, :], source).then_inc(raw_in[slot], 16)

            def load_up(f):
                w = w_gu[f // 2, f % 2].rearrange("(k p) c -> p k c", p=P)
                u0 = unit_at[f"up{f}"]
                with sp.Fori(0, KF // 2) as i:
                    for s in range(4):
                        col = (s % 2) * D_FF + P * (s // 2) + 2 * P * i
                        load_unit(u0 + 4 * i + s, (u0 + s) % 2, KD, w[:, :, bass.ds(col, P)])

            def load_down(f):
                w = w_down[f // 2, f % 2].rearrange("(s k p) c -> p s k c", p=P, k=KH)
                u0 = unit_at[f"down{f}"]
                with sp.Fori(0, KD // 2) as i:
                    for s in range(4):
                        load_unit(u0 + 4 * i + s, (u0 + s) % 2, KH,
                                  w[:, s % 2, :, bass.ds(2 * P * i + P * (s // 2), P)])

            sp.dma_start(PROWS[PAR_NORM:PAR_FINAL, :], norm_g.rearrange("l s (c p) -> (l s c) p", p=P)).then_inc(inputs_in, 16)
            sp.dma_start(PROWS[PAR_FINAL:PAR_CONV, :], final_g.rearrange("(c p) -> c p", p=P)).then_inc(inputs_in, 16)
            sp.dma_start(PROWS[PAR_CONV:PAR_GDN, :], conv_w[0].rearrange("w (c p) -> (w c) p", p=P)).then_inc(inputs_in, 16)
            sp.dma_start(PROWS[PAR_GDN:PAR_RET, :], gdn_g).then_inc(inputs_in, 16)
            sp.dma_start(PROWS[PAR_RET:PAR_ROWS, :], ret_g[0].rearrange("(c p) -> c p", p=P)).then_inc(inputs_in, 16)
            sp.dma_start(XTOKS[:, :], x_sample.rearrange("b o d -> (b o) d")).then_inc(inputs_in, 16)
            sp.dma_start(XTOK[:, :, :], x_prompt[0].rearrange("(n p) d -> p n d", p=P)).then_inc(inputs_in, 16)
            for tile, name in ((IDENT, "ident"), (MASKNEG, "maskneg"), (INCL, "incl"), (LATER, "later")):
                c0, n = CONST_AT[name]
                sp.dma_start(tile[:, :], consts[:, c0:c0 + n]).then_inc(consts_in, 16)
            for tile, src in ((COLS[ROW_LOGF:ROW_LOGF + 4, 0:1], fox_b), (COLS[ROW_GC:ROW_GC + 4, 0:1], dt_bias),
                              (COLS[ROW_GC:ROW_GC + 4, 1:2], a_log)):
                sp.wait_ge(cols_clear, 5)
                sp.dma_start(tile, src.rearrange("a h -> h a")).then_inc(cols_in, 16)
            c0, n = CONST_AT["levels"]
            sp.dma_start(LEV[:, :, :], consts[:, c0:c0 + n].rearrange("p (l c) -> p l c", l=LEVELS)).then_inc(lev_in, 16)
            sp.dma_start(PT_SB[:, :], page_table.rearrange("b (o g) -> o (b g)", o=1)).then_inc(pt_in, 16)
            load_up(0)
            load_down(0)
            abw = ab_in[0].rearrange("(k p) c -> p k c", p=P)
            for f0 in range(4):
                load_unit(AB_UNIT + f0, (AB_UNIT + f0) % 2, KD, abw[:, :, P * f0:P * (f0 + 1)])
            for f0, turns, shift in ((AB_K, 1, 0), (AB_CONV, 2, FOX_HEADS)):
                with sp.Fori(0, turns) as i:
                    for m in range(8):
                        load_unit(AB_UNIT + f0 + 8 * i + m, (AB_UNIT + m) % 2, KD,
                                  abw[:, :, bass.ds(P * (f0 + m) + shift + 8 * P * i, P)])
                        if f0 == AB_K and m == 0:
                            sp.wait_ge(used, AB_UNIT + 2)
                            sp.dma_start(CONVROWS[:, :], state_conv[0].rearrange("b w c -> (b w) c")).then_inc(convrows_in, 16)
            slot = (AB_UNIT + AB_CH) % 2
            hold(sp, split, AB_UNIT + AB_CH + 1)
            for at_col, c0, dst_sem in ((ROW_LOGF, 3 * 512, raw_in[slot]), (ROW_GC, 3588, small_in), (ROW_BETA, 3592, small_in)):
                sp.dma_start(RAW[:, slot, 0:KD, at_col:at_col + 4], abw[:, :, c0:c0 + 4]).then_inc(dst_sem, 16)
            sp.wait_ge(gate_dve.sem, gate_dve.value("rt"))
            store(fl_prompt[0, 0].rearrange("(n p) h -> p n h", p=P), RT[:, :, ROW_LOGF:ROW_LOGF + 4])
            sp.wait_ge(gate_dve.sem, gate_dve.value("rts"))
            store(fl_sample.rearrange("a b o h -> (a b o) h"), RTS[:, ROW_LOGF:ROW_LOGF + 4])
            sp.wait_ge(fs_act.sem, fs_act.value("vtok"))
            store(fk_sample[0].rearrange("b o h d -> (b o) (h d)"), KTOKS[:, :])
            store(fv_sample[0].rearrange("b o h d -> (b o) (h d)"), VTOKS)
            store(conv_sample[0][:, 0:CONV_W - 2, :], state_conv[0][:, 1:CONV_W - 1, :])
            sp.wait_ge(gp_act.sem, gp_act.value("tail2"))
            sp.dma_start(conv_prompt[0, 0], TAILS[0:CONV_W - 1, :]).then_inc(tails_stored, 16)
            sp.dma_start(conv_sample[0][:, CONV_W - 2, :], TAILS[CONV_W - 1:, :]).then_inc(tails_stored, 16)
            sp.wait_ge(used, AB_UNIT + AB_CH + 3)
            with sp.Fori(0, FOX_HEADS) as h:
                for m in range(2):
                    load_keys(sp, 1, m, N_PAGES * (EARLY + m) + KBATCH * h, 4 * EARLY + 2 * h + m)
                await_step(sp, fp_act, "ktok", h)
                sp.dma_start(fk_prompt[0, 0].rearrange("(n p) h d -> p n h d", p=P)[:, :, bass.ds(h, 1), :]
                             .rearrange("p n a d -> p n (a d)"), KT).then_inc(fk_stored, 16)
                await_step(sp, fp_dve, "vtok", h)
                sp.dma_start(fv_prompt[0, 0].rearrange("(n p) h d -> p n h d", p=P)[:, :, bass.ds(h, 1), :]
                             .rearrange("p n a d -> p n (a d)"), VT).then_inc(fv_stored, 16)
            sp.wait_ge(fk_stored, 16 * FOX_HEADS + 16)
            sp.wait_ge(fv_stored, 16 * FOX_HEADS + 16)
            sp.wait_ge(tails_stored, 32)
            sp.wait_ge(sum_done, DEC * N_PAGES // KBATCH + 1)
            sp.wait_ge(fs_dve.sem, FOX_PROBS)
            for h in range(GDN_HEADS):
                sp.dma_start(SS[:, h * DEC:(h + 1) * DEC, :], state_gdn[0][:, h].rearrange("b k v -> k b v")).then_inc(ss_in, 16)
            with sp.Fori(0, DEC) as b:
                for m in range(4):
                    hold(sp, vbatch_done, 4 * b + m + 1)
                    for g in range(4 * m, 4 * m + 4):
                        page = sp.value_load(PT_SB[0:1, bass.ds(N_PAGES * b + g, 1)], min_val=0, max_val=N_POOL - 1)
                        sp.dma_start(VPAGES[:, g, :], cache_v[0, bass.ds(page, 1)].rearrange("a t h d -> (a t) (h d)"))\
                          .then_inc(vpage_in[m], 16)
            sp.wait_ge(gl_dve.sem, gl_dve.value("s", NBLK - 1))
            store(gs_prompt[0, 0].rearrange("h k v -> k h v"), STATE[:, :, :])
            for h in range(GDN_HEADS):
                sp.wait_ge(gs_dve.sem, gs_dve.value(f"s{h}"))
                store(gs_sample[0][:, h].rearrange("b k v -> k b v"), SS[:, h * DEC:(h + 1) * DEC, :])
            gdn_stores = stores[0]
            sp.wait_ge(stored, 16 * gdn_stores)
            sp.sem_inc(gdn_stored, 1)
            abo = ab_out[0].rearrange("(k p) c -> p k c", p=P)
            with sp.Fori(0, KD // 2) as i:
                for s in range(2):
                    load_unit(unit_at["ab_out"] + 2 * i + s, (unit_at["ab_out"] + s) % 2, KD,
                              abo[:, :, bass.ds(2 * P * i + P * s, P)])
            load_up(1)
            load_down(1)
            load_up(2)
            load_down(2)
            for tile, name in ((ROPE, "rope"), (DMAT, "dmat"), (QDEC, "qdec")):
                c0, n = CONST_AT[name]
                n = int(np.prod(tile.shape[1:]))
                sp.wait_ge(used, RU + 2)
                sp.dma_start(tile[:, :, :], consts[:, c0:c0 + n].rearrange("p (a c) -> p a c", a=tile.shape[1])).then_inc(ret_consts_in, 16)
            c0, _ = CONST_AT["kdec"]
            sp.dma_start(DECS[:, :, :], consts[:, c0:c0 + 3 * RET_HEADS].rearrange("p (a c) -> p a c", a=3)).then_inc(ret_consts_in, 16)
            cw = c_in[0].rearrange("(k p) c -> p k c", p=P)
            V0, G0 = 2 * RET_HEADS * P, 2 * RET_HEADS * P + RET_HEADS * RET_DV

            def load_turn(h, parity):
                first = ret_first(h)
                n = 0
                if parity is not None and not (isinstance(h, int) and h == RET_HEADS):
                    for col in (h * P, h * P + RET_HEADS * P, h * RET_DV + V0, h * RET_DV + V0 + P):
                        load_unit(RU + first + n, (RU + n) % 2, KD, cw[:, :, bass.ds(col, P)])
                        n += 1
                if not (isinstance(h, int) and h == 0):
                    for col in ((h - 1) * RET_DV + G0, (h - 1) * RET_DV + G0 + P):
                        load_unit(RU + first + n, (RU + n) % 2, KD, cw[:, :, bass.ds(col, P)])
                        n += 1

            ret_turns(sp, load_turn)
            sp.wait_ge(rsp_stored, 16 * RET_HEADS + 16)
            sp.wait_ge(rss_stored, 16 * RET_HEADS + 16)
            co = c_out[0].rearrange("(s k p) c -> p s k c", p=P, k=KD)
            with sp.Fori(0, KD // 2) as i:
                for s in range(4):
                    load_unit(unit_at["ret_out"] + 4 * i + s, (unit_at["ret_out"] + s) % 2, KD,
                              co[:, s % 2, :, bass.ds(2 * P * i + P * (s // 2), P)])
            load_up(3)
            load_down(3)
            sp.wait_ge(final_copied.sem, final_copied.value("tok3"))
            store(y_prompt[0].rearrange("(n p) d -> p n d", p=P), YTOK[:, :, :])
            sp.wait_ge(final_copied.sem, final_copied.value("sample"))
            store(y_sample.rearrange("b o d -> (b o) d"), YTOKS[:, :])
            sp.wait_ge(stored, 16 * stores[0])

        @block.gpsimd
        def _(pool):
            def split_unit(unit, slot, nk, raw_count):
                hold(pool, raw_in[slot], 16 * raw_count, 16)
                hold(pool, used, unit + 1)
                pool.tensor_tensor(WHI[:, slot, 0:nk, :], RAW[:, slot, 0:nk, :], ZERO[:, :].broadcast_to([P, nk, P]),
                                   ALU.add).then_inc(hi_split, 1)
                hold(pool, hi_split, unit + 1)
                pool.tensor_tensor(WLO[:, slot, 0:nk, :], RAW[:, slot, 0:nk, :], WHI[:, slot, 0:nk, :].bitcast(F32),
                                   ALU.subtract).then_inc(split, 1)

            def split_phase(name, nk, turns, body):
                u0 = unit_at[name]
                with pool.Fori(0, turns) as i:
                    for s in range(body):
                        split_unit(u0 + body * i + s, (u0 + s) % 2, nk, (body // 2) * i + (u0 + s) // 2 + 1)

            pool.sem_inc(split, 2)
            pool.memset(ZERO[:, :], 0.0).then_inc(zero_set, 1)
            pool.wait_ge(zero_set, 1)
            split_phase("up0", KD, KF // 2, 4)
            split_phase("down0", KH, KD // 2, 4)
            split_phase("ab_in", KD, AB_CH // 4, 4)
            pool.wait_ge(small_in, 32)
            split_unit(AB_UNIT + AB_CH, (AB_UNIT + AB_CH) % 2, KD, (AB_UNIT + AB_CH) // 2 + 1)
            split_phase("ab_out", KD, KD // 2, 2)
            split_phase("up1", KD, KF // 2, 4)
            split_phase("down1", KH, KD // 2, 4)
            split_phase("up2", KD, KF // 2, 4)
            split_phase("down2", KH, KD // 2, 4)
            def split_turn(h, parity):
                first = ret_first(h)
                units = 4 if isinstance(h, int) and h == 0 else 2 if isinstance(h, int) and h == RET_HEADS else 6
                for n in range(units):
                    half_count = (RU + first + n) // 2 if isinstance(h, int) else 3 * h - 1 + (RU + n) // 2
                    split_unit(RU + first + n, (RU + n) % 2, KD, half_count + 1)

            ret_turns(pool, split_turn)
            split_phase("ret_out", KD, KD // 2, 4)
            split_phase("up3", KD, KF // 2, 4)
            split_phase("down3", KH, KD // 2, 4)

        @block.tensor
        def _(pe):
            def project(unit, slot, nk, acc, hi, lo, k0=0, last=True, ready=None):
                hold(pe, split, unit + 3)
                for k in range(nk):
                    if ready is not None:
                        pe.wait_ge(ready[0], ready[1] + k0 + k)
                    first = k == 0 and k0 == 0
                    final = last and k == nk - 1
                    for w, a, opens, closes in ((WHI, hi, True, False), (WHI, lo, False, False), (WLO, hi, False, True)):
                        for n in range(2):
                            ins = pe.matmul(ACC[acc][:, n, 0:HALF], w[:, slot, k, :],
                                            a[:, k0 + k, n * HALF:(n + 1) * HALF],
                                            start=first and opens, stop=final and closes)
                ins.then_inc(used, 1)

            def statistics(r):
                pe.wait_ge(ssq_ready, SSQ_STEPS * (r + 1))
                for n in range(2):
                    ins = pe.matmul(ACC[3][:, n, 0:HALF], ONES[:, :], SSQ[:, n * HALF:(n + 1) * HALF], start=True, stop=True)
                ins.then_inc(stat_done, 1)

            def up(f):
                u0, t0, r = unit_at[f"up{f}"], tile_at[f"up{f}"], NORM_OF[f"up{f}"]
                with pe.Fori(0, KF // 2) as i:
                    for s in range(4):
                        hold(pe, tile_free, t0 + 4 * i + s + 1)
                        if s == 2:
                            pe.wait_ge(std_ready, r + 1)
                        project(u0 + 4 * i + s, (u0 + s) % 2, KD, s, XH, XL, ready=(xl_ready, KD * r + 1))

            def down(name, hi, lo, nk, per_chunk, ready):
                u0, t0 = unit_at[name], tile_at[name]
                with pe.Fori(0, KD // 2) as i:
                    for s in range(2):
                        hold(pe, tile_free, t0 + 2 * i + s + 3)
                        for m in range(per_chunk):
                            n = per_chunk * s + m
                            project(u0 + 2 * per_chunk * i + n, (u0 + n) % 2, nk, s, hi, lo, k0=nk * m,
                                    last=m == per_chunk - 1, ready=ready)

            pe.sem_inc(used, 2)
            pe.sem_inc(vbatch_done, 4)
            pe.wait_ge(consts_in, 64)
            pe.wait_ge(inputs_in, 7 * 16)
            pe.transpose(bank(7, PAR_ROWS), PROWS[0:PAR_ROWS, :], IDENT[0:PAR_ROWS, 0:PAR_ROWS]).then_inc(par_turned, 1)
            for d in range(KD):
                if d >= 4:
                    pe.wait_ge(tile_free, d + 1)
                elif d == 3:
                    pe.wait_ge(par_ready, 1)
                for n in range(NBLK):
                    pe.transpose(ACC[d % 4][:, 0, n * P:(n + 1) * P], XTOK[:, n, d * P:(d + 1) * P], IDENT[:, :])
                pe.transpose(ACC[d % 4][:, 1, 0:DEC], XTOKS[:, d * P:(d + 1) * P], IDENT[0:DEC, 0:DEC]).then_inc(loaded_turned, 1)
            pe.wait_ge(tile_free, KD + 4)
            statistics(0)
            up(0)
            down("down0", HH, HL, KH, 2, (h_ready, 1))
            statistics(1)
            def project_ab(f, s):
                hold(pe, tile_free, AB_TILE + f + 3)
                project(AB_UNIT + f, (AB_UNIT + s) % 2, KD, s % 2, XH, XL, ready=(xl_ready, KD + 1))

            def broadcast_q(b):
                hold(pe, selb_ready, b + 1)
                pe.matmul(bank(4), SELB, QTOK, start=True, stop=True).then_inc(qb_ready, 1)

            for f in range(4):
                project_ab(f, f)
            pe.wait_ge(tile_free, AB_TILE + 8)
            for h in range(FOX_HEADS):
                ins = pe.transpose(bank(5)[0:DEC, h * P:(h + 1) * P], PRJ[:, AB_Q + h, SEQ:TOK], IDENT[:, :])
            ins.then_inc(qtok_turned, 1)
            with pe.Fori(0, (AB_CH - 4) // 8) as i:
                for m in range(8):
                    project_ab(8 * i + (m + 4), m)
                    if m == 0:
                        broadcast_q(2 * i)
                    elif m == 3:
                        broadcast_q(2 * i + 1)
            for b in (EARLY, EARLY + 1):
                broadcast_q(b)
            pe.wait_ge(tile_free, AB_TILE + AB_CH + 3)
            project(AB_UNIT + AB_CH, (AB_UNIT + AB_CH) % 2, KD, 0, XH, XL)

            pe.wait_ge(tile_free, AB_FREE)
            pe.wait_ge(gate_dve.sem, gate_dve.value("gcs"))
            pe.wait_ge(gate_act.sem, gate_act.value("beta"))
            for n in range(NBLK):
                pe.transpose(bank(2)[:, n * P:(n + 1) * P], R[:, n * P:(n + 1) * P], IDENT[:, :])
            gate_pe.done(pe.transpose(bank(3)[0:DEC, 0:P], R[:, SEQ:TOK], IDENT[:, :]), "rt")

            pe.wait_ge(gate_dve.sem, gate_dve.value("rts"))
            for j, ch in enumerate((AB_K, AB_V)):
                for h in range(FOX_HEADS):
                    ins = pe.transpose(bank(j)[0:DEC, h * P:(h + 1) * P], PRJ[:, ch + h, SEQ:TOK], IDENT[:, :])
            fs_pe.done(ins, "tok")
            pe.wait_ge(lf_in, 16 * DEC * N_PAGES)
            lf = LF[:, :, :, :].rearrange("p b g h -> p (b g h)")
            fs_pe.done(pe.matmul(bank(3), LATER[:, :], lf, start=True, stop=True), "later")
            pe.wait_ge(qbr_ready, DEC)
            fs_pe.done(pe.matmul(bank(4), ONES[:, :], lf, start=True, stop=True), "total")
            pe.wait_ge(convrows_in, 16)
            for c in range(CONV_CH):
                rows = DEC * (CONV_W - 1)
                ins = pe.transpose(bank(5)[:, c * rows:(c + 1) * rows], CONVROWS[:, c * P:(c + 1) * P], IDENT[0:rows, 0:rows])
            gp_pe.done(ins, "prev")
            for c in range(CONV_CH):
                ins = pe.transpose(bank((6, 7, 2)[c // 4])[0:DEC + CONV_W - 1, (c % 4) * P:(c % 4 + 1) * P],
                                   PRJ[:, AB_CONV + c, SEQ - CONV_W + 1:TOK], IDENT[:, :])
            gp_pe.done(ins, "tails")
            pe.wait_ge(gp_act.sem, gp_act.value("tail2"))
            pe.wait_ge(fs_dve.sem, fs_dve.value("addlater"))
            with pe.Fori(0, FOX_HEADS) as h:
                def score(q):
                    if q >= 2:
                        await_step(pe, fp_act, f"exp{q - 2}", h)
                    w = (q + 1) * P
                    pe.matmul(bank(q % 2, w), QS[:, q * P:w], PRJ[:, bass.ds(h + AB_K, 1), 0:w].rearrange("p a t -> p (a t)"),
                              start=True, stop=False)
                    pe.matmul(bank(q % 2, w), SELH[:, :], R[:, 0:w], start=False, stop=False)
                    fp_pe.done(pe.matmul(bank(q % 2)[:, q * P:w], IDENT[:, :], MASKNEG[:, :], start=False, stop=True), f"score{q}")

                def turn(q):
                    await_step(pe, fp_dve, f"norm{q}", h)
                    for k in range(q + 1):
                        ins = pe.transpose(bank(2 + q % 2)[:, k * P:(k + 1) * P], PROB[:, q % 2, k * P:(k + 1) * P], IDENT[:, :])
                    fp_pe.done(ins, f"turn{q}")

                def values(q):
                    await_step(pe, fp_act, f"pt{q}", h)
                    for k in range(q + 1):
                        ins = pe.matmul(bank(4)[:, q * P:(q + 1) * P], VT[:, k, :], PTR[:, q % 2, k, :], start=k == 0, stop=k == q)
                    fp_pe.done(ins, f"pv{q}")

                await_step(pe, fp_act, "sel", h)
                for n in range(NBLK):
                    ins = pe.transpose(bank(5)[:, n * P:(n + 1) * P], KS[:, n * P:(n + 1) * P], IDENT[:, :])
                fp_pe.done(ins, "ktok")
                for n in range(NBLK):
                    ins = pe.transpose(bank(6)[:, n * P:(n + 1) * P], VS[:, n * P:(n + 1) * P], IDENT[:, :])
                fp_pe.done(ins, "vtok")
                score(0)
                score(1)
                turn(0)
                values(0)
                score(2)
                turn(1)
                values(1)
                score(3)
                turn(2)
                values(2)
                turn(3)
                values(3)

            pe.wait_ge(fp_dve.sem, fp_dve.value("lo", FOX_HEADS - 1))
            for h in range(FOX_HEADS):
                pe.matmul(bank(4)[:, h * DEC:(h + 1) * DEC], IDENT[:, ROW_LOGF + h:ROW_LOGF + h + 1].broadcast_to([P, P]), R[:, SEQ:TOK], start=True, stop=True)
            pe.wait_ge(fs_dve.sem, fs_dve.value("qk"))
            fs_pe.done(pe.matmul(bank(4)[:, NDH:2 * NDH], ONES[:, :], QKS[:, :, :].rearrange("p b h -> p (b h)"), start=True, stop=True), "snew")
            pe.wait_ge(fs_dve.sem, fs_dve.value("mx"))
            fs_pe.done(pe.transpose(bank(5)[0:NDH, 0:P], MX[:, :, :].rearrange("p b h -> p (b h)"), IDENT[:, :]), "turn")
            pe.wait_ge(fs_dve.sem, fs_dve.value("dg"))
            fs_pe.done(pe.matmul(bank(6, NDH), ONES[0:NDH, :], DG[:, :], start=True, stop=True), "max")
            pe.wait_ge(fs_dve.sem, fs_dve.value("dn"))
            fs_pe.done(pe.matmul(bank(7, NDH), ONES[:, :], DEN[:, :, :].rearrange("p b h -> p (b h)"), start=True, stop=True), "den")
            pe.wait_ge(fs_dve.sem, fs_dve.value("norm"))
            with pe.Fori(0, GDN_HEADS) as h:
                for m, tile in enumerate((SQ, SSQ)):
                    await_step(pe, ln_act, f"sq{m}", h)
                    for n in range(2):
                        ins = pe.matmul(ACC[1 + m][:, n, 0:HALF], ONES[:, :], tile[:, n * HALF:(n + 1) * HALF], start=True, stop=True)
                    ln_pe.done(ins, f"sum{m}")
            def per_head(b, left, right, start=True, stop=True):
                for h in range(GDN_HEADS):
                    ins = pe.matmul(bank(b)[:, h * P:(h + 1) * P], left(h), right(h), start=start, stop=stop)
                return ins

            with pe.Fori(0, NBLK) as c:
                def rows_of(c=c):
                    return R[:, bass.ds(c * P, P)]

                page = [0]

                def values(count):
                    for n in range(page[0], page[0] + count):
                        s, g = n // N_PAGES, n % N_PAGES
                        if n == 0:
                            hold(pe, vo_copied, c + 1)
                        if g % 4 == 0:
                            hold(pe, vpage_in[g // 4], 64 * (2 * c + s + 1), 64)
                        for h in range(FOX_HEADS):
                            ins = pe.matmul(bank(7)[:, s * FOX_HEADS + h:s * FOX_HEADS + h + 1], VPAGES[:, g, h * P:(h + 1) * P],
                                            SC[:, bass.ds(2 * c + s, 1), g, h:h + 1].rearrange("p a c -> p (a c)"),
                                            start=n == 0 and h == 0, stop=g == N_PAGES - 1, skip_group_check=True)
                        if g % 4 == 3:
                            ins.then_inc(vbatch_done, 1)
                    page[0] += count

                await_turns(pe, gl_dve, c)
                await_turns(pe, gl_act, c)
                gl_pe.done(per_head(0, lambda h: IDENT[:, ROW_GC + h:ROW_GC + h + 1].broadcast_to([P, P]), lambda h: rows_of()), "gcb")
                gl_pe.done(per_head(1, lambda h: IDENT[:, ROW_BETA + h:ROW_BETA + h + 1].broadcast_to([P, P]), lambda h: rows_of()), "bb")
                values(2)
                await_step(pe, gl_act, "vts", c)
                for b, tile, name in ((2, KTS, "ktok"), (3, VTS, "vtok")):
                    for h in range(GDN_HEADS):
                        ins = pe.transpose(bank(b)[:, h * P:(h + 1) * P], tile[:, h, :], IDENT[:, :])
                    gl_pe.done(ins, name)
                values(2)
                await_step(pe, gl_dve, "kbt", c)
                gl_pe.done(per_head(4, lambda h: KTS[:, h, :], lambda h: KBT[:, h, :]), "a")
                gl_pe.done(per_head(5, lambda h: KTS[:, h, :], lambda h: PRJ[:, GQ + h, bass.ds(c * P, P)]), "qk")
                for n in range(LEVELS):
                    await_step(pe, gl_dve, f"x{n - 1}" if n else "ats0", c)
                    gl_pe.done(per_head(6, lambda h: ATS[:, h, :], lambda h: XI[:, h, :]), f"t{n}")
                    values(1)
                    if n == 0:
                        continue
                    await_step(pe, gl_act, f"t{n}", c)
                    await_step(pe, gl_dve, f"xt{n - 1}", c)
                    if n < LEVELS - 1:
                        gl_pe.done(per_head(5, lambda h: XIT[:, h, :], lambda h: T1[:, h, :]), f"x{n}")
                    gl_pe.done(per_head(0, lambda h: T1[:, h, :], lambda h: XIT[:, h, :]), f"xt{n}")
                    values(2)
                await_step(pe, gl_dve, f"xt{LEVELS - 1}", c)
                gl_pe.done(per_head(1, lambda h: XIT[:, h, :], lambda h: VB[:, h, :]), "u")
                gl_pe.done(per_head(2, lambda h: KBE[:, h, :], lambda h: XIT[:, h, :]), "wt")
                values(2)
                await_step(pe, gl_act, "wt", c)
                gl_pe.done(per_head(3, lambda h: WT[:, h, :], lambda h: STATE[:, h, :]), "ws")
                values(2 * N_PAGES - page[0])
                await_step(pe, gl_dve, "vn", c)
                for h in range(GDN_HEADS):
                    pe.matmul(bank(4)[:, h * P:(h + 1) * P], STATE[:, h, :], QET[:, h, :], start=True, stop=False)
                    ins = pe.matmul(bank(4)[:, h * P:(h + 1) * P], VNEW[:, h, :], ATTN[:, h, :], start=False, stop=True)
                gl_pe.done(ins, "o")
                gl_pe.done(per_head(5, lambda h: KDE[:, h, :], lambda h: VNEW[:, h, :]), "s")
            pe.wait_ge(gl_dve.sem, gl_dve.value("s", NBLK - 1))
            pe.wait_ge(gl_act.sem, gl_act.value("o", NBLK - 1))
            pe.wait_ge(ss_in, 16 * GDN_HEADS)
            pe.wait_ge(gs_dve.sem, gs_dve.value("qkp"))
            for j in range(NJ):
                ins = pe.matmul(bank(0)[:, 2 * j:2 * j + 2], SS[:, j, :], KQ[:, j, :], start=True, stop=True)
            gs_pe.done(ins, "r")
            for k, row in ((0, ROW_BETA), (1, ROW_GC)):
                for h in range(GDN_HEADS):
                    pe.matmul(bank(1)[:, k * NJ + h * DEC:k * NJ + (h + 1) * DEC], IDENT[:, row + h:row + h + 1].broadcast_to([P, P]),
                              R[:, SEQ:TOK], start=True, stop=True)
            gs_pe.done(pe.matmul(bank(1)[:, 2 * NJ:3 * NJ], ONES[:, :], QKP[:, :, :].rearrange("p h b -> p (h b)"), start=True, stop=True), "bc")
            gs_pe.done(pe.transpose(bank(2)[0:NJ, 0:P], KC[:, :, :].rearrange("p h b -> p (h b)"), IDENT[:, :]), "kt")
            pe.wait_ge(gs_dve.sem, gs_dve.value("a3"))
            gs_pe.done(pe.transpose(bank(3)[0:NJ, 0:P], VN2[:, :, :].rearrange("p h b -> p (h b)"), IDENT[:, :]), "vt")
            pe.wait_ge(gs_act.sem, gs_act.value("vt"))
            for h in range(GDN_HEADS):
                pe.wait_ge(gs_dve.sem, gs_dve.value(f"bd{h}"))
                for n in range(2):
                    ins = pe.matmul(ACC[2 + h % 2][:, n, :], KTK[:, :], VBD[:, h % 2, 4 * n:4 * n + 4, :].rearrange("j b d -> j (b d)"),
                                    start=True, stop=True)
                gs_pe.done(ins, f"up{h}")
            pe.wait_ge(gs_dve.sem, gs_dve.value(f"s{GDN_HEADS - 1}"))
            with pe.Fori(0, GDN_HEADS) as h:
                await_step(pe, go_act, "sq", h)
                for n in range(2):
                    ins = pe.matmul(ACC[0][:, n, 0:HALF], ONES[:, :], SQ[:, n * HALF:(n + 1) * HALF], start=True, stop=True)
                go_pe.done(ins, "sum")
            pe.wait_ge(go_dve.sem, go_dve.value("lo", GDN_HEADS - 1))
            with pe.Fori(0, KD // 2) as i:
                for s in range(2):
                    hold(pe, tile_free, tile_at["ab_out"] + 2 * i + s + 3)
                    project(unit_at["ab_out"] + 2 * i + s, (unit_at["ab_out"] + s) % 2, KD, s, MOH, MOL)
            statistics(2)
            up(1)
            down("down1", HH, HL, KH, 2, (h_ready, KF + 1))
            statistics(3)
            up(2)
            down("down2", HH, HL, KH, 2, (h_ready, 2 * KF + 1))
            statistics(4)
            pe.wait_ge(ret_consts_in, 64)

            def ret_turn(h, p):
                first, is_first, is_last = ret_first(h), isinstance(h, int) and h == 0, isinstance(h, int) and h == RET_HEADS
                g, o = h - 1, 1 - p
                count = [0]

                def tile():
                    n = count[0]
                    count[0] += 1
                    hold(pe, tile_free, RTILE + first + n + 3)
                    project(RU + first + n, (RU + n) % 2, KD, n % 2, XH, XL, ready=(xl_ready, KD * 4 + 1))

                def turned(b, source, name):
                    for n in range(NBLK):
                        ins = pe.transpose(bank(b)[:, n * P:(n + 1) * P], source(n), IDENT[:, :])
                    rm_pe.done(ins, name)

                def update(n):
                    if n >= 2:
                        await_step(pe, rm_dve, f"u{n - 2}", g)
                    for b in range(2):
                        ins = pe.matmul(bank(6 + n % 2)[:, b * RET_DV:(b + 1) * RET_DV], KBLK[:, (2 * n + b) % (DEC // 2), :],
                                        KVT[:, P:3 * P], start=True, stop=True)
                    rm_pe.done(ins, f"r{n}")

                if not is_last:
                    tile()
                if not is_first:
                    hold(pe, tile_free, RTILE + first + 4)
                    await_step(pe, rp_dve, "k", g)
                    hold(pe, states_stepped, g + 1)
                    turned(4, lambda n: KB[o][:, n * P:(n + 1) * P], "ktok")
                    turned(5, lambda n: VBH[o][:, 0, n * P:(n + 1) * P], "v0")
                    turned(6, lambda n: VBH[o][:, 1, n * P:(n + 1) * P], "v1")
                    for n in range(NBLK):
                        ins = pe.matmul(bank(7)[:, n * P:(n + 1) * P], KB[o][:, n * P:(n + 1) * P], QB[o][:, n * P:(n + 1) * P],
                                        start=True, stop=True)
                    rm_pe.done(ins, "a")
                if not is_last:
                    tile()
                if not is_first:
                    await_step(pe, rm_dve, "att", g)
                    await_step(pe, rm_act, "vt1", g)
                    for n in range(NBLK):
                        ins = pe.matmul(bank(6 + n // 2)[:, (n % 2) * RET_DV:(n % 2 + 1) * RET_DV], KD_[:, n, :], VTK_R[:, n, :],
                                        start=True, stop=True)
                    rm_pe.done(ins, "kv")
                if not is_last:
                    tile()
                if not is_first:
                    await_step(pe, rm_dve, "s3", g)
                    for v in range(2):
                        for n in range(NBLK):
                            out = bank(4 + v)[:, n * P:(n + 1) * P]
                            ins = pe.matmul(out, VTK_R[:, n, v * P:(v + 1) * P], ATT[:, n * P:(n + 1) * P], start=True, stop=n == 0)
                            if n > 0:
                                ins = pe.matmul(out, SALL[n - 1][:, v * P:(v + 1) * P], QB[o][:, n * P:(n + 1) * P],
                                                start=False, stop=True)
                    rm_pe.done(ins, "o")
                    hold(pe, rss_in, 16 * g + 16, 16)
                    for b in range(DEC):
                        for v in range(2):
                            pe.matmul(bank(6)[:, v * DEC + b:v * DEC + b + 1], SSR[:, b, v * P:(v + 1) * P], QSD[:, b:b + 1],
                                      start=True, stop=True)
                    rm_pe.done(pe.matmul(bank(6)[:, 2 * DEC:3 * DEC], ONES[:, :], QKR[:, :], start=True, stop=True), "cross")
                if not is_last:
                    tile()
                if not is_first:
                    await_step(pe, rm_act, "o1", g)
                    await_step(pe, rm_dve, "os", g)
                    for n in range(2):
                        for v in range(2):
                            ins = pe.matmul(ACC[2][:, n, 0:HALF], ONES[:, :], VBH[o][:, v, n * HALF:(n + 1) * HALF],
                                            start=v == 0, stop=v == 1)
                    rm_pe.done(ins, "mean")
                    pe.transpose(bank(7)[0:DEC, 0:P], KB[o][:, SEQ:TOK], IDENT[:, :])
                    for v in range(2):
                        ins = pe.transpose(bank(7)[0:DEC, (v + 1) * P:(v + 2) * P], VSC[:, v, :], IDENT[:, :])
                    rm_pe.done(ins, "tok")
                    tile()
                    await_step(pe, rm_act, "sq1", g)
                    for n in range(2):
                        for v, squares in enumerate((SQ, SSQ)):
                            ins = pe.matmul(ACC[2][:, n, 0:HALF], ONES[:, :], squares[:, n * HALF:(n + 1) * HALF],
                                            start=v == 0, stop=v == 1)
                    rm_pe.done(ins, "var")
                    await_step(pe, rm_dve, "kb0", g)
                    update(0)
                    update(1)
                    tile()
                    await_step(pe, rm_dve, "kb1", g)
                    update(2)
                    update(3)

            ret_turns(pe, ret_turn)
            pe.wait_ge(rm_dve.sem, rm_dve.value("lo1", RET_HEADS - 1))
            down("ret_out", RMOH, RMOL, KD, 2, None)
            statistics(5)
            up(3)
            down("down3", HH, HL, KH, 2, (h_ready, 3 * KF + 1))
            statistics(6)
            for n in range(NBLK):
                for d in range(KD):
                    pe.wait_ge(y_ready, d + 1)
                    if n >= 2 and d == 0:
                        pe.wait_ge(final_copied.sem, n - 1)
                    ins = pe.transpose(ACC[n % 2][:, d // 4, (d % 4) * P:(d % 4 + 1) * P], YF[:, d, n * P:(n + 1) * P], IDENT[:, :])
                ins.then_inc(final_turned, 1)
            for d in range(KD):
                ins = pe.transpose(ACC[2][0:DEC, d // 4, (d % 4) * P:(d % 4 + 1) * P], YF[:, d, SEQ:TOK], IDENT[:, :])
            ins.then_inc(final_turned, 1)

        @block.scalar
        def _(act):
            def norm_chunk(r, d):
                n = KD * r + d
                hold(act, tile_free, tile_at_update[r] + d + 5)
                hold(act, ssq_ready, SSQ_STEPS * r + d + 1)
                act.activation(SQ[:, :], X[:, bass.ds(d, 1), :].rearrange("p a t -> p (a t)"), ACT.Square).then_inc(sq_ready, 1)
                act.activation(XH[:, bass.ds(d, 1), :].rearrange("p a t -> p (a t)"),
                               X[:, bass.ds(d, 1), :].rearrange("p a t -> p (a t)"), ACT.Identity,
                               scale=PAR[:, bass.ds(PAR_NORM + KD * r + d, 1)]).then_inc(xh_ready, 1)

            def load_logf(first, count):
                pairs = LF[:, :, :, :].rearrange("p b g h -> p (b g) h")
                for n in range(count):
                    page = act.value_load(PT_SB[0:1, bass.ds(first + n, 1)], min_val=0, max_val=N_POOL - 1)
                    act.dma_start(pairs[:, bass.ds(first + n, 1), :].rearrange("p a h -> p (a h)"),
                                  cache_logf[0, bass.ds(page, 1)].rearrange("a t h -> (a t) h")).then_inc(lf_in, 16)

            def norm_chunks(r, logf_first=None, logf_count=0):
                with act.Fori(0, KD) as d:
                    norm_chunk(r, d)
                    if logf_count:
                        load_logf(logf_count * d + logf_first, logf_count)

            def deviation(r):
                act.wait_ge(stat_done, r + 1)
                act.activation(halves(RSTD[:, :]), ACC[3][:, :, 0:HALF], ACT.Sqrt, bias=EPSC[:, 0:1],
                               scale=1.0 / D_MODEL).then_inc(std_ready, 1)

            def up(f, logf_count=0):
                t0 = tile_at[f"up{f}"]
                with act.Fori(0, KF) as j:
                    hold(act, tile_free, t0 + 2 * j + 5)
                    act.activation(TA[:, :], TA[:, :], ACT.Silu).then_inc(act_ready, 1)
                    hold(act, hfull_ready, KF * f + j + 1)
                    act.activation(HH[:, bass.ds(j, 1), :].rearrange("p a t -> p (a t)"), TH[:, :], ACT.Copy).then_inc(hh_ready, 1)
                    if logf_count:
                        load_logf(logf_count * j, logf_count)

            for steps in OPENED["act"]:
                act.sem_inc(steps.sem, 1)
            act.sem_inc(vo_copied, 1)
            act.wait_ge(par_turned, 1)
            act.activation(PAR[:, 0:PAR_ROWS], bank(7, PAR_ROWS), ACT.Copy).then_inc(par_ready, 1)
            act.wait_ge(par_ready, 1)
            act.wait_ge(ones_set, 4)
            norm_chunks(0)
            deviation(0)
            act.wait_ge(pt_in, 16)
            up(0, 4)
            norm_chunks(1, 4 * KF, 5)
            deviation(1)
            def select(b):
                act.activation(SELB, IDENT[0:DEC, bass.ds(b, 1)].broadcast_to([DEC, P]), ACT.Copy).then_inc(selb_ready, 1)

            def keep_q(b, parity, multiplied):
                hold(act, qb_ready, b + 1)
                hold(act, prod_done, multiplied)
                act.activation(QBR[:, parity, :], bank(4), ACT.Copy).then_inc(qbr_ready, 1)

            act.wait_ge(qtok_turned, 1)
            act.activation(QTOK, bank(5)[0:DEC, :], ACT.Copy).then_inc(qtok_ready, 1)
            select(0)
            act.wait_ge(used, AB_UNIT + 2)
            act.wait_ge(pt_in, 16)
            with act.Fori(0, EARLY // 2) as i:
                for s in range(2):
                    keep_q(2 * i + s, s, 8 * i + s + 1)
                    select(2 * i + s + 1)
                    for m in range(4 * s, 4 * s + 4):
                        load_keys(act, 0, m % 2, KBATCH * (8 * i + m), 8 * i + m)
            keep_q(EARLY, 0, 4 * (EARLY - 1) + 2)
            select(EARLY + 1)
            keep_q(EARLY + 1, 1, 4 * EARLY + 2)
            act.wait_ge(cols_in, 48)
            gate_act.done(act.activation(COLS[ROW_GC:ROW_GC + 4, 3:4], COLS[ROW_GC:ROW_GC + 4, 1:2], ACT.Exp), "fac")
            act.wait_ge(gate_dve.sem, gate_dve.value("az"))
            gate_act.done(act.activation(TB[:, :], TB[:, :], ACT.Exp, scale=-1.0), "e")
            act.wait_ge(gate_act.sem, gate_act.value("e"))
            gate_act.done(act.activation(TB[:, :], TB[:, :], ACT.Ln, bias=EPSC[:, 2:3]), "l")
            act.wait_ge(gate_dve.sem, gate_dve.value("t"))
            gate_act.done(act.activation(R[ROW_BETA:ROW_BETA + 4, :], TH[ROW_BETA:ROW_BETA + 4, :], ACT.Exp), "beta")

            act.wait_ge(fs_pe.sem, fs_pe.value("tok"))
            fs_act.done(act.activation(KTOKS[:, :], bank(0)[0:DEC, :], ACT.Copy), "ktok")
            fs_act.done(act.activation(VTOKS, bank(1)[0:DEC, :], ACT.Copy), "vtok")
            act.wait_ge(gp_pe.sem, gp_pe.value("prev"))
            gp_act.done(act.activation(PREV[:, :, :, :].rearrange("p c b w -> p (c b w)"), bank(5, CONV_CH * DEC * (CONV_W - 1)), ACT.Copy), "prev")
            act.wait_ge(gp_pe.sem, gp_pe.value("tails"))
            for n, b in enumerate((6, 7, 2)):
                gp_act.done(act.activation(TAILS[:, n * 512:(n + 1) * 512], bank(b)[0:DEC + CONV_W - 1, :], ACT.Copy), f"tail{n}")
            with act.Fori(0, FOX_HEADS) as h:
                def chunk(first):
                    return PRJ[:, bass.ds(h + first, 1), 0:SEQ].rearrange("p a t -> p (a t)")

                def exponent(q):
                    await_step(act, fp_dve, f"neg{q}", h)
                    fp_act.done(act.activation(PROB[:, q % 2, 0:(q + 1) * P], bank(q % 2, (q + 1) * P), ACT.Exp,
                                               bias=STAT[:, q % 2, 1:2], accum_out=STAT[:, q % 2, 2:3]), f"exp{q}")

                def turned(q):
                    await_step(act, fp_pe, f"turn{q}", h)
                    fp_act.done(act.activation(PTR[:, q % 2, 0:q + 1, :].rearrange("p k q -> p (k q)"),
                                               bank(2 + q % 2, (q + 1) * P), ACT.Copy), f"pt{q}")

                fp_act.done(act.activation(QS[:, :], chunk(AB_Q), ACT.Copy, scale=SCALE), "q")
                fp_act.done(act.activation(KS[:, :], chunk(AB_K), ACT.Copy), "k")
                fp_act.done(act.activation(VS[:, :], chunk(AB_V), ACT.Copy), "v")
                fp_act.done(act.activation(SELH[:, :], IDENT[:, bass.ds(h + ROW_NEGC, 1)].broadcast_to([P, P]), ACT.Copy), "sel")
                await_step(act, fp_pe, "ktok", h)
                hold(act, fk_stored, 16 * h + 16, 16)
                fp_act.done(act.activation(TA[:, 0:SEQ], bank(5), ACT.Copy), "ktok")
                exponent(0)
                exponent(1)
                turned(0)
                exponent(2)
                turned(1)
                exponent(3)
                turned(2)
                turned(3)
                await_step(act, fp_pe, "pv3", h)
                fp_act.done(act.activation(MOH[:, bass.ds(h, 1), 0:SEQ].rearrange("p a t -> p (a t)"), bank(4), ACT.Copy), "hi")

            act.wait_ge(fk_stored, 16 * FOX_HEADS + 16)
            act.wait_ge(fv_stored, 16 * FOX_HEADS + 16)
            def whole(chunk):
                return PRJ[:, bass.ds(chunk, 1), :].rearrange("p a t -> p (a t)")

            act.wait_ge(cv_dve.sem, cv_dve.value("w3", CONV_CH - 1))
            with act.Fori(0, CONV_CH + GDN_HEADS) as c:
                act.activation(whole(c + AB_CONV), whole(c + AB_CONV), ACT.Silu).then_inc(cv_act, 1)
            act.wait_ge(fs_dve.sem, fs_dve.value("sub"))
            sc = SC[:, :, :, :].rearrange("p b g h -> p (b g h)")
            fs_act.done(act.activation(sc, sc, ACT.Exp), "exp")
            act.wait_ge(fs_dve.sem, fs_dve.value("subn"))
            sn = SN[:, :, :].rearrange("p b h -> p (b h)")
            fs_act.done(act.activation(sn, sn, ACT.Exp), "expn")
            act.wait_ge(cv_act, CONV_CH + GDN_HEADS)
            with act.Fori(0, GDN_HEADS) as h:
                for m, (tile, chunk) in enumerate(((SQ, GQ), (SSQ, GK))):
                    await_turns(act, ln_dve, h)
                    ln_act.done(act.activation(tile[:, :], whole(h + chunk), ACT.Square), f"sq{m}")
                for m, (tile, chunk) in enumerate(((TA, GQ), (TB, GK))):
                    await_step(act, ln_pe, f"sum{m}", h)
                    ln_act.done(act.activation(halves(tile[:, :]), ACC[1 + m][:, :, 0:HALF], ACT.Sqrt,
                                               bias=EPSC[:, 1 - m:2 - m], scale=float(P) if m == 0 else 1.0), f"std{m}")
            act.wait_ge(ln_dve.sem, ln_dve.value("mul1", GDN_HEADS - 1))
            act.wait_ge(tails_stored, 32)
            with act.Fori(0, NBLK) as c:
                def chunk_of(first):
                    return PRJ[:, first:first + GDN_HEADS, bass.ds(c * P, P)]

                await_turns(act, gl_dve, c)
                gl_act.done(act.activation(KTS[:, :, :], chunk_of(GK), ACT.Copy), "kts")
                gl_act.done(act.activation(VTS[:, :, :], chunk_of(GV), ACT.Copy), "vts")
                await_step(act, gl_dve, "gd", c)
                gl_act.done(act.activation(GAM[:, :, :], GAM[:, :, :], ACT.Exp), "gam")
                gl_act.done(act.activation(EG[:, :, :].rearrange("p h i -> p (h i)"), bank(0), ACT.Exp), "eg")
                gl_act.done(act.activation(KDC[:, :], KDC[:, :], ACT.Exp), "kdc")
                gl_act.done(act.activation(EGC[:, :], RT[:, bass.ds(c, 1), ROW_GC:ROW_GC + 4].rearrange("p a h -> p (a h)"), ACT.Exp), "egc")
                for n in range(1, LEVELS):
                    await_step(act, gl_pe, f"t{n}", c)
                    gl_act.done(act.activation(T1[:, :, :].rearrange("p h i -> p (h i)"), bank(6), ACT.Copy), f"t{n}")
                await_step(act, gl_pe, "u", c)
                gl_act.done(act.activation(VNEW[:, :, :].rearrange("p h i -> p (h i)"), bank(1), ACT.Copy), "u")
                await_step(act, gl_pe, "wt", c)
                gl_act.done(act.activation(WT[:, :, :].rearrange("p h i -> p (h i)"), bank(2), ACT.Copy), "wt")
                await_step(act, gl_pe, "o", c)
                gl_act.done(act.activation(chunk_of(GQ), bank(4).rearrange("p (h i) -> p h i", h=GDN_HEADS), ACT.Copy), "o")
                hold(act, vbatch_done, 8 * c + 12)
                act.activation(OS[:, :, bass.ds(2 * c, 2)], bank(7, 2 * FOX_HEADS).rearrange("p (s h) -> p h s", s=2), ACT.Copy).then_inc(vo_copied, 1)
            act.wait_ge(fs_dve.sem, fs_dve.value("add"))
            fs_act.done(act.activation(MOH[:, 0:FOX_HEADS, SEQ:TOK], OS[:, :, :], ACT.Copy), "hi")
            act.wait_ge(gs_pe.sem, gs_pe.value("bc"))
            gs_act.done(act.activation(EGS[:, :, :].rearrange("p h b -> p (h b)"), bank(1)[:, NJ:2 * NJ], ACT.Exp), "egs")
            gs_act.done(act.activation(BEQ[:, :, :].rearrange("p n j -> p (n j)"), bank(1, 3 * NJ), ACT.Copy), "beq")
            act.wait_ge(gs_pe.sem, gs_pe.value("kt"))
            gs_act.done(act.activation(KTK[:, :], bank(2)[0:NJ, 0:P], ACT.Copy), "kt")
            act.wait_ge(gs_pe.sem, gs_pe.value("vt"))
            gs_act.done(act.activation(VTK[:, :], bank(3)[0:NJ, 0:P], ACT.Copy), "vt")
            act.wait_ge(gs_dve.sem, gs_dve.value("o3"))
            with act.Fori(0, GDN_HEADS) as h:
                await_turns(act, go_dve, h)
                go_act.done(act.activation(SQ[:, :], whole(h + GQ), ACT.Square), "sq")
                await_step(act, go_pe, "sum", h)
                go_act.done(act.activation(halves(TA[:, :]), ACC[0][:, :, 0:HALF], ACT.Sqrt, bias=EPSC[:, 0:1], scale=1.0 / P), "std")
                await_step(act, go_dve, "gate", h)
                go_act.done(act.activation(MOH[:, bass.ds(h + FOX_HEADS, 1), :].rearrange("p a t -> p (a t)"), TH[:, :], ACT.Copy), "hi")
            act.wait_ge(gdn_stored, 1)
            norm_chunks(2)
            deviation(2)
            up(1)
            norm_chunks(3)
            deviation(3)
            up(2)
            norm_chunks(4)
            deviation(4)
            act.wait_ge(ret_consts_in, 64)

            def ret_turn(h, p):
                first, is_first, is_last = ret_first(h), isinstance(h, int) and h == 0, isinstance(h, int) and h == RET_HEADS
                g, o = h - 1, 1 - p

                def swap(n, name):
                    hold(act, tile_free, RTILE + first + n + 5)
                    act.activation(TB[0:64, :], TA[64:P, :], ACT.Copy)
                    rp_act.done(act.activation(TB[64:P, :], TA[0:64, :], ACT.Copy), name)

                def gate(v):
                    gated = RGATE[:, bass.ds(2 * g + v, 1), :].rearrange("p a t -> p (a t)")
                    await_step(act, rm_dve, f"ga{v}", g)
                    rm_act.done(act.activation(gated, gated, ACT.Silu), f"si{v}")
                    await_step(act, rm_dve, f"g{v}", g)
                    rm_act.done(act.activation(RMOH[:, bass.ds(2 * g + v, 1), :].rearrange("p a t -> p (a t)"), VBH[o][:, v, :], ACT.Copy), f"hi{v}")

                if not is_last:
                    swap(0, "q")
                if not is_first:
                    await_step(act, rm_pe, "v1", g)
                    for v in range(2):
                        rm_act.done(act.activation(VTK_R[:, :, v * P:(v + 1) * P], bank(5 + v).rearrange("p (n d) -> p n d", n=NBLK),
                                                   ACT.Copy), f"vt{v}")
                if not is_last:
                    swap(1, "k")
                if not is_first:
                    hold(act, rss_stored, 16 * g + 16, 16)
                    act.dma_start(SSR[:, :, :], state_ret[0][:, bass.ds(g, 1)].rearrange("b a k v -> k b (a v)")).then_inc(rss_in, 16)
                    await_step(act, rm_dve, "s3", g)
                    act.dma_start(rs_prompt[0, 0, bass.ds(g, 1)].rearrange("a k v -> (a k) v"), SALL[NBLK - 1][:, :]).then_inc(rsp_stored, 16)
                    await_step(act, rm_pe, "o", g)
                    await_step(act, rm_dve, "vsc", g)
                    for v in range(2):
                        rm_act.done(act.activation(VBH[o][:, v, 0:SEQ], bank(4 + v), ACT.Copy), f"o{v}")
                    await_step(act, rm_pe, "tok", g)
                    rm_act.done(act.activation(KVT[:, :], bank(7)[0:DEC, 0:3 * P], ACT.Copy), "tk")
                    for v, (squares, name) in enumerate(((SQ, "c0"), (SSQ, "c1"))):
                        await_step(act, rm_dve, name, g)
                        rm_act.done(act.activation(squares[:, :], VBH[o][:, v, :], ACT.Square), f"sq{v}")
                    await_step(act, rm_pe, "var", g)
                    rm_act.done(act.activation(halves(TB[:, :]), ACC[2][:, :, 0:HALF], ACT.Sqrt, bias=EPSC[:, 0:1],
                                               scale=1.0 / RET_DV), "std")
                    gate(0)
                    gate(1)
                    hold(act, states_stepped, g + 2)
                    act.dma_start(rs_sample[0][:, bass.ds(g, 1)].rearrange("b a k v -> k b (a v)"), SSR[:, :, :]).then_inc(rss_stored, 16)

            ret_turns(act, ret_turn)
            norm_chunks(5)
            deviation(5)
            up(3)
            norm_chunks(6)
            deviation(6)
            for n in range(NBLK):
                act.wait_ge(final_turned, n + 1)
                final_copied.done(act.activation(YTOK[:, n, :].rearrange("p (h c) -> p h c", h=2), ACC[n % 2][:, :, :], ACT.Copy), f"tok{n}")
            act.wait_ge(final_turned, NBLK + 1)
            final_copied.done(act.activation(YTOKS[:, :].rearrange("p (h c) -> p h c", h=2), ACC[2][0:DEC, :, :], ACT.Copy), "sample")

        @block.vector
        def _(dve):
            def clear_squares(r):
                if r >= 1:
                    dve.wait_ge(stat_done, r)
                dve.memset(SSQ[:, :], 0.0).then_inc(ssq_ready, 1)

            def norm_chunk(r, d):
                n = KD * r + d
                hold(dve, sq_ready, n + 1)
                hold(dve, ssq_ready, SSQ_STEPS * r + d + 1)
                dve.tensor_tensor(SSQ[:, :], SSQ[:, :], SQ[:, :], ALU.add).then_inc(ssq_ready, 1)
                hold(dve, xh_ready, n + 1)
                dve.scalar_tensor_tensor(out=XL[:, bass.ds(d, 1), :].rearrange("p a t -> p (a t)"),
                                         in0=X[:, bass.ds(d, 1), :].rearrange("p a t -> p (a t)"),
                                         scalar=PAR[:, bass.ds(PAR_NORM + KD * r + d, 1)],
                                         in1=XH[:, bass.ds(d, 1), :].rearrange("p a t -> p (a t)").bitcast(F32),
                                         op0=ALU.mult, op1=ALU.subtract).then_inc(xl_ready, 1)

            def update(name, scale, per_chunk=2):
                u0, r = unit_at[name], UPDATE[name]
                clear_squares(r)
                with dve.Fori(0, KD // 2) as i:
                    for s in range(2):
                        d = 2 * i + s
                        hold(dve, used, u0 + per_chunk * d + per_chunk + 2)
                        xd = X[:, bass.ds(d, 1), :].rearrange("p a (n t) -> p (a n) t", n=2)
                        dve.scalar_tensor_tensor(out=xd, in0=ACC[s][:, :, 0:HALF], scalar=scale, in1=xd,
                                                 op0=ALU.mult, op1=ALU.add).then_inc(tile_free, 1)
                        norm_chunk(r, d)

            def reciprocal(r):
                dve.wait_ge(std_ready, r + 1)
                dve.reciprocal(RSTD[:, :], RSTD[:, :]).then_inc(rstd_ready, 1)
                dve.wait_ge(rstd_ready, r + 1)

            def up(f):
                t0, u0 = tile_at[f"up{f}"], unit_at[f"up{f}"]
                with dve.Fori(0, KF // 2) as i:
                    for s in range(2):
                        t = t0 + 4 * i + 2 * s
                        n = KF * f + 2 * i + s
                        hold(dve, used, u0 + 4 * i + 2 * s + 3)
                        dve.tensor_tensor(halves(TA[:, :]), ACC[2 * s][:, :, 0:HALF], halves(RSTD[:, :]),
                                          ALU.mult).then_inc(tile_free, 1)
                        hold(dve, used, u0 + 4 * i + 2 * s + 4)
                        dve.tensor_tensor(halves(TB[:, :]), ACC[2 * s + 1][:, :, 0:HALF], halves(RSTD[:, :]),
                                          ALU.mult).then_inc(tile_free, 1)
                        hold(dve, act_ready, n + 1)
                        hold(dve, tile_free, t + 6)
                        dve.tensor_tensor(TH[:, :], TA[:, :], TB[:, :], ALU.mult).then_inc(hfull_ready, 1)
                        hold(dve, hh_ready, n + 1)
                        dve.tensor_tensor(HL[:, bass.ds(2 * i + s, 1), :].rearrange("p a t -> p (a t)"), TH[:, :],
                                          HH[:, bass.ds(2 * i + s, 1), :].rearrange("p a t -> p (a t)").bitcast(F32),
                                          ALU.subtract).then_inc(h_ready, 1)

            dve.sem_inc(tile_free, 4)
            dve.sem_inc(states_stepped, 1)
            for steps in OPENED["dve"]:
                dve.sem_inc(steps.sem, 1)
            dve.memset(ONES[:, :], 1.0).then_inc(ones_set, 1)
            dve.memset(EPSC[:, 0:1], EPS).then_inc(ones_set, 1)
            dve.memset(EPSC[:, 1:2], P * EPS).then_inc(ones_set, 1)
            dve.memset(EPSC[:, 2:3], 1.0).then_inc(ones_set, 1)
            dve.memset(COLS[:, 0:2], 0.0).then_inc(cols_clear, 1)
            dve.memset(COLS[:, 2:3], 1.0).then_inc(cols_clear, 1)
            dve.memset(COLS[:, 3:4], 0.0).then_inc(cols_clear, 1)
            dve.wait_ge(cols_clear, 3)
            dve.memset(COLS[ROW_GC:ROW_GC + 4, 2:3], -1.0).then_inc(cols_clear, 1)
            dve.memset(COLS[ROW_LOGF:ROW_LOGF + 4, 3:4], 1.0).then_inc(cols_clear, 1)
            dve.sem_inc(prod_done, 2)
            dve.sem_inc(sum_done, 1)
            dve.wait_ge(par_ready, 1)
            clear_squares(0)
            for d in range(KD + 1):
                if d >= 1:
                    norm_chunk(0, d - 1)
                if d == KD:
                    break
                dve.wait_ge(loaded_turned, d + 1)
                dve.tensor_copy(X[:, d, 0:SEQ], ACC[d % 4][:, 0, 0:SEQ]).then_inc(x_part, 1)
                dve.wait_ge(x_part, d + 1)
                dve.tensor_copy(X[:, d, SEQ:TOK], ACC[d % 4][:, 1, 0:DEC]).then_inc(tile_free, 1)
            reciprocal(0)
            up(0)
            update("down0", 0.5)
            reciprocal(1)
            def take(f, s):
                hold(dve, used, AB_UNIT + f + 3)
                dve.tensor_tensor(PRJ[:, bass.ds(f, 1), :].rearrange("p a (n t) -> p (a n) t", n=2),
                                  ACC[s % 2][:, :, 0:HALF], halves(RSTD[:, :]), ALU.mult).then_inc(tile_free, 1)

            def key_scores(place, slot, n, b, scores):
                sem_count = 16 * KBATCH
                hold(dve, kpage_in[slot], sem_count * n[1] + sem_count, sem_count)
                hold(dve, qbr_ready, b + 1)
                hold(dve, sum_done, n[0] + 1)
                dve.tensor_tensor(PROD[place][:, :, :], KPAGES[place][:, slot, :, :],
                                  QBR[:, n[2]:n[2] + 1, :].broadcast_to([P, KBATCH, FOX_HEADS * P]), ALU.mult).then_inc(prod_done, 1)
                hold(dve, prod_done, n[0] + 3)
                dve.tensor_reduce(scores, PROD[place][:, :, :].rearrange("p g (h d) -> p g h d", h=FOX_HEADS),
                                  AX, ALU.add).then_inc(sum_done, 1)

            for f in range(4):
                take(f, f)
            with dve.Fori(0, (AB_CH - 4) // 8) as i:
                for m in range(8):
                    take(8 * i + (m + 4), m)
                    g = KBATCH * (m % 4)
                    key_scores(0, m % 2, (8 * i + m, 4 * i + m // 2, m // 4), 2 * i + m // 4,
                               SC[:, bass.ds(2 * i + m // 4, 1), g:g + KBATCH, :].rearrange("p a g h -> p (a g) h"))
            dve.memset(R[:, :], 0.0).then_inc(clear_r, 1)
            dve.wait_ge(clear_r, 1)
            dve.wait_ge(cols_in, 48)
            dve.wait_ge(cols_clear, 5)
            dve.wait_ge(used, AB_UNIT + AB_CH + 3)
            dve.tensor_tensor(halves(TA[:, :]), ACC[0][:, :, 0:HALF], halves(RSTD[:, :]), ALU.mult).then_inc(tile_free, 1)

            dve.wait_ge(qbr_ready, DEC)
            dve.wait_ge(tile_free, AB_FREE)
            gate_dve.done(dve.tensor_scalar(TA[:, :], TA[:, :], COLS[:, 0:1], None, ALU.add), "z")
            dve.wait_ge(gate_dve.sem, gate_dve.value("z"))
            gate_dve.done(dve.scalar_tensor_tensor(out=TB[:, :], in0=TA[:, :], scalar=-1.0, in1=TA[:, :], op0=ALU.mult, op1=ALU.max), "az")
            dve.wait_ge(gate_act.sem, gate_act.value("l"))
            dve.tensor_scalar(TH[:, :], TA[:, :], COLS[:, 2:3], 0.0, ALU.mult, ALU.min).then_inc(clear_r, 1)
            dve.wait_ge(clear_r, 2)
            gate_dve.done(dve.tensor_tensor(TH[:, :], TH[:, :], TB[:, :], ALU.subtract), "t")
            dve.wait_ge(gate_dve.sem, gate_dve.value("t"))
            gate_dve.done(dve.tensor_scalar(TA[:, :], TH[:, :], COLS[:, 3:4], None, ALU.mult), "g")
            dve.wait_ge(gate_dve.sem, gate_dve.value("g"))
            lo, hi = ROW_LOGF, ROW_LOGF + 4
            gate_dve.done(dve.tensor_copy(R[lo:hi, :], TA[lo:hi, :]), "logf")
            gate_dve.done(dve.tensor_tensor_scan(SQ[lo:hi, 0:SEQ], ONES[lo:hi, 0:1].broadcast_to([4, SEQ]), TA[lo:hi, 0:SEQ],
                                                 0.0, ALU.mult, ALU.add), "c")
            dve.wait_ge(gate_dve.sem, gate_dve.value("c"))
            gate_dve.done(dve.tensor_scalar(R[ROW_NEGC:ROW_NEGC + 4, 0:SEQ], SQ[lo:hi, 0:SEQ], -1.0, None, ALU.mult), "negc")
            lo, hi = ROW_GC, ROW_GC + 4
            for n in range(NBLK):
                gate_dve.done(dve.tensor_tensor_scan(R[lo:hi, n * P:(n + 1) * P], ONES[lo:hi, :], TA[lo:hi, n * P:(n + 1) * P],
                                                     0.0, ALU.mult, ALU.add), f"gc{n}")
            gate_dve.done(dve.tensor_copy(R[lo:hi, SEQ:TOK], TA[lo:hi, SEQ:TOK]), "gcs")
            dve.wait_ge(gate_pe.sem, gate_pe.value("rt"))
            gate_dve.done(dve.tensor_copy(RT[:, :, :].rearrange("p n c -> p (n c)"), bank(2)), "rt")
            gate_dve.done(dve.tensor_copy(RTS[:, :], bank(3)[0:DEC, 0:P]), "rts")

            def chain(ins, name):
                fs_dve.done(ins, name)
                dve.wait_ge(fs_dve.sem, fs_dve.value(name))

            def by_head(chunk):
                return PRJ[:, chunk:chunk + FOX_HEADS, SEQ:TOK].rearrange("p h b -> p b h")

            def over_pages(tile):
                return tile[:, :, None, :].broadcast_to([P, DEC, N_PAGES, FOX_HEADS])

            dve.wait_ge(fs_pe.sem, fs_pe.value("total"))
            chain(dve.memset(SUF[:, :, 15, :], 0.0), "suf15")
            total = bank(4).rearrange("p (b g h) -> p b g h", g=N_PAGES, h=FOX_HEADS)
            for g in range(14, -1, -1):
                chain(dve.tensor_tensor(SUF[:, :, g, :], total[:, :, g + 1, :], SUF[:, :, g + 1, :], ALU.add), f"suf{g}")
            suf = SUF[:, :, :, :].rearrange("p b g h -> p (b g h)")
            chain(dve.tensor_tensor(suf, bank(3), suf, ALU.add), "addlater")

            dve.wait_ge(gp_act.sem, gp_act.value("prev"))
            dve.wait_ge(gp_pe.sem, gp_pe.value("tails"))
            with dve.Fori(0, FOX_HEADS) as h:
                def keys(m):
                    key_scores(1, m, (2 * h + (4 * EARLY + m), h + 2 * EARLY, m), EARLY + m, SC[:, EARLY + m, bass.ds(KBATCH * h, KBATCH), :])

                def convolve(j):
                    c, tile = 3 * h + j, (SQ, SSQ, TH)[j]
                    source = PRJ[:, bass.ds(c + AB_CONV, 1), :].rearrange("p a t -> p (a t)")

                    def tap(w):
                        return PAR[:, bass.ds(c + PAR_CONV + CONV_CH * w, 1)]

                    cv_dve.done(dve.memset(tile[:, 0:CONV_W - 1], 0.0), "z")
                    for s in range(CONV_W - 1, 0, -1):
                        k = CONV_W - 1 - s
                        prev = PREV[:, bass.ds(c, 1), :, k:k + 1].rearrange("p a b w -> p (a b w)")
                        if k == 0:
                            cv_dve.done(dve.tensor_scalar(tile[:, s:SEQ], source[:, 0:SEQ - s], tap(k), None, ALU.mult), f"p{s}")
                            cv_dve.done(dve.tensor_scalar(tile[:, SEQ:TOK], prev, tap(k), None, ALU.mult), f"s{k}")
                            continue
                        await_step(dve, cv_dve, f"s{k - 1}", c)
                        cv_dve.done(dve.scalar_tensor_tensor(out=tile[:, s:SEQ], in0=source[:, 0:SEQ - s], scalar=tap(k),
                                                             in1=tile[:, s:SEQ], op0=ALU.mult, op1=ALU.add), f"p{s}")
                        cv_dve.done(dve.scalar_tensor_tensor(out=tile[:, SEQ:TOK], in0=prev, scalar=tap(k),
                                                             in1=tile[:, SEQ:TOK], op0=ALU.mult, op1=ALU.add), f"s{k}")
                    await_step(dve, cv_dve, f"s{CONV_W - 2}", c)
                    cv_dve.done(dve.scalar_tensor_tensor(out=source, in0=source, scalar=tap(CONV_W - 1), in1=tile[:, :],
                                                         op0=ALU.mult, op1=ALU.add), "w3")

                def row_max(q):
                    await_step(dve, fp_pe, f"score{q}", h)
                    fp_dve.done(dve.tensor_reduce(STAT[:, q % 2, 0:1], bank(q % 2, (q + 1) * P), AX, ALU.max), f"max{q}")
                    await_step(dve, fp_dve, f"max{q}", h)
                    fp_dve.done(dve.tensor_scalar(STAT[:, q % 2, 1:2], STAT[:, q % 2, 0:1], -1.0, None, ALU.mult), f"neg{q}")

                def normalize(q):
                    await_step(dve, fp_act, f"exp{q}", h)
                    fp_dve.done(dve.reciprocal(STAT[:, q % 2, 3:4], STAT[:, q % 2, 2:3]), f"rinv{q}")
                    await_step(dve, fp_dve, f"rinv{q}", h)
                    p = PROB[:, q % 2, 0:(q + 1) * P]
                    fp_dve.done(dve.tensor_scalar(p, p, STAT[:, q % 2, 3:4], None, ALU.mult), f"norm{q}")

                await_step(dve, fp_pe, "vtok", h)
                hold(dve, fv_stored, 16 * h + 16, 16)
                fp_dve.done(dve.tensor_copy(TB[:, 0:SEQ], bank(6)), "vtok")
                row_max(0)
                row_max(1)
                convolve(0)
                normalize(0)
                row_max(2)
                keys(0)
                normalize(1)
                row_max(3)
                convolve(1)
                normalize(2)
                keys(1)
                normalize(3)
                convolve(2)
                await_step(dve, fp_act, "hi", h)
                fp_dve.done(dve.tensor_tensor(MOL[:, bass.ds(h, 1), 0:SEQ].rearrange("p a t -> p (a t)"), bank(4),
                                              MOH[:, bass.ds(h, 1), 0:SEQ].rearrange("p a t -> p (a t)").bitcast(F32),
                                              ALU.subtract), "lo")

            chain(dve.tensor_tensor(QKS[:, :, :], by_head(AB_Q), by_head(AB_K), ALU.mult), "qk")
            dve.wait_ge(sum_done, 4 * DEC + 1)
            chain(dve.scalar_tensor_tensor(out=SC[:, :, :, :].rearrange("p b g h -> p (b g h)"),
                                           in0=SC[:, :, :, :].rearrange("p b g h -> p (b g h)"), scalar=SCALE, in1=suf,
                                           op0=ALU.mult, op1=ALU.add), "scale")
            dve.wait_ge(fs_pe.sem, fs_pe.value("snew"))
            cn = bank(4, NDH).rearrange("p (h b) -> p b h", b=DEC)[:, :, None, :].broadcast_to([P, DEC, N_PAGES, FOX_HEADS])
            chain(dve.tensor_tensor(SC[:, :, :, :], cn, SC[:, :, :, :], ALU.add), "addcn")
            chain(dve.tensor_scalar(SN[:, :, :].rearrange("p b h -> p (b h)"), bank(4)[:, NDH:2 * NDH], SCALE, None, ALU.mult), "sn")
            chain(dve.tensor_reduce(MX[:, :, :], SC[:, :, :, :].rearrange("p b g h -> p b h g"), AX, ALU.max), "mx")
            dve.wait_ge(fs_pe.sem, fs_pe.value("turn"))
            chain(dve.tensor_reduce(MXC[:, :], bank(5)[0:NDH, 0:P], AX, ALU.max), "mxc")
            chain(dve.tensor_scalar(DG[:, :], IDENT[0:NDH, 0:NDH], MXC[:, 0:1], None, ALU.mult), "dg")
            dve.wait_ge(fs_pe.sem, fs_pe.value("max"))
            chain(dve.tensor_tensor(MX[:, :, :], bank(6, NDH).rearrange("p (b h) -> p b h", h=FOX_HEADS), SN[:, :, :], ALU.max), "m")
            chain(dve.tensor_tensor(SC[:, :, :, :], SC[:, :, :, :], over_pages(MX), ALU.subtract), "sub")
            chain(dve.tensor_tensor(SN[:, :, :], SN[:, :, :], MX[:, :, :], ALU.subtract), "subn")
            dve.wait_ge(fs_act.sem, fs_act.value("expn"))
            chain(dve.tensor_reduce(DEN[:, :, :], SC[:, :, :, :].rearrange("p b g h -> p b h g"), AX, ALU.add), "dn")
            dve.wait_ge(fs_pe.sem, fs_pe.value("den"))
            chain(dve.tensor_tensor(DEN[:, :, :], bank(7, NDH).rearrange("p (b h) -> p b h", h=FOX_HEADS), SN[:, :, :], ALU.add), "den")
            chain(dve.reciprocal(DEN[:, :, :], DEN[:, :, :]), "rinv")
            chain(dve.tensor_tensor(SC[:, :, :, :], SC[:, :, :, :], over_pages(DEN), ALU.mult), "norm")
            chain(dve.tensor_tensor(SN[:, :, :], SN[:, :, :], DEN[:, :, :], ALU.mult), "normn")
            chain(dve.tensor_tensor(OT[:, :, :].rearrange("p h b -> p b h"), by_head(AB_V), SN[:, :, :], ALU.mult), "vn")
            dve.wait_ge(cv_act, CONV_CH + GDN_HEADS)
            with dve.Fori(0, GDN_HEADS) as h:
                for m, (tile, chunk) in enumerate(((TA, GQ), (TB, GK))):
                    await_step(dve, ln_act, f"std{m}", h)
                    ln_dve.done(dve.reciprocal(tile[:, :], tile[:, :]), f"inv{m}")
                    await_step(dve, ln_dve, f"inv{m}", h)
                    x = PRJ[:, bass.ds(h + chunk, 1), :].rearrange("p a t -> p (a t)")
                    ln_dve.done(dve.tensor_tensor(x, x, tile[:, :], ALU.mult), f"mul{m}")
            dve.wait_ge(tails_stored, 32)
            dve.wait_ge(ln_dve.sem, ln_dve.value("mul1", GDN_HEADS - 1))
            dve.wait_ge(lev_in, 16)
            dve.memset(STATE[:, :, :], 0.0).then_inc(state_clear, 1)
            dve.wait_ge(state_clear, 1)
            with dve.Fori(0, NBLK) as c:
                def flat(tile):
                    return tile[:, :, :].rearrange("p h i -> p (h i)")

                def heads_of(b):
                    return bank(b).rearrange("p (h i) -> p h i", h=GDN_HEADS)

                def column(row, h):
                    return RT[:, bass.ds(c, 1), row + h:row + h + 1].rearrange("p a h -> p (a h)")

                def same(a):
                    return a[:, None, :].broadcast_to(GCH)

                await_step(dve, gl_pe, "gcb", c)
                gl_dve.done(dve.tensor_copy(XI[:, :, :], same(IDENT)), "xi")
                gl_dve.done(dve.tensor_copy(XIT[:, :, :], same(IDENT)), "xit")
                for h in range(GDN_HEADS):
                    ins = dve.tensor_scalar(GAM[:, h, :], bank(0)[:, h * P:(h + 1) * P], column(ROW_GC, h), 0.0, ALU.subtract, ALU.min)
                gl_dve.done(ins, "dt")
                gl_dve.done(dve.tensor_tensor(KDC[:, :], heads_of(0)[:, :, P - 1:P].rearrange("p h a -> p (h a)"),
                                              RT[:, bass.ds(c, 1), ROW_GC:ROW_GC + 4].rearrange("p a h -> p (a h)"), ALU.subtract), "gd")
                await_step(dve, gl_act, "gam", c)
                gl_dve.done(dve.tensor_tensor(GAM[:, :, :], GAM[:, :, :], same(INCL), ALU.mult), "gamm")
                await_step(dve, gl_pe, "bb", c)
                await_step(dve, gl_act, "kts", c)
                gl_dve.done(dve.tensor_tensor(KBT[:, :, :], heads_of(1), KTS[:, :, :], ALU.mult), "kbt")
                await_step(dve, gl_act, "eg", c)
                gl_dve.done(dve.tensor_tensor(QET[:, :, :], PRJ[:, GQ:GQ + GDN_HEADS, bass.ds(c * P, P)], EG[:, :, :], ALU.mult), "qet")
                await_step(dve, gl_pe, "a", c)
                await_step(dve, gl_dve, "gamm", c)
                gl_dve.done(dve.tensor_tensor(AT[:, :, :], heads_of(4), GAM[:, :, :], ALU.mult), "at")
                await_step(dve, gl_pe, "qk", c)
                gl_dve.done(dve.tensor_tensor(ATTN[:, :, :], heads_of(5), GAM[:, :, :], ALU.mult), "attn")
                await_step(dve, gl_act, "egc", c)
                gl_dve.done(dve.tensor_tensor(BEGE[:, :], RT[:, bass.ds(c, 1), ROW_BETA:ROW_BETA + 4].rearrange("p a h -> p (a h)"),
                                              EGC[:, :], ALU.mult), "bege")
                for h in range(GDN_HEADS):
                    ins = dve.tensor_scalar(VB[:, h, :], bank(3)[:, h * P:(h + 1) * P], column(ROW_BETA, h), None, ALU.mult)
                gl_dve.done(ins, "vb")
                await_step(dve, gl_dve, "bege", c)
                for h in range(GDN_HEADS):
                    ins = dve.tensor_scalar(KBE[:, h, :], bank(2)[:, h * P:(h + 1) * P], BEGE[:, h:h + 1], None, ALU.mult)
                gl_dve.done(ins, "kbe")
                for h in range(GDN_HEADS):
                    ins = dve.tensor_scalar(KDE[:, h, :], bank(2)[:, h * P:(h + 1) * P], KDC[:, h:h + 1], None, ALU.mult)
                gl_dve.done(ins, "kd")
                def blocks(n):
                    gl_dve.done(dve.tensor_tensor(ATS[:, :, :], AT[:, :, :], same(LEV[:, n, :]), ALU.mult), f"ats{n}")

                blocks(0)
                await_step(dve, gl_dve, "ats0", c)
                gl_dve.done(dve.tensor_tensor(flat(XIT), flat(XIT), flat(ATS), ALU.subtract), "xt0")
                await_step(dve, gl_pe, "t0", c)
                await_step(dve, gl_dve, "xt0", c)
                blocks(1)
                gl_dve.done(dve.tensor_tensor(flat(XI), flat(XI), bank(6), ALU.subtract), "x0")
                for n in range(1, LEVELS):
                    await_step(dve, gl_pe, f"t{n}", c)
                    if n < LEVELS - 1:
                        blocks(n + 1)
                        await_step(dve, gl_pe, f"x{n}", c)
                        gl_dve.done(dve.tensor_tensor(flat(XI), flat(XI), bank(5), ALU.subtract), f"x{n}")
                    await_step(dve, gl_pe, f"xt{n}", c)
                    gl_dve.done(dve.tensor_tensor(flat(XIT), flat(XIT), bank(0), ALU.subtract), f"xt{n}")
                await_step(dve, gl_pe, "ws", c)
                await_step(dve, gl_act, "u", c)
                gl_dve.done(dve.tensor_tensor(flat(VNEW), flat(VNEW), bank(3), ALU.subtract), "vn")
                await_step(dve, gl_pe, "s", c)
                for h in range(GDN_HEADS):
                    ins = dve.scalar_tensor_tensor(out=STATE[:, h, :], in0=STATE[:, h, :], scalar=EG[:, h, P - 1:P],
                                                   in1=bank(5)[:, h * P:(h + 1) * P], op0=ALU.mult, op1=ALU.add)
                gl_dve.done(ins, "s")

            dve.wait_ge(vo_copied, NBLK + 1)
            chain(dve.tensor_tensor(OS[:, :, :], OS[:, :, :], OT[:, :, :], ALU.add), "add")
            dve.wait_ge(fs_act.sem, fs_act.value("hi"))
            chain(dve.tensor_tensor(MOL[:, 0:FOX_HEADS, SEQ:TOK], OS[:, :, :],
                                    MOH[:, 0:FOX_HEADS, SEQ:TOK].bitcast(F32), ALU.subtract), "lo")
            dve.wait_ge(gl_act.sem, gl_act.value("o", NBLK - 1))
            dve.wait_ge(gl_dve.sem, gl_dve.value("s", NBLK - 1))

            def new_tokens(chunk):
                return PRJ[:, chunk:chunk + GDN_HEADS, SEQ:TOK]

            def grid(a):
                return a.rearrange("p (h b) -> p h b", h=GDN_HEADS)

            def chain_g(ins, name):
                gs_dve.done(ins, name)
                dve.wait_ge(gs_dve.sem, gs_dve.value(name))

            kq = KQ[:, :, :].rearrange("p (h b) n -> p h b n", h=GDN_HEADS)
            chain_g(dve.tensor_copy(kq[:, :, :, 0], new_tokens(GK)), "kq0")
            chain_g(dve.tensor_copy(kq[:, :, :, 1], new_tokens(GQ)), "kq1")
            chain_g(dve.tensor_copy(KC[:, :, :], new_tokens(GK)), "kc")
            chain_g(dve.tensor_tensor(QKP[:, :, :], new_tokens(GK), new_tokens(GQ), ALU.mult), "qkp")
            dve.wait_ge(gs_act.sem, gs_act.value("beq"))
            read = bank(0, 2 * NJ).rearrange("p (h b n) -> p h b n", h=GDN_HEADS, n=2)
            chain_g(dve.tensor_tensor(W1[:, :, :], read[:, :, :, 0], EGS[:, :, :], ALU.mult), "a1")
            chain_g(dve.tensor_tensor(W1[:, :, :], new_tokens(GV), W1[:, :, :], ALU.subtract), "a2")
            chain_g(dve.tensor_tensor(VN2[:, :, :], W1[:, :, :], grid(BEQ[:, 0, :]), ALU.mult), "a3")
            chain_g(dve.tensor_tensor(W1[:, :, :], read[:, :, :, 1], EGS[:, :, :], ALU.mult), "o1")
            chain_g(dve.tensor_tensor(W2[:, :, :], VN2[:, :, :], grid(BEQ[:, 2, :]), ALU.mult), "o2")
            chain_g(dve.tensor_tensor(new_tokens(GQ), W1[:, :, :], W2[:, :, :], ALU.add), "o3")
            dve.wait_ge(gs_act.sem, gs_act.value("vt"))
            for h in range(GDN_HEADS):
                if h >= 2:
                    dve.wait_ge(gs_pe.sem, gs_pe.value(f"up{h - 2}"))
                gs_dve.done(dve.tensor_tensor(VBD[:, h % 2, :, :], VTK[:, None, :].broadcast_to([NJ, DEC, P]),
                                              IDENT[0:NJ, h * DEC:(h + 1) * DEC][:, :, None].broadcast_to([NJ, DEC, P]), ALU.mult), f"bd{h}")
                dve.wait_ge(gs_pe.sem, gs_pe.value(f"up{h}"))
                for b in range(DEC):
                    ins = dve.scalar_tensor_tensor(out=SS[:, h * DEC + b, :], in0=SS[:, h * DEC + b, :], scalar=EGS[:, h, b:b + 1],
                                                   in1=ACC[2 + h % 2][:, b // 4, (b % 4) * P:(b % 4 + 1) * P], op0=ALU.mult, op1=ALU.add)
                gs_dve.done(ins, f"s{h}")

            with dve.Fori(0, GDN_HEADS) as h:
                def whole(chunk):
                    return PRJ[:, bass.ds(h + chunk, 1), :].rearrange("p a t -> p (a t)")

                await_step(dve, go_act, "std", h)
                go_dve.done(dve.reciprocal(TA[:, :], TA[:, :]), "inv")
                await_step(dve, go_dve, "inv", h)
                go_dve.done(dve.scalar_tensor_tensor(out=TB[:, :], in0=whole(GQ), scalar=PAR[:, PAR_GDN:PAR_GDN + 1], in1=TA[:, :],
                                                     op0=ALU.mult, op1=ALU.mult), "norm")
                await_step(dve, go_dve, "norm", h)
                go_dve.done(dve.tensor_tensor(TH[:, :], TB[:, :], whole(AB_Z), ALU.mult), "gate")
                await_step(dve, go_act, "hi", h)
                go_dve.done(dve.tensor_tensor(MOL[:, bass.ds(h + FOX_HEADS, 1), :].rearrange("p a t -> p (a t)"), TH[:, :],
                                              MOH[:, bass.ds(h + FOX_HEADS, 1), :].rearrange("p a t -> p (a t)").bitcast(F32), ALU.subtract), "lo")
            dve.wait_ge(gdn_stored, 1)
            update("ab_out", 1.0, 1)
            reciprocal(2)
            up(1)
            update("down1", 0.5)
            reciprocal(3)
            up(2)
            update("down2", 0.5)
            reciprocal(4)
            dve.wait_ge(ret_consts_in, 64)

            def ret_turn(h, p):
                first, is_first, is_last = ret_first(h), isinstance(h, int) and h == 0, isinstance(h, int) and h == RET_HEADS
                g, o = h - 1, 1 - p
                K_SCALE = float(P) ** -0.5

                def scaled(n, out):
                    hold(dve, used, RU + first + n + 3)
                    dve.tensor_tensor(halves(out), ACC[n % 2][:, :, 0:HALF], halves(RSTD[:, :]), ALU.mult).then_inc(tile_free, 1)

                def rotate(out, factor, name):
                    rp_dve.done(dve.scalar_tensor_tensor(out=out[:, :], in0=TA[:, :], scalar=factor, in1=ROPE[:, 0, :],
                                                         op0=ALU.mult, op1=ALU.mult), f"{name}c")
                    await_step(dve, rp_act, name, h)
                    rp_dve.done(dve.scalar_tensor_tensor(out=TB[:, :], in0=TB[:, :], scalar=factor, in1=ROPE[:, 1, :],
                                                         op0=ALU.mult, op1=ALU.mult), f"{name}s")
                    await_step(dve, rp_dve, f"{name}s", h)
                    rp_dve.done(dve.tensor_tensor(out[:, :], out[:, :], TB[:, :], ALU.add), name)

                def decay(kind):
                    return DECS[:, kind, bass.ds(g, 1)]

                def by_chunk(tile):
                    return tile[:, 0:SEQ].rearrange("p (n i) -> p n i", n=NBLK)

                def of_head(table):
                    return table[:, bass.ds(g, 1), :].broadcast_to([P, NBLK, P])

                def block_rows(n):
                    rm_dve.done(dve.tensor_tensor(KBLK, KVT[:, None, 0:P].broadcast_to([DEC, DEC // 2, P]),
                                                  IDENT[0:DEC, DEC // 2 * n:DEC // 2 * (n + 1)][:, :, None].broadcast_to([DEC, DEC // 2, P]),
                                                  ALU.mult), f"kb{n}")

                def state_update(n):
                    await_step(dve, rm_pe, f"r{n}", g)
                    s = SSR[:, 2 * n:2 * n + 2, :].rearrange("p b v -> p (b v)")
                    return rm_dve.done(dve.scalar_tensor_tensor(out=s, in0=s, scalar=decay(2), in1=bank(6 + n % 2), op0=ALU.mult, op1=ALU.add), f"u{n}")

                def gate_tile(v, n):
                    hold(dve, used, RU + first + n + 3)
                    rm_dve.done(dve.tensor_tensor(RGATE[:, bass.ds(2 * g + v, 1), :].rearrange("p a (n t) -> p (a n) t", n=2),
                                                  ACC[n % 2][:, :, 0:HALF], halves(RSTD[:, :]), ALU.mult), f"ga{v}")
                    await_step(dve, rm_dve, f"ga{v}", g)
                    dve.sem_inc(tile_free, 1)

                def gate(v):
                    low, gated = (t[:, bass.ds(2 * g + v, 1), :].rearrange("p a t -> p (a t)") for t in (RMOL, RGATE))
                    await_step(dve, rm_act, f"si{v}", g)
                    rm_dve.done(dve.tensor_tensor(VBH[o][:, v, :], gated, VBH[o][:, v, :], ALU.mult), f"g{v}")
                    await_step(dve, rm_act, f"hi{v}", g)
                    rm_dve.done(dve.tensor_tensor(low, VBH[o][:, v, :],
                                                  RMOH[:, bass.ds(2 * g + v, 1), :].rearrange("p a t -> p (a t)").bitcast(F32),
                                                  ALU.subtract), f"lo{v}")

                if not is_last:
                    scaled(0, TA[:, :])
                    hold(dve, tile_free, RTILE + first + 5)
                    rotate(QB[p], 1.0, "q")
                if not is_first:
                    await_step(dve, rm_pe, "a", g)
                    rm_dve.done(dve.tensor_scalar(KD_[:, :, :].rearrange("p n d -> p (n d)"), bank(4), decay(0), None, ALU.mult), "kd")
                    rm_dve.done(dve.tensor_tensor(by_chunk(ATT), bank(7).rearrange("p (n i) -> p n i", n=NBLK), of_head(DMAT), ALU.mult), "att")
                    rm_dve.done(dve.tensor_tensor(by_chunk(QB[o]), by_chunk(QB[o]), of_head(QDEC), ALU.mult), "qd")
                    rm_dve.done(dve.tensor_scalar(QSD[:, :], QB[o][:, SEQ:TOK], decay(2), None, ALU.mult), "qsd")
                    rm_dve.done(dve.tensor_tensor(QKR[:, :], QB[o][:, SEQ:TOK], KB[o][:, SEQ:TOK], ALU.mult), "qkp")
                    rm_dve.done(dve.tensor_copy(VSC[:, :, :], VBH[o][:, :, SEQ:TOK]), "vsc")
                if not is_last:
                    scaled(1, TA[:, :])
                    hold(dve, tile_free, RTILE + first + 6)
                    rotate(KB[p], K_SCALE, "k")
                if not is_first:
                    await_step(dve, rm_pe, "kv", g)
                    for n in range(NBLK):
                        kv = bank(6 + n // 2)[:, (n % 2) * RET_DV:(n % 2 + 1) * RET_DV]
                        if n == 0:
                            rm_dve.done(dve.tensor_copy(SALL[0][:, :], kv), "s0")
                            continue
                        await_step(dve, rm_dve, f"s{n - 1}", g)
                        if n == NBLK - 1:
                            hold(dve, rsp_stored, 16 * g + 16, 16)
                        rm_dve.done(dve.scalar_tensor_tensor(out=SALL[n][:, :], in0=SALL[n - 1][:, :], scalar=decay(1), in1=kv,
                                                             op0=ALU.mult, op1=ALU.add), f"s{n}")
                if not is_last:
                    scaled(2, VBH[p][:, 0, :])
                if not is_first:
                    await_step(dve, rm_pe, "cross", g)
                    read = bank(6)[:, 0:2 * DEC].rearrange("p (v b) -> p v b", v=2)
                    qk = bank(6)[:, 2 * DEC:3 * DEC][:, None, :].broadcast_to([P, 2, DEC])
                    rm_dve.done(dve.tensor_tensor(WSC[:, :, :], qk, VSC[:, :, :], ALU.mult), "ov")
                    await_step(dve, rm_dve, "ov", g)
                    rm_dve.done(dve.tensor_tensor(VBH[o][:, :, SEQ:TOK], read, WSC[:, :, :], ALU.add), "os")
                if not is_last:
                    scaled(3, VBH[p][:, 1, :])
                if not is_first:
                    await_step(dve, rm_pe, "mean", g)
                    for v in range(2):
                        out = halves(VBH[o][:, v, :])
                        rm_dve.done(dve.scalar_tensor_tensor(out=out, in0=ACC[2][:, :, 0:HALF], scalar=-1.0 / RET_DV, in1=out,
                                                             op0=ALU.mult, op1=ALU.add), f"c{v}")
                    await_step(dve, rm_act, "tk", g)
                    block_rows(0)
                    gate_tile(0, 0 if is_last else 4)
                    await_step(dve, rm_act, "std", g)
                    rm_dve.done(dve.reciprocal(TB[:, :], TB[:, :]), "inv")
                    await_step(dve, rm_dve, "inv", g)
                    for v in range(2):
                        rm_dve.done(dve.scalar_tensor_tensor(out=VBH[o][:, v, :], in0=VBH[o][:, v, :],
                                                             scalar=PAR[:, bass.ds(2 * g + PAR_RET + v, 1)], in1=TB[:, :],
                                                             op0=ALU.mult, op1=ALU.mult), f"n{v}")
                    state_update(0)
                    state_update(1)
                    block_rows(1)
                    await_step(dve, rm_dve, "n0", g)
                    gate(0)
                    gate_tile(1, 1 if is_last else 5)
                    state_update(2)
                    state_update(3)
                    await_step(dve, rm_dve, "u3", g)
                    dve.sem_inc(states_stepped, 1)
                    gate(1)

            ret_turns(dve, ret_turn)
            update("ret_out", 1.0)
            reciprocal(5)
            up(3)
            update("down3", 0.5)
            reciprocal(6)
            for d in range(KD):
                dve.scalar_tensor_tensor(out=YF[:, d, :], in0=X[:, d, :], scalar=PAR[:, PAR_FINAL + d:PAR_FINAL + d + 1],
                                         in1=RSTD[:, :], op0=ALU.mult, op1=ALU.mult).then_inc(y_ready, 1)


_INS = ["x_prompt", "x_sample", "cache_fox_k", "cache_fox_v", "cache_fox_logf", "page_table", "state_gdn_conv",
        "state_gdn_S", "state_ret_S", "norm_g", "final_norm_g", "ffn_w_gu", "ffn_w_down", "ab_w_in", "ab_w_out",
        "fox_b_f", "gdn_conv_w", "gdn_A_log", "gdn_dt_bias", "gdn_norm_g", "c_w_in", "c_w_out", "ret_norm_g"]
_OUTS = [(1, 512, 1024), (8, 1, 1024), (1, 1, 512, 4, 128), (1, 1, 512, 4, 128), (1, 1, 512, 4), (1, 8, 1, 4, 128),
         (1, 8, 1, 4, 128), (1, 8, 1, 4), (1, 1, 3, 1536), (1, 1, 4, 128, 128), (1, 8, 3, 1536), (1, 8, 4, 128, 128),
         (1, 1, 8, 128, 256), (1, 8, 8, 128, 256)]


def kernel(**inputs):
    import concourse.bacc as _bacc
    from concourse.bass_utils import run_bass_kernel_spmd as _run

    nc = _bacc.Bacc("TRN2", target_bir_lowering=False, num_devices=1)
    arrays, args = {}, []
    for name in _INS + ["shape_constants"]:
        a = shape_constants() if name == "shape_constants" else np.ascontiguousarray(inputs[name])
        arrays[f"in_{name}"] = a
        args.append(nc.dram_tensor(f"in_{name}", a.shape, mybir.dt.from_np(a.dtype), kind="ExternalInput").ap())
    for i, shape in enumerate(_OUTS):
        args.append(nc.dram_tensor(f"out_{i}", shape, F32, kind="ExternalOutput").ap())
    trunk_program(nc, *args)
    r = _run(nc, [arrays], core_ids=[0])
    return tuple(r.results[0][f"out_{i}"] for i in range(len(_OUTS)))
```

```python
from contextlib import ExitStack

import numpy as np

import concourse.bass as bass
from concourse import mybir

F32 = mybir.dt.float32
F32R = mybir.dt.float32r
I32 = mybir.dt.int32
ALU = mybir.AluOpType
ACT = mybir.ActivationFunctionType
AX = mybir.AxisListType.X

P = 128
D_MODEL, D_FF = 1024, 2816
SEQ, DEC = 512, 8
TOK = SEQ + DEC
HALF = TOK // 2
KD = D_MODEL // P
KF = D_FF // P
KH = KF // 2
NBLK = SEQ // P
FOX_HEADS = GDN_HEADS = 4
RET_HEADS, RET_DV = 8, 256
N_PAGES, N_POOL = 16, 160
CONV_W, CONV_CH = 4, 12
AB_CH = 28
EPS = 1e-6
LEVELS = 7
NEG = -1e30

CONST_PARTS = [("ident", P), ("maskneg", P), ("incl", P), ("later", P),
               ("levels", LEVELS * P), ("rope", 2 * TOK), ("dmat", RET_HEADS * P), ("qdec", RET_HEADS * P),
               ("kdec", RET_HEADS), ("chunkdec", RET_HEADS), ("stepdec", RET_HEADS)]
CONST_AT = {}
for _name, _n in CONST_PARTS:
    CONST_AT[_name] = (sum(n for _, n in CONST_PARTS[:len(CONST_AT)]), _n)
CONST_COLS = sum(n for _, n in CONST_PARTS)

PAR_NORM, PAR_FINAL, PAR_CONV, PAR_GDN, PAR_RET, PAR_ROWS = 0, 48, 56, 104, 105, 121
"""PAR_NORM + 8*n + d: norm n, chunk d; PAR_CONV + 12*tap + channel chunk; PAR_RET + 2*head + half."""

ROW_LOGF, ROW_GC, ROW_BETA, ROW_NEGC = 0, 32, 64, 96


def shape_constants():
    i = np.arange(P)
    f = np.float32
    c = np.zeros((P, CONST_COLS), f)

    def put(name, a):
        at, n = CONST_AT[name]
        c[:, at:at + n] = a.reshape(P, n)

    put("ident", np.eye(P, dtype=f))
    put("maskneg", np.where(i[None, :] > i[:, None], f(NEG), f(0)))
    put("incl", (i[None, :] >= i[:, None]).astype(f))
    put("later", (i[:, None] > i[None, :]).astype(f))
    lev = np.zeros((P, LEVELS, P), f)
    for n in range(LEVELS):
        s = 1 << n
        row, col = i[:, None], i[None, :]
        lev[:, n] = (row // (2 * s) == col // (2 * s)) & (row // s % 2 == 0) & (col // s % 2 == 1)
    put("levels", lev)
    half = P // 2
    freqs = f(10000.0) ** (-np.arange(half, dtype=f) / f(half))
    pos = np.concatenate([np.arange(SEQ, dtype=f), np.full(DEC, N_PAGES * P, f)])
    ang = (pos[:, None] * freqs[None, :].astype(f)).astype(f).T.astype(np.float64)
    cos, sin = np.cos(ang), np.sin(ang)
    cc, ss = np.concatenate([cos, cos]), np.concatenate([-sin, sin])
    put("rope", np.stack([cc, ss], 1).astype(f))
    lg = np.log(1.0 - 2.0 ** (-5.0 - np.arange(RET_HEADS)))
    diff = i[None, None, :] - i[:, None, None]
    put("dmat", np.where(diff >= 0, np.exp(np.maximum(diff, 0) * lg[None, :, None]), 0.0).astype(f))
    put("qdec", np.broadcast_to(np.exp(lg[None, :, None] * (i[None, None, :] + 1.0)), (P, RET_HEADS, P)).astype(f))
    put("kdec", np.exp(lg[None, :] * (P - 1.0 - i[:, None])).astype(f))
    put("chunkdec", np.broadcast_to(np.exp(lg * P), (P, RET_HEADS)).astype(f))
    put("stepdec", np.broadcast_to(np.exp(lg), (P, RET_HEADS)).astype(f))
    return c


class Steps:

    def __init__(self, sem, names):
        self.sem, self.names, self.next = sem, names, 0
        self.opened = 0


    def done(self, instruction, name):
        assert self.names[self.next % len(self.names)] == name, (name, self.names[self.next % len(self.names)])
        self.next += 1
        instruction.then_inc(self.sem, 1)

    def value(self, name, turn=0):
        return turn * len(self.names) + (self.names.index(name) + 1) + self.opened

    def turns(self, n):
        return len(self.names) * n + self.opened


def hold(engine, sem, value, least=1):
    if not isinstance(value, int):
        engine.wait_ge(sem, least)
    engine.wait_ge(sem, value)


def await_turns(engine, steps, n):
    hold(engine, steps.sem, steps.turns(n))


def await_step(engine, steps, name, turn=0):
    hold(engine, steps.sem, steps.value(name, turn))


def trunk_program(nc, x_prompt, x_sample, cache_k, cache_v, cache_logf, page_table, state_conv, state_gdn, state_ret,
                  norm_g, final_g, w_gu, w_down, ab_in, ab_out, fox_b, conv_w, a_log, dt_bias, gdn_g, c_in, c_out,
                  ret_g, consts, y_prompt, y_sample, fk_prompt, fv_prompt, fl_prompt, fk_sample, fv_sample,
                  fl_sample, conv_prompt, gs_prompt, conv_sample, gs_sample, rs_prompt, rs_sample):
    ctx = ExitStack()
    base = nc.sbuf_base + (-nc.sbuf_base) % 32
    room = nc.sbuf_usable_end - base
    cursor = {"main": 0}

    def at(name, shape, offset, dt=F32):
        size = 4 * int(np.prod(shape[1:]))
        assert offset % 32 == 0 and offset + size <= room, (name, offset, size, room)
        return nc.alloc_sbuf_tensor_at(name, shape, dt, offset=base + offset)

    def new(name, shape, dt=F32, area="main"):
        offset = cursor[area]
        cursor[area] = offset + -(-4 * int(np.prod(shape[1:])) // 32) * 32
        return at(name, shape, offset, dt)

    with ctx:
        def sem(name):
            return ctx.enter_context(nc.semaphore(name))

        X = new("X", [P, KD, TOK])
        IDENT = new("IDENT", [P, P])
        ONES = new("ONES", [P, P])
        MASKNEG = new("MASKNEG", [P, P])
        INCL = new("INCL", [P, P])
        LATER = new("LATER", [P, P])
        PAR = new("PAR", [P, P])
        RSTD = new("RSTD", [P, TOK])
        SSQ = new("SSQ", [P, TOK])
        SQ = new("SQ", [P, TOK])
        EPSC = new("EPSC", [P, 4])
        ZERO = new("ZERO", [P, 1, 1])
        ROWSEL = new("ROWSEL", [P, 104])
        COLS = new("COLS", [P, 4])
        TA = new("TA", [P, TOK])
        TB = new("TB", [P, TOK])
        TH = new("TH", [P, TOK])
        ring_at = cursor["main"]
        RAW = new("RAW", [P, 2, KH, P])
        WHI = new("WHI", [P, 2, KH, P], F32R)
        WLO = new("WLO", [P, 2, KH, P], F32R)
        cursor["xs"] = cursor["main"]
        XH = new("XH", [P, KD, TOK], F32R, "xs")
        XL = new("XL", [P, KD, TOK], F32R, "xs")
        cursor["abwork"] = cursor["main"]
        cursor["h"] = cursor["xs"]
        cursor["load"] = cursor["proj"] = cursor["ret"] = cursor["fin"] = cursor["h"]
        HH = new("HH", [P, KF, TOK], F32R, "h")
        HL = new("HL", [P, KF, TOK], F32R, "h")
        cursor["ab"] = cursor["retc"] = cursor["h"]
        XTOK = new("XTOK", [P, NBLK, D_MODEL], area="load")
        XTOKS = new("XTOKS", [DEC, D_MODEL], area="load")
        PROWS = new("PROWS", [P, P], area="load")
        YF = new("YF", [P, KD, TOK], area="fin")
        YTOK = new("YTOK", [P, NBLK, D_MODEL], area="fin")
        YTOKS = new("YTOKS", [DEC, D_MODEL], area="fin")

        ACC = [ctx.enter_context(nc.psum_tensor(f"ACC{i}", [P, 2, 512], F32)) for i in range(4)]

        def bank(b, n=512):
            return ACC[b // 2][:, b % 2, 0:n]

        def halves(a):
            return a.rearrange("p (n t) -> p n t", n=2)

        consts_in = sem("consts_in")
        inputs_in = sem("inputs_in")
        cols_clear = sem("cols_clear")
        ones_set = sem("ones_set")
        rowsel_set = sem("rowsel_set")
        raw_in = [sem("raw_in0"), sem("raw_in1")]
        zero_set = sem("zero_set")
        hi_split = sem("hi_split")
        split = sem("split")
        used = sem("used")
        tile_free = sem("tile_free")
        sq_ready = sem("sq_ready")
        ssq_ready = sem("ssq_ready")
        xh_ready = sem("xh_ready")
        xl_ready = sem("xl_ready")
        stat_done = sem("stat_done")
        std_ready = sem("std_ready")
        rstd_ready = sem("rstd_ready")
        act_ready = sem("act_ready")
        hfull_ready = sem("hfull_ready")
        hh_ready = sem("hh_ready")
        h_ready = sem("h_ready")
        stored = sem("stored")
        stores = [0]

        unit_at, tile_at = {}, {}
        u = 0
        t = KD
        for name, units, tiles in (("up0", 2 * KF, 2 * KF), ("down0", 2 * KD, KD), ("ab_in", AB_CH + 1, AB_CH + 1),
                                   ("ab_out", KD, KD), ("up1", 2 * KF, 2 * KF), ("down1", 2 * KD, KD),
                                   ("up2", 2 * KF, 2 * KF), ("down2", 2 * KD, KD), ("ret_in", 6 * RET_HEADS, 6 * RET_HEADS),
                                   ("ret_out", 2 * KD, KD), ("up3", 2 * KF, 2 * KF), ("down3", 2 * KD, KD)):
            unit_at[name], tile_at[name] = u, t
            u, t = u + units, t + tiles
        UPDATE = {"load": 0, "down0": 1, "ab_out": 2, "down1": 3, "down2": 4, "ret_out": 5, "down3": 6}
        NORM_OF = {"up0": 0, "ab_in": 1, "up1": 2, "up2": 3, "ret_in": 4, "up3": 5, "final": 6}
        SSQ_STEPS = KD + 1
        tile_at_update = [0] + [tile_at[n] for n in UPDATE if n != "load"]

        par_turned = sem("par_turned")
        par_ready = sem("par_ready")
        loaded_turned = sem("loaded_turned")
        x_part = sem("x_part")
        y_ready = sem("y_ready")
        final_turned = sem("final_turned")
        final_copied = Steps(sem("final_copied"), [f"tok{n}" for n in range(NBLK)] + ["sample"])
        AB_Q, AB_K, AB_V, AB_CONV, AB_Z = 0, 4, 8, 12, 24
        PRJ = new("PRJ", [P, AB_CH, TOK], area="proj")
        MOH = new("MOH", [P, KD, TOK], F32R, "proj")
        MOL = new("MOL", [P, KD, TOK], F32R, "proj")
        LEV = new("LEV", [P, LEVELS, P], area="ab")
        R = new("R", [P, TOK], area="ab")
        RT = new("RT", [P, NBLK, P], area="ab")
        RTS = new("RTS", [DEC, P], area="ab")
        SC = new("SC", [P, DEC, N_PAGES, FOX_HEADS], area="ab")
        LF = new("LF", [P, DEC, N_PAGES, FOX_HEADS], area="ab")
        SUF = new("SUF", [P, DEC, N_PAGES, FOX_HEADS], area="ab")
        NDH = DEC * FOX_HEADS
        SN, MX, DEN, QKS = (new(n, [P, DEC, FOX_HEADS], area="ab") for n in ("SN", "MX", "DEN", "QKS"))
        OS = new("OS", [P, FOX_HEADS, DEC], area="ab")
        OT = new("OT", [P, FOX_HEADS, DEC], area="ab")
        MXC = new("MXC", [NDH, 1], area="ab")
        DG = new("DG", [NDH, NDH], area="ab")
        PT_SB = new("PT_SB", [1, DEC * N_PAGES], I32, "ab")
        cursor["fp"] = cursor["fs"] = cursor["gd"] = cursor["abwork"]
        QS, KS, VS = (new(n, [P, SEQ], area="fp") for n in ("QS", "KS", "VS"))
        SELH = new("SELH", [P, P], area="fp")
        KT, VT = (t[:, 0:SEQ].rearrange("p (n d) -> p n d", n=NBLK) for t in (TA, TB))
        PROB = new("PROB", [P, NBLK, SEQ], area="fp")
        PTR = new("PTR", [P, 2, NBLK, P], area="fp")
        STAT = new("STAT", [P, NBLK, 4], area="fp")
        SCORE_BANK = (0, 1, 7, 5)
        KTOKS = new("KTOKS", [DEC, FOX_HEADS * P], area="fp")
        VTOKS, QTOK = RSTD[0:DEC, 0:FOX_HEADS * P], TH[0:DEC, 0:FOX_HEADS * P]
        QBR = new("QBR", [P, 2, FOX_HEADS * P], area="ab")
        SELB = SQ[0:DEC, 0:P]
        KBATCH = 4
        EARLY = 6
        mo_at = cursor["proj"] - 2 * 4 * KD * TOK
        PAGES_BYTES = 4 * 2 * KBATCH * FOX_HEADS * P
        KPAGES = [at(f"KPAGES{n}", [P, 2, KBATCH, FOX_HEADS * P], a) for n, a in enumerate((mo_at, ring_at))]
        PROD = [at(f"PROD{n}", [P, KBATCH, FOX_HEADS * P], a + PAGES_BYTES) for n, a in enumerate((mo_at, ring_at))]
        CONVROWS = at("CONVROWS", [DEC * (CONV_W - 1), CONV_CH * P], mo_at + PAGES_BYTES * 3 // 2)
        TAILS = new("TAILS", [DEC + CONV_W - 1, CONV_CH * P], area="fp")
        PREV = new("PREV", [P, CONV_CH, DEC, CONV_W - 1], area="fp")
        VPAGES = at("VPAGES", [P, N_PAGES, FOX_HEADS * P], ring_at)

        small_in = sem("small_in")
        cols_in = sem("cols_in")
        lev_in = sem("lev_in")
        pt_in = sem("pt_in")
        clear_r = sem("clear_r")
        gate_dve = Steps(sem("gate_dve"), ["z", "az", "t", "g", "logf", "c", "negc"] + [f"gc{n}" for n in range(NBLK)]
                         + ["gcs", "rt", "rts"])
        gate_act = Steps(sem("gate_act"), ["fac", "e", "l", "beta"])
        gate_pe = Steps(sem("gate_pe"), ["rt"])
        fp_pe = Steps(sem("fp_pe"), ["ktok", "vtok", "score0", "score1", "score2", "score3", "turn0", "pv0",
                                     "turn1", "pv1", "turn2", "pv2", "turn3", "pv3"])
        fp_act = Steps(sem("fp_act"), ["q", "k", "v", "sel", "ktok", "exp0", "exp1", "exp2", "exp3", "pt0", "pt1",
                                       "pt2", "pt3", "hi"])
        fp_dve = Steps(sem("fp_dve"), ["vtok"] + [f"{w}{q}" for q in range(NBLK) for w in ("max", "neg")]
                       + [f"{w}{q}" for q in range(NBLK) for w in ("rinv", "norm")] + ["lo"])
        fk_stored = sem("fk_stored")
        fv_stored = sem("fv_stored")
        kpage_in = [sem("kpage_in0"), sem("kpage_in1")]
        vpage_in = [sem(f"vpage_in{m}") for m in range(4)]
        lf_in = sem("lf_in")
        prod_done = sem("prod_done")
        sum_done = sem("sum_done")
        v_pool = Steps(sem("v_pool"), [f"{s}{w}" for s in range(2) for w in ("p2", "own", "add2", "p", "add", "fold")])
        v_pe = Steps(sem("v_pe"), [f"{s}{w}" for s in range(2) for w in ("raw", "folded")])
        values_seen = sem("values_seen")
        qtok_ready = sem("qtok_ready")
        qtok_turned = sem("qtok_turned")
        selb_ready = sem("selb_ready")
        qb_ready = sem("qb_ready")
        qbr_ready = sem("qbr_ready")
        vo_copied = sem("vo_copied")
        fs_pe = Steps(sem("fs_pe"), ["tok", "later", "total", "snew", "turn", "max", "den"])
        fs_act = Steps(sem("fs_act"), ["ktok", "vtok", "exp", "expn", "hi"])
        fs_dve = Steps(sem("fs_dve"), ["suf15"] + [f"suf{g}" for g in range(14, -1, -1)]
                       + ["addlater", "qk", "scale", "addcn", "sn", "mx", "mxc", "dg", "m", "sub", "subn", "dn", "den", "rinv",
                          "norm", "normn", "vn", "add", "lo"])
        GATE_UNIT, GATE_TILE = unit_at["ab_in"], tile_at["ab_in"]
        AB_UNIT, AB_TILE = GATE_UNIT + 1, GATE_TILE + 1
        AB_FREE = AB_TILE + AB_CH + 4
        SCALE = float(P) ** -0.5
        GQ, GK, GV = AB_CONV, AB_CONV + 4, AB_CONV + 8
        NJ = GDN_HEADS * DEC
        GCH = [P, GDN_HEADS, P]
        (KTS, VTS, GAM, EG, KBT, QET, AT, ATS, ATTN, XI, XIT, T1, VB, KBE, KDE, WT, VNEW, STATE) = (
            new(n, GCH, area="gd") for n in ("KTS", "VTS", "GAM", "EG", "KBT", "QET", "AT", "ATS", "ATTN", "XI", "XIT",
                                             "T1", "VB", "KBE", "KDE", "WT", "VNEW", "STATE"))
        SS = new("SS", [P, NJ, P], area="gd")
        assert cursor["gd"] <= cursor["abwork"] + 4 * (2 * KD + AB_CONV) * TOK
        cursor["gs"] = cursor["abwork"]
        KQ = new("KQ", [P, NJ, 2], area="gs")
        KC, QKP, EGS, VN2, W1, W2 = (new(n, [P, GDN_HEADS, DEC], area="gs") for n in ("KC", "QKP", "EGS", "VN2", "W1", "W2"))
        BEQ = new("BEQ", [P, 3, NJ], area="gs")
        KTK, VTK = (new(n, [NJ, P], area="gs") for n in ("KTK", "VTK"))
        VBD = new("VBD", [NJ, 2, DEC, P], area="gs")
        ROWSEL_ONE, NORM_ROWS = 35, 64
        SQH = at("SQH", [P, 2 * GDN_HEADS, TOK], cursor["abwork"])
        SQO, NRM = (at(n, [P, GDN_HEADS, TOK], cursor["abwork"] + a) for n, a in (("SQO", 12 * 1024), ("NRM", 12 * 1024 + 4 * GDN_HEADS * TOK)))
        assert cursor["gs"] <= cursor["abwork"] + 12 * 1024

        def row_select(r):
            return ROWSEL[:, ROWSEL_ONE - r:ROWSEL_ONE - r + NORM_ROWS]

        KDC, EGC, BEGE = (new(n, [P, GDN_HEADS], area="ab") for n in ("KDC", "EGC", "BEGE"))

        tails_stored = sem("tails_stored")
        gdn_stored = sem("gdn_stored")
        convrows_in = sem("convrows_in")
        ss_in = sem("ss_in")
        gp_pe = Steps(sem("gp_pe"), ["prev", "tails"])
        gp_act = Steps(sem("gp_act"), ["prev", "tail0", "tail1", "tail2"])
        cv_dve = Steps(sem("cv_dve"), ["z", "p3", "s0", "p2", "s1", "p1", "s2", "w3"])
        cv_act = sem("cv_act")
        ln_act = Steps(sem("ln_act"), ["sqq", "sqk", "stdq", "stdk"])
        ln_pe = Steps(sem("ln_pe"), ["sum"] + [f"b{j}" for j in range(2 * GDN_HEADS)])
        ln_dve = Steps(sem("ln_dve"), ["inv"] + [f"mul{j}" for j in range(2 * GDN_HEADS)])
        gl_pe = Steps(sem("gl_pe"), ["gcb", "bb", "ktok", "vtok", "a", "qk"]
                      + ["t0"] + [f"{w}{n}" for n in range(1, LEVELS) for w in (("t", "x", "xt") if n < LEVELS - 1 else ("t", "xt"))]
                      + ["u", "wt", "ws", "o", "s"])
        gl_act = Steps(sem("gl_act"), ["kts", "vts", "gam", "eg", "kdc", "egc"] + [f"t{n}" for n in range(1, LEVELS)]
                       + ["u", "wt", "o"])
        gl_dve = Steps(sem("gl_dve"), ["xi", "xit", "dt", "gd", "gamm", "kbt", "qet", "at", "attn", "bege", "ats0", "xt0", "ats1", "x0"]
                       + [w for n in range(1, LEVELS) for w in {1: ["vb"], 2: ["kbe"], 3: ["kd"]}.get(n, [])
                          + ([f"ats{n + 1}", f"x{n}", f"xt{n}"] if n < LEVELS - 1 else [f"xt{n}"])]
                       + ["vn", "s"])
        state_clear = sem("state_clear")
        gs_pe = Steps(sem("gs_pe"), ["r", "bc", "kt", "vt"] + [f"up{h}" for h in range(GDN_HEADS)])
        gs_act = Steps(sem("gs_act"), ["egs", "beq", "kt", "vt"])
        gs_dve = Steps(sem("gs_dve"), ["kq0", "kq1", "kc", "qkp", "a1", "a2", "a3", "o1", "o2", "o3"]
                       + ["bd0", "bd1", "s0", "bd2", "s1", "bd3", "s2", "s3"])
        go_act = Steps(sem("go_act"), ["sq", "std", "hi"])
        go_pe = Steps(sem("go_pe"), ["sum"] + [f"b{j}" for j in range(GDN_HEADS)])
        go_dve = Steps(sem("go_dve"), ["inv"] + [f"norm{j}" for j in range(GDN_HEADS)] + ["gate", "lo"])
        FOX_PROBS = fs_dve.value("vn")
        FOX_END = fs_dve.value("lo")
        RCH = 2 * RET_HEADS
        RMOH = new("RMOH", [P, RCH, TOK], F32R, "ret")
        RGATE = at("RGATE", [P, RCH, TOK], cursor["ret"])
        RMOL = new("RMOL", [P, RCH, TOK], F32R, "ret")
        QB = [new(f"QB{i}", [P, TOK], area="ret") for i in range(2)]
        KB = [new(f"KB{i}", [P, TOK], area="ret") for i in range(2)]
        VBH = [new(f"VBH{i}", [P, 2, TOK], area="ret") for i in range(2)]
        VTK_R = new("VTK_R", [P, NBLK, RET_DV], area="ret")
        cursor["retc"] = max(cursor["retc"], cursor["ret"])
        ROPE = new("ROPE", [P, 2, TOK], area="retc")
        DMAT = new("DMAT", [P, RET_HEADS, P], area="retc")
        QDEC = new("QDEC", [P, RET_HEADS, P], area="retc")
        DECS = new("DECS", [P, 3, RET_HEADS], area="retc")
        KD_ = SQ[:, 0:SEQ].rearrange("p (n d) -> p n d", n=NBLK)

        def ring_tail(name, n, shape):
            assert 4 * int(np.prod(shape[1:])) <= 4 * (KH - KD) * P
            return at(name, shape, ring_at + 4 * (n * KH + KD) * P)

        SALL = [ring_tail(f"SALL{n}", n + 2, [P, RET_DV]) for n in range(NBLK)]
        SSR = new("SSR", [P, DEC, RET_DV], area="retc")
        VSC = new("VSC", [P, 2, DEC], area="retc")
        WSC = new("WSC", [P, 2, DEC], area="retc")
        QSD, QKR = (new(n, [P, DEC], area="retc") for n in ("QSD", "QKR"))
        KVT = ring_tail("KVT", 0, [DEC, 3 * P])
        ATT = TH
        KBLK = TH[0:DEC, 0:DEC // 2 * P].rearrange("j (b d) -> j b d", b=DEC // 2)

        ret_consts_in = sem("ret_consts_in")
        rp_act = Steps(sem("rp_act"), ["q", "k"])
        rp_dve = Steps(sem("rp_dve"), ["qc", "qs", "q", "kc", "ks", "k"])
        rm_pe = Steps(sem("rm_pe"), ["ktok", "v0", "v1", "a", "kv", "o", "cross", "mean", "tok", "var", "r0", "r1", "r2", "r3"])
        rm_act = Steps(sem("rm_act"), ["vt0", "vt1", "o0", "o1", "tk", "sq0", "sq1", "std", "si0", "hi0", "si1", "hi1"])
        rm_dve = Steps(sem("rm_dve"), ["kd", "att", "qd", "qsd", "qkp", "vsc", "s0", "s1", "s2", "s3", "ov", "os", "c0", "c1",
                                       "kb0", "ga0", "inv", "n0", "n1", "u0", "u1", "kb1", "g0", "lo0", "ga1", "u2", "u3", "g1", "lo1"])
        states_stepped = sem("states_stepped")
        rss_in = sem("rss_in")
        rss_stored = sem("rss_stored")
        rsp_stored = sem("rsp_stored")
        RU, RTILE = unit_at["ret_in"], tile_at["ret_in"]

        def ret_first(turn):
            return 0 if isinstance(turn, int) and turn == 0 else 6 * turn - 2

        def ret_turns(engine, turn):
            turn(0, 0)
            with engine.Fori(0, RET_HEADS // 2 - 1) as i:
                turn(2 * i + 1, 1)
                turn(2 * i + 2, 0)
            turn(RET_HEADS - 1, 1)
            turn(RET_HEADS, 0)

        OPENED = {"act": (gl_act,), "dve": (gl_dve,)}
        for group in OPENED.values():
            for steps in group:
                steps.opened = 1
        v_pool.opened, v_pe.opened = len(v_pool.names), len(v_pe.names)

        def load_keys(engine, store, slot, first, n):
            hold(engine, prod_done, n + 1)
            for g in range(KBATCH):
                page = engine.value_load(PT_SB[0:1, bass.ds(first + g, 1)], min_val=0, max_val=N_POOL - 1)
                engine.dma_start(KPAGES[store][:, slot, g, :], cache_k[0, bass.ds(page, 1)].rearrange("a t h d -> (a t) (h d)"))\
                      .then_inc(kpage_in[slot], 16)

        block = ctx.enter_context(nc.Block())

        @block.sync
        def _(sp):
            def store(to, of):
                stores[0] += 1
                sp.dma_start(to, of).then_inc(stored, 16)

            for s in (fk_stored, fv_stored, rss_stored, rsp_stored):
                sp.sem_inc(s, 16)

            def load_unit(unit, slot, nk, source):
                hold(sp, split, unit + 1)
                sp.dma_start(RAW[:, slot, 0:nk, :], source).then_inc(raw_in[slot], 16)

            def load_up(f):
                w = w_gu[f // 2, f % 2].rearrange("(k p) c -> p k c", p=P)
                u0 = unit_at[f"up{f}"]
                with sp.Fori(0, KF // 2) as i:
                    for s in range(4):
                        col = (s % 2) * D_FF + P * (s // 2) + 2 * P * i
                        load_unit(u0 + 4 * i + s, (u0 + s) % 2, KD, w[:, :, bass.ds(col, P)])

            def load_down(f):
                w = w_down[f // 2, f % 2].rearrange("(s k p) c -> p s k c", p=P, k=KH)
                u0 = unit_at[f"down{f}"]
                with sp.Fori(0, KD // 2) as i:
                    for s in range(4):
                        load_unit(u0 + 4 * i + s, (u0 + s) % 2, KH,
                                  w[:, s % 2, :, bass.ds(2 * P * i + P * (s // 2), P)])

            sp.dma_start(PROWS[PAR_NORM:PAR_FINAL, :], norm_g.rearrange("l s (c p) -> (l s c) p", p=P)).then_inc(inputs_in, 16)
            sp.dma_start(PROWS[PAR_FINAL:PAR_CONV, :], final_g.rearrange("(c p) -> c p", p=P)).then_inc(inputs_in, 16)
            sp.dma_start(PROWS[PAR_CONV:PAR_GDN, :], conv_w[0].rearrange("w (c p) -> (w c) p", p=P)).then_inc(inputs_in, 16)
            sp.dma_start(PROWS[PAR_GDN:PAR_RET, :], gdn_g).then_inc(inputs_in, 16)
            sp.dma_start(PROWS[PAR_RET:PAR_ROWS, :], ret_g[0].rearrange("(c p) -> c p", p=P)).then_inc(inputs_in, 16)
            sp.dma_start(XTOKS[:, :], x_sample.rearrange("b o d -> (b o) d")).then_inc(inputs_in, 16)
            sp.dma_start(XTOK[:, :, :], x_prompt[0].rearrange("(n p) d -> p n d", p=P)).then_inc(inputs_in, 16)
            for tile, name in ((IDENT, "ident"), (MASKNEG, "maskneg"), (INCL, "incl"), (LATER, "later")):
                c0, n = CONST_AT[name]
                sp.dma_start(tile[:, :], consts[:, c0:c0 + n]).then_inc(consts_in, 16)
            for tile, src in ((COLS[ROW_LOGF:ROW_LOGF + 4, 0:1], fox_b), (COLS[ROW_GC:ROW_GC + 4, 0:1], dt_bias),
                              (COLS[ROW_GC:ROW_GC + 4, 1:2], a_log)):
                sp.wait_ge(cols_clear, 5)
                sp.dma_start(tile, src.rearrange("a h -> h a")).then_inc(cols_in, 16)
            c0, n = CONST_AT["levels"]
            sp.dma_start(LEV[:, :, :], consts[:, c0:c0 + n].rearrange("p (l c) -> p l c", l=LEVELS)).then_inc(lev_in, 16)
            sp.dma_start(PT_SB[:, :], page_table.rearrange("b (o g) -> o (b g)", o=1)).then_inc(pt_in, 16)
            load_up(0)
            load_down(0)
            abw = ab_in[0].rearrange("(k p) c -> p k c", p=P)
            slot = GATE_UNIT % 2
            hold(sp, split, GATE_UNIT + 1)
            for at_col, c0, dst_sem in ((ROW_LOGF, 3 * 512, raw_in[slot]), (ROW_GC, 3588, small_in), (ROW_BETA, 3592, small_in)):
                sp.dma_start(RAW[:, slot, 0:KD, at_col:at_col + 4], abw[:, :, c0:c0 + 4]).then_inc(dst_sem, 16)
            for f0 in range(4):
                load_unit(AB_UNIT + f0, (AB_UNIT + f0) % 2, KD, abw[:, :, P * f0:P * (f0 + 1)])
            for f0, turns, shift in ((AB_K, 1, 0), (AB_CONV, 2, FOX_HEADS)):
                with sp.Fori(0, turns) as i:
                    for m in range(8):
                        load_unit(AB_UNIT + f0 + 8 * i + m, (AB_UNIT + m) % 2, KD,
                                  abw[:, :, bass.ds(P * (f0 + m) + shift + 8 * P * i, P)])
                        if f0 == AB_K and m == 0:
                            sp.wait_ge(used, AB_UNIT + 2)
                            sp.dma_start(CONVROWS[:, :], state_conv[0].rearrange("b w c -> (b w) c")).then_inc(convrows_in, 16)
            sp.wait_ge(gate_dve.sem, gate_dve.value("rt"))
            store(fl_prompt[0, 0].rearrange("(n p) h -> p n h", p=P), RT[:, :, ROW_LOGF:ROW_LOGF + 4])
            sp.wait_ge(gate_dve.sem, gate_dve.value("rts"))
            store(fl_sample.rearrange("a b o h -> (a b o) h"), RTS[:, ROW_LOGF:ROW_LOGF + 4])
            sp.wait_ge(fs_act.sem, fs_act.value("vtok"))
            sp.dma_start(fk_sample[0].rearrange("b o h d -> (b o) (h d)"), KTOKS[:, :]).then_inc(tails_stored, 16)
            sp.dma_start(fv_sample[0].rearrange("b o h d -> (b o) (h d)"), VTOKS).then_inc(tails_stored, 16)
            store(conv_sample[0][:, 0:CONV_W - 2, :], state_conv[0][:, 1:CONV_W - 1, :])
            sp.wait_ge(gp_act.sem, gp_act.value("tail2"))
            sp.dma_start(conv_prompt[0, 0], TAILS[0:CONV_W - 1, :]).then_inc(tails_stored, 16)
            sp.dma_start(conv_sample[0][:, CONV_W - 2, :], TAILS[CONV_W - 1:, :]).then_inc(tails_stored, 16)
            sp.wait_ge(used, AB_UNIT + AB_CH + 2)
            with sp.Fori(0, FOX_HEADS) as h:
                for m in range(2):
                    load_keys(sp, 1, m, N_PAGES * (EARLY + m) + KBATCH * h, 4 * EARLY + 2 * h + m)
                await_step(sp, fp_act, "ktok", h)
                sp.dma_start(fk_prompt[0, 0].rearrange("(n p) h d -> p n h d", p=P)[:, :, bass.ds(h, 1), :]
                             .rearrange("p n a d -> p n (a d)"), KT).then_inc(fk_stored, 16)
                await_step(sp, fp_dve, "vtok", h)
                sp.dma_start(fv_prompt[0, 0].rearrange("(n p) h d -> p n h d", p=P)[:, :, bass.ds(h, 1), :]
                             .rearrange("p n a d -> p n (a d)"), VT).then_inc(fv_stored, 16)
            sp.wait_ge(fk_stored, 16 * FOX_HEADS + 16)
            sp.wait_ge(fv_stored, 16 * FOX_HEADS + 16)
            sp.wait_ge(tails_stored, 64)
            sp.wait_ge(sum_done, DEC * N_PAGES // KBATCH + 1)
            sp.wait_ge(fs_dve.sem, FOX_PROBS)
            for h in range(GDN_HEADS):
                sp.dma_start(SS[:, h * DEC:(h + 1) * DEC, :], state_gdn[0][:, h].rearrange("b k v -> k b v")).then_inc(ss_in, 16)
            with sp.Fori(0, NBLK) as c:
                for s in range(2):
                    last, turn = 1 - s, c if s == 1 else c - 1
                    for m, steps, name in ((2, v_pool, "add2"), (3, v_pe, "raw"), (s, v_pool, "add"), (last, v_pe, "folded")):
                        await_step(sp, steps, f"{last}{name}", turn)
                        for g in range(4 * m, 4 * m + 4):
                            page = sp.value_load(PT_SB[0:1, bass.ds(2 * N_PAGES * c + (N_PAGES * s + g), 1)], min_val=0, max_val=N_POOL - 1)
                            sp.dma_start(VPAGES[:, g, :], cache_v[0, bass.ds(page, 1)].rearrange("a t h d -> (a t) (h d)"))\
                              .then_inc(vpage_in[m], 16)
            abo = ab_out[0].rearrange("(k p) c -> p k c", p=P)

            def load_out(i):
                for s in range(2):
                    load_unit(unit_at["ab_out"] + 2 * i + s, (unit_at["ab_out"] + s) % 2, KD,
                              abo[:, :, bass.ds(2 * P * i + P * s, P)])

            sp.wait_ge(v_pe.sem, v_pe.value("1folded", NBLK - 1))
            load_out(0)
            sp.wait_ge(gl_dve.sem, gl_dve.value("s", NBLK - 1))
            store(gs_prompt[0, 0].rearrange("h k v -> k h v"), STATE[:, :, :])
            for h in range(GDN_HEADS):
                sp.wait_ge(gs_dve.sem, gs_dve.value(f"s{h}"))
                store(gs_sample[0][:, h].rearrange("b k v -> k b v"), SS[:, h * DEC:(h + 1) * DEC, :])
            sp.wait_ge(stored, 16 * stores[0])
            sp.sem_inc(gdn_stored, 1)
            with sp.Fori(1, KD // 2) as i:
                load_out(i)
            load_up(1)
            load_down(1)
            for tile, name in ((ROPE, "rope"), (DMAT, "dmat"), (QDEC, "qdec")):
                c0, n = CONST_AT[name]
                n = int(np.prod(tile.shape[1:]))
                sp.dma_start(tile[:, :, :], consts[:, c0:c0 + n].rearrange("p (a c) -> p a c", a=tile.shape[1])).then_inc(ret_consts_in, 16)
            c0, _ = CONST_AT["kdec"]
            sp.dma_start(DECS[:, :, :], consts[:, c0:c0 + 3 * RET_HEADS].rearrange("p (a c) -> p a c", a=3)).then_inc(ret_consts_in, 16)
            load_up(2)
            load_down(2)
            cw = c_in[0].rearrange("(k p) c -> p k c", p=P)
            V0, G0 = 2 * RET_HEADS * P, 2 * RET_HEADS * P + RET_HEADS * RET_DV

            def load_turn(h, parity):
                first = ret_first(h)
                n = 0
                if parity is not None and not (isinstance(h, int) and h == RET_HEADS):
                    for col in (h * P, h * P + RET_HEADS * P, h * RET_DV + V0, h * RET_DV + V0 + P):
                        load_unit(RU + first + n, (RU + n) % 2, KD, cw[:, :, bass.ds(col, P)])
                        n += 1
                if not (isinstance(h, int) and h == 0):
                    for col in ((h - 1) * RET_DV + G0, (h - 1) * RET_DV + G0 + P):
                        load_unit(RU + first + n, (RU + n) % 2, KD, cw[:, :, bass.ds(col, P)])
                        n += 1

            ret_turns(sp, load_turn)
            co = c_out[0].rearrange("(s k p) c -> p s k c", p=P, k=KD)
            with sp.Fori(0, KD // 2) as i:
                for s in range(4):
                    load_unit(unit_at["ret_out"] + 4 * i + s, (unit_at["ret_out"] + s) % 2, KD,
                              co[:, s % 2, :, bass.ds(2 * P * i + P * (s // 2), P)])
            load_up(3)
            sp.wait_ge(rsp_stored, 16 * RET_HEADS + 16)
            sp.wait_ge(rss_stored, 16 * RET_HEADS + 16)
            load_down(3)
            sp.wait_ge(final_copied.sem, final_copied.value("tok3"))
            store(y_prompt[0].rearrange("(n p) d -> p n d", p=P), YTOK[:, :, :])
            sp.wait_ge(final_copied.sem, final_copied.value("sample"))
            store(y_sample.rearrange("b o d -> (b o) d"), YTOKS[:, :])
            sp.wait_ge(stored, 16 * stores[0])

        @block.gpsimd
        def _(pool):
            def split_unit(unit, slot, nk, raw_count):
                hold(pool, raw_in[slot], 16 * raw_count, 16)
                hold(pool, used, unit + 1)
                pool.tensor_tensor(WHI[:, slot, 0:nk, :], RAW[:, slot, 0:nk, :], ZERO[:, :].broadcast_to([P, nk, P]),
                                   ALU.add).then_inc(hi_split, 1)
                hold(pool, hi_split, unit + 1)
                pool.tensor_tensor(WLO[:, slot, 0:nk, :], RAW[:, slot, 0:nk, :], WHI[:, slot, 0:nk, :].bitcast(F32),
                                   ALU.subtract).then_inc(split, 1)

            def split_phase(name, nk, turns, body, skip=0):
                u0 = unit_at[name] + skip
                with pool.Fori(0, turns) as i:
                    for s in range(body):
                        split_unit(u0 + body * i + s, (u0 + s) % 2, nk, (body // 2) * i + (u0 + s) // 2 + 1)

            pool.sem_inc(split, 2)
            pool.memset(ZERO[:, :], 0.0).then_inc(zero_set, 1)
            pool.wait_ge(zero_set, 1)
            split_phase("up0", KD, KF // 2, 4)
            split_phase("down0", KH, KD // 2, 4)
            pool.wait_ge(small_in, 32)
            split_unit(GATE_UNIT, GATE_UNIT % 2, KD, GATE_UNIT // 2 + 1)
            split_phase("ab_in", KD, AB_CH // 4, 4, skip=1)
            pool.sem_inc(v_pool.sem, v_pool.opened)
            pool.wait_ge(fs_dve.sem, fs_dve.value("norm"))
            with pool.Fori(0, NBLK) as c:
                for s in range(2):
                    def weigh(m, name):
                        hold(pool, vpage_in[m], 64 * (2 * c + s + 1), 64)
                        pool.sem_inc(values_seen, 1)
                        pages = VPAGES[:, 4 * m:4 * m + 4, :].rearrange("p g (h d) -> p (g h) d", d=P)
                        probs = SC[:, bass.ds(2 * c + s, 1), 4 * m:4 * m + 4, :].rearrange("p a g h -> p (a g h)")
                        v_pool.done(pool.tensor_tensor(pages, pages, probs[:, :, None].broadcast_to([P, 4 * FOX_HEADS, P]), ALU.mult), f"{s}{name}")

                    def add(to, of, count, after, name):
                        await_step(pool, v_pool, f"{s}{after}", c)
                        to, of = (VPAGES[:, n:n + count, :].rearrange("p g c -> p (g c)") for n in (to, of))
                        v_pool.done(pool.tensor_tensor(to, to, of, ALU.add), f"{s}{name}")

                    weigh(2, "p2")
                    weigh(s, "own")
                    add(4 * s, 8, 4, "own", "add2")
                    weigh(1 - s, "p")
                    add(4 * s, 4 * (1 - s), 4, "p", "add")
                    add(4 * s, 4 * s + 2, 2, "add", "fold")
            split_phase("ab_out", KD, KD // 2, 2)
            split_phase("up1", KD, KF // 2, 4)
            split_phase("down1", KH, KD // 2, 4)
            split_phase("up2", KD, KF // 2, 4)
            split_phase("down2", KH, KD // 2, 4)

            def split_turn(h, parity):
                first = ret_first(h)
                units = 4 if isinstance(h, int) and h == 0 else 2 if isinstance(h, int) and h == RET_HEADS else 6
                for n in range(units):
                    half_count = (RU + first + n) // 2 if isinstance(h, int) else 3 * h - 1 + (RU + n) // 2
                    split_unit(RU + first + n, (RU + n) % 2, KD, half_count + 1)

            ret_turns(pool, split_turn)
            split_phase("ret_out", KD, KD // 2, 4)
            split_phase("up3", KD, KF // 2, 4)
            split_phase("down3", KH, KD // 2, 4)

        @block.tensor
        def _(pe):
            def project(unit, slot, nk, acc, hi, lo, k0=0, last=True, ready=None, late=None):
                hold(pe, split, unit + 3)
                for k in range(nk):
                    if ready is not None:
                        pe.wait_ge(ready[0], ready[1] + k0 + k)
                    if late is not None and k0 + k == late[0]:
                        pe.wait_ge(late[1], late[2])
                    first = k == 0 and k0 == 0
                    final = last and k == nk - 1
                    for w, a, opens, closes in ((WHI, hi, True, False), (WHI, lo, False, False), (WLO, hi, False, True)):
                        for n in range(2):
                            ins = pe.matmul(ACC[acc][:, n, 0:HALF], w[:, slot, k, :],
                                            a[:, k0 + k, n * HALF:(n + 1) * HALF],
                                            start=first and opens, stop=final and closes)
                ins.then_inc(used, 1)

            def statistics(r):
                pe.wait_ge(ssq_ready, SSQ_STEPS * (r + 1))
                for n in range(2):
                    ins = pe.matmul(ACC[3][:, n, 0:HALF], ONES[:, :], SSQ[:, n * HALF:(n + 1) * HALF], start=True, stop=True)
                ins.then_inc(stat_done, 1)

            def up(f):
                u0, t0, r = unit_at[f"up{f}"], tile_at[f"up{f}"], NORM_OF[f"up{f}"]

                def two_pairs(i, first=False):
                    for s in range(4):
                        hold(pe, tile_free, t0 + s + 3 if first and s < 2 else t0 + 4 * i + s + 1)
                        if first and s == 3:
                            pe.wait_ge(std_ready, r + 1)
                        project(u0 + 4 * i + s, (u0 + s) % 2, KD, s, XH, XL, ready=(xl_ready, KD * r + 1))
                        if first and s == 0:
                            statistics(r)

                two_pairs(0, first=True)
                with pe.Fori(1, KF // 2) as i:
                    two_pairs(i)

            def down(name, hi, lo, nk, per_chunk, ready, late=None):
                u0, t0 = unit_at[name], tile_at[name]
                with pe.Fori(0, KD // 2) as i:
                    for s in range(2):
                        hold(pe, tile_free, t0 + 2 * i + s + 3)
                        for m in range(per_chunk):
                            n = per_chunk * s + m
                            project(u0 + 2 * per_chunk * i + n, (u0 + n) % 2, nk, s, hi, lo, k0=nk * m,
                                    last=m == per_chunk - 1, ready=ready, late=late)

            pe.sem_inc(used, 2)
            pe.sem_inc(v_pe.sem, v_pe.opened)
            pe.wait_ge(consts_in, 64)
            pe.wait_ge(inputs_in, 7 * 16)
            pe.transpose(bank(7, PAR_ROWS), PROWS[0:PAR_ROWS, :], IDENT[0:PAR_ROWS, 0:PAR_ROWS]).then_inc(par_turned, 1)
            for d in range(KD):
                if d >= 4:
                    pe.wait_ge(tile_free, d + 1)
                elif d == 3:
                    pe.wait_ge(par_ready, 1)
                for n in range(NBLK):
                    pe.transpose(ACC[d % 4][:, 0, n * P:(n + 1) * P], XTOK[:, n, d * P:(d + 1) * P], IDENT[:, :])
                pe.transpose(ACC[d % 4][:, 1, 0:DEC], XTOKS[:, d * P:(d + 1) * P], IDENT[0:DEC, 0:DEC]).then_inc(loaded_turned, 1)
            pe.wait_ge(tile_free, KD + 4)
            up(0)
            down("down0", HH, HL, KH, 2, (h_ready, 1))
            def project_ab(f, s):
                hold(pe, tile_free, AB_TILE + f + 3)
                project(AB_UNIT + f, (AB_UNIT + s) % 2, KD, (s + 1) % 2, XH, XL)

            def broadcast_q(b):
                hold(pe, selb_ready, b + 1)
                pe.matmul(bank(4), SELB, QTOK, start=True, stop=True).then_inc(qb_ready, 1)

            hold(pe, tile_free, GATE_TILE + 3)
            project(GATE_UNIT, GATE_UNIT % 2, KD, 0, XH, XL, ready=(xl_ready, KD + 1))
            statistics(1)
            for f in range(4):
                project_ab(f, f)
            pe.wait_ge(tile_free, AB_TILE + 8)
            for h in range(FOX_HEADS):
                ins = pe.transpose(bank(5)[0:DEC, h * P:(h + 1) * P], PRJ[:, AB_Q + h, SEQ:TOK], IDENT[:, :])
            ins.then_inc(qtok_turned, 1)
            pe.wait_ge(qtok_ready, 1)
            broadcast_q(0)
            with pe.Fori(0, (AB_CH - 4) // 8) as i:
                for m in range(8):
                    project_ab(8 * i + (m + 4), m)
                    if m in (0, 4):
                        broadcast_q(2 * i + (m // 4 + 1))
            broadcast_q(EARLY + 1)

            pe.wait_ge(tile_free, AB_FREE)
            pe.wait_ge(gate_dve.sem, gate_dve.value("gcs"))
            pe.wait_ge(gate_act.sem, gate_act.value("beta"))
            for n in range(NBLK):
                pe.transpose(bank(2)[:, n * P:(n + 1) * P], R[:, n * P:(n + 1) * P], IDENT[:, :])
            gate_pe.done(pe.transpose(bank(3)[0:DEC, 0:P], R[:, SEQ:TOK], IDENT[:, :]), "rt")

            pe.wait_ge(gate_dve.sem, gate_dve.value("rts"))
            for j, ch in enumerate((AB_K, AB_V)):
                for h in range(FOX_HEADS):
                    ins = pe.transpose(bank(j)[0:DEC, h * P:(h + 1) * P], PRJ[:, ch + h, SEQ:TOK], IDENT[:, :])
            fs_pe.done(ins, "tok")
            pe.wait_ge(lf_in, 16 * DEC * N_PAGES)
            lf = LF[:, :, :, :].rearrange("p b g h -> p (b g h)")
            fs_pe.done(pe.matmul(bank(3), LATER[:, :], lf, start=True, stop=True), "later")
            pe.wait_ge(qbr_ready, DEC)
            fs_pe.done(pe.matmul(bank(4), ONES[:, :], lf, start=True, stop=True), "total")
            pe.wait_ge(convrows_in, 16)
            for c in range(CONV_CH):
                rows = DEC * (CONV_W - 1)
                ins = pe.transpose(bank(5)[:, c * rows:(c + 1) * rows], CONVROWS[:, c * P:(c + 1) * P], IDENT[0:rows, 0:rows])
            gp_pe.done(ins, "prev")
            for c in range(CONV_CH):
                ins = pe.transpose(bank((6, 7, 2)[c // 4])[0:DEC + CONV_W - 1, (c % 4) * P:(c % 4 + 1) * P],
                                   PRJ[:, AB_CONV + c, SEQ - CONV_W + 1:TOK], IDENT[:, :])
            gp_pe.done(ins, "tails")
            pe.wait_ge(gp_act.sem, gp_act.value("tail2"))
            pe.wait_ge(fs_dve.sem, fs_dve.value("addlater"))
            with pe.Fori(0, FOX_HEADS) as h:
                def score(q):
                    if q == NBLK - 1:
                        await_step(pe, fp_act, "ktok", h)
                    w = (q + 1) * P
                    pe.matmul(bank(SCORE_BANK[q], w), QS[:, q * P:w], PRJ[:, bass.ds(h + AB_K, 1), 0:w].rearrange("p a t -> p (a t)"),
                              start=True, stop=False)
                    pe.matmul(bank(SCORE_BANK[q], w), SELH[:, :], R[:, 0:w], start=False, stop=False)
                    fp_pe.done(pe.matmul(bank(SCORE_BANK[q])[:, q * P:w], IDENT[:, :], MASKNEG[:, :], start=False, stop=True), f"score{q}")

                def turn(q):
                    await_step(pe, fp_dve, f"norm{q}", h)
                    for k in range(q + 1):
                        ins = pe.transpose(bank(2 + q % 2)[:, k * P:(k + 1) * P], PROB[:, q, k * P:(k + 1) * P], IDENT[:, :])
                    fp_pe.done(ins, f"turn{q}")

                def values(q):
                    await_step(pe, fp_act, f"pt{q}", h)
                    for k in range(q + 1):
                        ins = pe.matmul(bank(4)[:, q * P:(q + 1) * P], VT[:, k, :], PTR[:, q % 2, k, :], start=k == 0, stop=k == q)
                    fp_pe.done(ins, f"pv{q}")

                await_step(pe, fp_act, "sel", h)
                for n in range(NBLK):
                    ins = pe.transpose(bank(5)[:, n * P:(n + 1) * P], KS[:, n * P:(n + 1) * P], IDENT[:, :])
                fp_pe.done(ins, "ktok")
                for n in range(NBLK):
                    ins = pe.transpose(bank(6)[:, n * P:(n + 1) * P], VS[:, n * P:(n + 1) * P], IDENT[:, :])
                fp_pe.done(ins, "vtok")
                for q in range(NBLK):
                    score(q)
                for q in range(NBLK):
                    turn(q)
                    values(q)

            pe.wait_ge(fp_dve.sem, fp_dve.value("lo", FOX_HEADS - 1))
            for h in range(FOX_HEADS):
                pe.matmul(bank(4)[:, h * DEC:(h + 1) * DEC], IDENT[:, ROW_LOGF + h:ROW_LOGF + h + 1].broadcast_to([P, P]), R[:, SEQ:TOK], start=True, stop=True)
            pe.wait_ge(fs_dve.sem, fs_dve.value("qk"))
            fs_pe.done(pe.matmul(bank(4)[:, NDH:2 * NDH], ONES[:, :], QKS[:, :, :].rearrange("p b h -> p (b h)"), start=True, stop=True), "snew")
            pe.wait_ge(fs_dve.sem, fs_dve.value("mx"))
            fs_pe.done(pe.transpose(bank(5)[0:NDH, 0:P], MX[:, :, :].rearrange("p b h -> p (b h)"), IDENT[:, :]), "turn")
            pe.wait_ge(fs_dve.sem, fs_dve.value("dg"))
            fs_pe.done(pe.matmul(bank(6, NDH), ONES[0:NDH, :], DG[:, :], start=True, stop=True), "max")
            pe.wait_ge(fs_dve.sem, fs_dve.value("dn"))
            fs_pe.done(pe.matmul(bank(7, NDH), ONES[:, :], DEN[:, :, :].rearrange("p b h -> p (b h)"), start=True, stop=True), "den")
            pe.wait_ge(fs_dve.sem, fs_dve.value("norm"))
            pe.wait_ge(rowsel_set, 2)
            for j in range(2 * GDN_HEADS):
                r = j if j < GDN_HEADS else 32 + j - GDN_HEADS
                pe.wait_ge(ln_act.sem, ln_act.value("sqq" if j < GDN_HEADS else "sqk"))
                for n in range(2):
                    ins = pe.matmul(ACC[0][0:NORM_ROWS, n, 0:HALF], row_select(r), SQH[:, j, n * HALF:(n + 1) * HALF],
                                    start=j == 0, stop=j == 2 * GDN_HEADS - 1)
            ln_pe.done(ins, "sum")
            pe.wait_ge(ln_dve.sem, ln_dve.value("inv"))
            for j in range(2 * GDN_HEADS):
                r = j if j < GDN_HEADS else 32 + j - GDN_HEADS
                if j >= 3:
                    pe.wait_ge(ln_dve.sem, ln_dve.value(f"mul{j - 3}"))
                for n in range(2):
                    ins = pe.matmul(ACC[1 + j % 3][:, n, 0:HALF], IDENT[0:NORM_ROWS, r:r + 1].broadcast_to([NORM_ROWS, P]),
                                    TA[0:NORM_ROWS, n * HALF:(n + 1) * HALF], start=True, stop=True)
                ln_pe.done(ins, f"b{j}")
            pe.wait_ge(ln_dve.sem, ln_dve.value(f"mul{2 * GDN_HEADS - 1}"))
            def per_head(b, left, right, start=True, stop=True):
                for h in range(GDN_HEADS):
                    ins = pe.matmul(bank(b)[:, h * P:(h + 1) * P], left(h), right(h), start=start, stop=stop)
                return ins

            with pe.Fori(0, NBLK) as c:
                def rows_of(c=c):
                    return R[:, bass.ds(c * P, P)]

                def values(s, part):
                    if part == "raw":
                        if s == 0:
                            hold(pe, vo_copied, c + 1)
                        hold(pe, vpage_in[3], 64 * (2 * c + s + 1), 64)
                        pages = range(3 * 4, 4 * 4)
                    else:
                        await_step(pe, v_pool, f"{s}fold", c)
                        pages = range(4 * s, 4 * s + 2)
                    for g in pages:
                        for h in range(FOX_HEADS):
                            probs = SC[:, bass.ds(2 * c + s, 1), g, h:h + 1].rearrange("p a c -> p (a c)") if part == "raw" else ONES[:, 0:1]
                            ins = pe.matmul(bank(7)[:, s * FOX_HEADS + h:s * FOX_HEADS + h + 1], VPAGES[:, g, h * P:(h + 1) * P], probs,
                                            start=s == 0 and g == 12 and h == 0, stop=part != "raw" and g == pages[-1],
                                            skip_group_check=True)
                    v_pe.done(ins, f"{s}{part}")

                await_turns(pe, gl_dve, c)
                await_turns(pe, gl_act, c)
                gl_pe.done(per_head(0, lambda h: IDENT[:, ROW_GC + h:ROW_GC + h + 1].broadcast_to([P, P]), lambda h: rows_of()), "gcb")
                gl_pe.done(per_head(1, lambda h: IDENT[:, ROW_BETA + h:ROW_BETA + h + 1].broadcast_to([P, P]), lambda h: rows_of()), "bb")
                values(0, "raw")
                await_step(pe, gl_act, "vts", c)
                for b, tile, name in ((2, KTS, "ktok"), (3, VTS, "vtok")):
                    for h in range(GDN_HEADS):
                        ins = pe.transpose(bank(b)[:, h * P:(h + 1) * P], tile[:, h, :], IDENT[:, :])
                    gl_pe.done(ins, name)
                await_step(pe, gl_dve, "kbt", c)
                gl_pe.done(per_head(4, lambda h: KTS[:, h, :], lambda h: KBT[:, h, :]), "a")
                gl_pe.done(per_head(5, lambda h: KTS[:, h, :], lambda h: PRJ[:, GQ + h, bass.ds(c * P, P)]), "qk")
                for n in range(LEVELS):
                    await_step(pe, gl_dve, f"x{n - 1}" if n else "ats0", c)
                    gl_pe.done(per_head(6, lambda h: ATS[:, h, :], lambda h: XI[:, h, :]), f"t{n}")
                    if n == 0:
                        continue
                    await_step(pe, gl_act, f"t{n}", c)
                    await_step(pe, gl_dve, f"xt{n - 1}", c)
                    if n < LEVELS - 1:
                        gl_pe.done(per_head(5, lambda h: XIT[:, h, :], lambda h: T1[:, h, :]), f"x{n}")
                    gl_pe.done(per_head(0, lambda h: T1[:, h, :], lambda h: XIT[:, h, :]), f"xt{n}")
                    if n == 2:
                        values(0, "folded")
                    elif n == 4:
                        values(1, "raw")
                await_step(pe, gl_dve, f"xt{LEVELS - 1}", c)
                gl_pe.done(per_head(1, lambda h: XIT[:, h, :], lambda h: VB[:, h, :]), "u")
                gl_pe.done(per_head(2, lambda h: KBE[:, h, :], lambda h: XIT[:, h, :]), "wt")
                await_step(pe, gl_act, "wt", c)
                gl_pe.done(per_head(3, lambda h: WT[:, h, :], lambda h: STATE[:, h, :]), "ws")
                await_step(pe, gl_dve, "vn", c)
                for h in range(GDN_HEADS):
                    pe.matmul(bank(4)[:, h * P:(h + 1) * P], STATE[:, h, :], QET[:, h, :], start=True, stop=False)
                    ins = pe.matmul(bank(4)[:, h * P:(h + 1) * P], VNEW[:, h, :], ATTN[:, h, :], start=False, stop=True)
                gl_pe.done(ins, "o")
                gl_pe.done(per_head(5, lambda h: KDE[:, h, :], lambda h: VNEW[:, h, :]), "s")
                values(1, "folded")
            pe.wait_ge(gl_dve.sem, gl_dve.value("s", NBLK - 1))
            pe.wait_ge(gl_act.sem, gl_act.value("o", NBLK - 1))
            pe.wait_ge(ss_in, 16 * GDN_HEADS)
            pe.wait_ge(gs_dve.sem, gs_dve.value("qkp"))
            for j in range(NJ):
                ins = pe.matmul(bank(0)[:, 2 * j:2 * j + 2], SS[:, j, :], KQ[:, j, :], start=True, stop=True)
            gs_pe.done(ins, "r")
            for k, row in ((0, ROW_BETA), (1, ROW_GC)):
                for h in range(GDN_HEADS):
                    pe.matmul(bank(1)[:, k * NJ + h * DEC:k * NJ + (h + 1) * DEC], IDENT[:, row + h:row + h + 1].broadcast_to([P, P]),
                              R[:, SEQ:TOK], start=True, stop=True)
            gs_pe.done(pe.matmul(bank(1)[:, 2 * NJ:3 * NJ], ONES[:, :], QKP[:, :, :].rearrange("p h b -> p (h b)"), start=True, stop=True), "bc")
            gs_pe.done(pe.transpose(bank(2)[0:NJ, 0:P], KC[:, :, :].rearrange("p h b -> p (h b)"), IDENT[:, :]), "kt")
            pe.wait_ge(gs_dve.sem, gs_dve.value("a3"))
            gs_pe.done(pe.transpose(bank(3)[0:NJ, 0:P], VN2[:, :, :].rearrange("p h b -> p (h b)"), IDENT[:, :]), "vt")
            pe.wait_ge(gs_act.sem, gs_act.value("vt"))
            for h in range(GDN_HEADS):
                pe.wait_ge(gs_dve.sem, gs_dve.value(f"bd{h}"))
                if h >= 2:
                    pe.wait_ge(gs_dve.sem, gs_dve.value(f"s{h - 2}"))
                for n in range(2):
                    ins = pe.matmul(ACC[2 + h % 2][:, n, :], KTK[:, :], VBD[:, h % 2, 4 * n:4 * n + 4, :].rearrange("j b d -> j (b d)"),
                                    start=True, stop=True)
                gs_pe.done(ins, f"up{h}")
            pe.wait_ge(go_act.sem, go_act.value("sq"))
            for j in range(GDN_HEADS):
                for n in range(2):
                    ins = pe.matmul(ACC[0][0:NORM_ROWS, n, 0:HALF], row_select(j), SQO[:, j, n * HALF:(n + 1) * HALF],
                                    start=j == 0, stop=j == GDN_HEADS - 1)
            go_pe.done(ins, "sum")
            pe.wait_ge(gs_dve.sem, gs_dve.value(f"s{GDN_HEADS - 1}"))
            pe.wait_ge(go_dve.sem, go_dve.value("inv"))
            for j in range(GDN_HEADS):
                if j >= 2:
                    pe.wait_ge(go_dve.sem, go_dve.value(f"norm{j - 2}"))
                for n in range(2):
                    ins = pe.matmul(ACC[2 + j % 2][:, n, 0:HALF], IDENT[0:NORM_ROWS, j:j + 1].broadcast_to([NORM_ROWS, P]),
                                    TA[0:NORM_ROWS, n * HALF:(n + 1) * HALF], start=True, stop=True)
                go_pe.done(ins, f"b{j}")
            pe.wait_ge(fs_dve.sem, FOX_END)
            with pe.Fori(0, KD // 2) as i:
                for s in range(2):
                    hold(pe, tile_free, tile_at["ab_out"] + 2 * i + s + 3)
                    project(unit_at["ab_out"] + 2 * i + s, (unit_at["ab_out"] + s) % 2, KD, s, MOH, MOL,
                            late=(FOX_HEADS, go_dve.sem, go_dve.value("lo")))
            up(1)
            down("down1", HH, HL, KH, 2, (h_ready, KF + 1))
            up(2)
            down("down2", HH, HL, KH, 2, (h_ready, 2 * KF + 1))

            def ret_turn(h, p):
                first, is_first, is_last = ret_first(h), isinstance(h, int) and h == 0, isinstance(h, int) and h == RET_HEADS
                g, o = h - 1, 1 - p
                count = [0]

                def tile():
                    n = count[0]
                    count[0] += 1
                    hold(pe, tile_free, RTILE + first + n + 3)
                    project(RU + first + n, (RU + n) % 2, KD, n % 2, XH, XL, ready=(xl_ready, KD * 4 + 1))

                def turned(b, source, name):
                    for n in range(NBLK):
                        ins = pe.transpose(bank(b)[:, n * P:(n + 1) * P], source(n), IDENT[:, :])
                    rm_pe.done(ins, name)

                def update(n):
                    if n >= 2:
                        await_step(pe, rm_dve, f"u{n - 2}", g)
                    for b in range(2):
                        ins = pe.matmul(bank(6 + n % 2)[:, b * RET_DV:(b + 1) * RET_DV], KBLK[:, (2 * n + b) % (DEC // 2), :],
                                        KVT[:, P:3 * P], start=True, stop=True)
                    rm_pe.done(ins, f"r{n}")

                if not is_last:
                    tile()
                if is_first:
                    statistics(4)
                if not is_first:
                    hold(pe, tile_free, RTILE + first + 4)
                    await_step(pe, rp_dve, "k", g)
                    hold(pe, states_stepped, g + 1)
                    turned(4, lambda n: KB[o][:, n * P:(n + 1) * P], "ktok")
                    turned(5, lambda n: VBH[o][:, 0, n * P:(n + 1) * P], "v0")
                    turned(6, lambda n: VBH[o][:, 1, n * P:(n + 1) * P], "v1")
                    for n in range(NBLK):
                        ins = pe.matmul(bank(7)[:, n * P:(n + 1) * P], KB[o][:, n * P:(n + 1) * P], QB[o][:, n * P:(n + 1) * P],
                                        start=True, stop=True)
                    rm_pe.done(ins, "a")
                if not is_last:
                    tile()
                if not is_first:
                    await_step(pe, rm_dve, "att", g)
                    await_step(pe, rm_act, "vt1", g)
                    for n in range(NBLK):
                        ins = pe.matmul(bank(6 + n // 2)[:, (n % 2) * RET_DV:(n % 2 + 1) * RET_DV], KD_[:, n, :], VTK_R[:, n, :],
                                        start=True, stop=True)
                    rm_pe.done(ins, "kv")
                if not is_last:
                    tile()
                if not is_first:
                    await_step(pe, rm_dve, "s3", g)
                    for v in range(2):
                        for n in range(NBLK):
                            out = bank(4 + v)[:, n * P:(n + 1) * P]
                            ins = pe.matmul(out, VTK_R[:, n, v * P:(v + 1) * P], ATT[:, n * P:(n + 1) * P], start=True, stop=n == 0)
                            if n > 0:
                                ins = pe.matmul(out, SALL[n - 1][:, v * P:(v + 1) * P], QB[o][:, n * P:(n + 1) * P],
                                                start=False, stop=True)
                    rm_pe.done(ins, "o")
                    hold(pe, rss_in, 16 * g + 16, 16)
                    for b in range(DEC):
                        for v in range(2):
                            pe.matmul(bank(6)[:, v * DEC + b:v * DEC + b + 1], SSR[:, b, v * P:(v + 1) * P], QSD[:, b:b + 1],
                                      start=True, stop=True)
                    rm_pe.done(pe.matmul(bank(6)[:, 2 * DEC:3 * DEC], ONES[:, :], QKR[:, :], start=True, stop=True), "cross")
                if not is_last:
                    tile()
                if not is_first:
                    await_step(pe, rm_act, "o1", g)
                    await_step(pe, rm_dve, "os", g)
                    for n in range(2):
                        for v in range(2):
                            ins = pe.matmul(ACC[2][:, n, 0:HALF], ONES[:, :], VBH[o][:, v, n * HALF:(n + 1) * HALF],
                                            start=v == 0, stop=v == 1)
                    rm_pe.done(ins, "mean")
                    pe.transpose(bank(7)[0:DEC, 0:P], KB[o][:, SEQ:TOK], IDENT[:, :])
                    for v in range(2):
                        ins = pe.transpose(bank(7)[0:DEC, (v + 1) * P:(v + 2) * P], VSC[:, v, :], IDENT[:, :])
                    rm_pe.done(ins, "tok")
                    tile()
                    await_step(pe, rm_act, "sq1", g)
                    for n in range(2):
                        for v, squares in enumerate((SQ, SSQ)):
                            ins = pe.matmul(ACC[2][:, n, 0:HALF], ONES[:, :], squares[:, n * HALF:(n + 1) * HALF],
                                            start=v == 0, stop=v == 1)
                    rm_pe.done(ins, "var")
                    await_step(pe, rm_dve, "kb0", g)
                    update(0)
                    update(1)
                    tile()
                    await_step(pe, rm_dve, "kb1", g)
                    update(2)
                    update(3)

            ret_turns(pe, ret_turn)
            down("ret_out", RMOH, RMOL, KD, 2, None, late=(RCH - 2, rm_dve.sem, rm_dve.value("lo1", RET_HEADS - 1)))
            up(3)
            down("down3", HH, HL, KH, 2, (h_ready, 3 * KF + 1))
            statistics(6)
            for n in range(NBLK):
                for d in range(KD):
                    pe.wait_ge(y_ready, d + 1)
                    if n >= 2 and d == 0:
                        pe.wait_ge(final_copied.sem, n - 1)
                    ins = pe.transpose(ACC[n % 2][:, d // 4, (d % 4) * P:(d % 4 + 1) * P], YF[:, d, n * P:(n + 1) * P], IDENT[:, :])
                ins.then_inc(final_turned, 1)
            for d in range(KD):
                ins = pe.transpose(ACC[2][0:DEC, d // 4, (d % 4) * P:(d % 4 + 1) * P], YF[:, d, SEQ:TOK], IDENT[:, :])
            ins.then_inc(final_turned, 1)

        @block.scalar
        def _(act):
            def norm_chunk(r, d):
                hold(act, tile_free, tile_at_update[r] + d + 5)
                hold(act, ssq_ready, SSQ_STEPS * r + d + 1)
                act.activation(SQ[:, :], X[:, bass.ds(d, 1), :].rearrange("p a t -> p (a t)"), ACT.Square).then_inc(sq_ready, 1)
                act.activation(XH[:, bass.ds(d, 1), :].rearrange("p a t -> p (a t)"),
                               X[:, bass.ds(d, 1), :].rearrange("p a t -> p (a t)"), ACT.Identity,
                               scale=PAR[:, bass.ds(PAR_NORM + KD * r + d, 1)]).then_inc(xh_ready, 1)

            def load_logf(first, count):
                pairs = LF[:, :, :, :].rearrange("p b g h -> p (b g) h")
                for n in range(count):
                    page = act.value_load(PT_SB[0:1, bass.ds(first + n, 1)], min_val=0, max_val=N_POOL - 1)
                    act.dma_start(pairs[:, bass.ds(first + n, 1), :].rearrange("p a h -> p (a h)"),
                                  cache_logf[0, bass.ds(page, 1)].rearrange("a t h -> (a t) h")).then_inc(lf_in, 16)

            def norm_chunks(r, logf_first=None, logf_count=0):
                with act.Fori(0, KD) as d:
                    norm_chunk(r, d)
                    if logf_count:
                        load_logf(logf_count * d + logf_first, logf_count)

            def deviation(r):
                act.wait_ge(stat_done, r + 1)
                act.activation(halves(RSTD[:, :]), ACC[3][:, :, 0:HALF], ACT.Sqrt, bias=EPSC[:, 0:1],
                               scale=1.0 / D_MODEL).then_inc(std_ready, 1)

            def up(f, logf_count=0):
                t0 = tile_at[f"up{f}"]
                with act.Fori(0, KF) as j:
                    hold(act, tile_free, t0 + 2 * j + 5)
                    act.activation(TA[:, :], TA[:, :], ACT.Silu).then_inc(act_ready, 1)
                    hold(act, hfull_ready, KF * f + j + 1)
                    act.activation(HH[:, bass.ds(j, 1), :].rearrange("p a t -> p (a t)"), TH[:, :], ACT.Copy).then_inc(hh_ready, 1)
                    if logf_count:
                        load_logf(logf_count * j, logf_count)

            for steps in OPENED["act"]:
                act.sem_inc(steps.sem, 1)
            act.sem_inc(vo_copied, 1)
            act.wait_ge(par_turned, 1)
            act.activation(PAR[:, 0:PAR_ROWS], bank(7, PAR_ROWS), ACT.Copy).then_inc(par_ready, 1)
            act.wait_ge(par_ready, 1)
            act.wait_ge(ones_set, 4)
            norm_chunks(0)
            deviation(0)
            act.wait_ge(pt_in, 16)
            up(0, 4)
            norm_chunks(1, 4 * KF, 5)
            deviation(1)
            act.wait_ge(cols_in, 48)
            gate_act.done(act.activation(COLS[ROW_GC:ROW_GC + 4, 3:4], COLS[ROW_GC:ROW_GC + 4, 1:2], ACT.Exp), "fac")
            act.wait_ge(gate_dve.sem, gate_dve.value("az"))
            gate_act.done(act.activation(TB[:, :], TB[:, :], ACT.Exp, scale=-1.0), "e")
            act.wait_ge(gate_act.sem, gate_act.value("e"))
            gate_act.done(act.activation(TB[:, :], TB[:, :], ACT.Ln, bias=EPSC[:, 2:3]), "l")
            act.wait_ge(gate_dve.sem, gate_dve.value("t"))
            gate_act.done(act.activation(R[ROW_BETA:ROW_BETA + 4, :], TH[ROW_BETA:ROW_BETA + 4, :], ACT.Exp), "beta")


            def select(b):
                act.activation(SELB, IDENT[0:DEC, bass.ds(b, 1)].broadcast_to([DEC, P]), ACT.Copy).then_inc(selb_ready, 1)

            def keep_q(b, parity, multiplied):
                hold(act, qb_ready, b + 1)
                hold(act, prod_done, multiplied)
                act.activation(QBR[:, parity, :], bank(4), ACT.Copy).then_inc(qbr_ready, 1)

            act.wait_ge(qtok_turned, 1)
            act.wait_ge(gate_dve.sem, gate_dve.value("negc"))
            act.activation(QTOK, bank(5)[0:DEC, :], ACT.Copy).then_inc(qtok_ready, 1)
            select(0)
            act.wait_ge(used, AB_UNIT + 2)
            act.wait_ge(pt_in, 16)
            act.wait_ge(qb_ready, 1)
            act.activation(QBR[:, 0, :], bank(4), ACT.Copy).then_inc(qbr_ready, 1)
            select(1)
            with act.Fori(0, EARLY // 2) as i:
                for s in range(2):
                    for m in range(4 * s, 4 * s + 4):
                        load_keys(act, 0, m % 2, KBATCH * (8 * i + m), 8 * i + m)
                        if m % 4 == 1:
                            keep_q(2 * i + (s + 1), 1 - s, 8 * i + (4 * s + 2))
                            select(2 * i + (s + 2))
            keep_q(EARLY + 1, 1, 4 * EARLY + 2)
            act.wait_ge(fs_pe.sem, fs_pe.value("tok"))
            fs_act.done(act.activation(KTOKS[:, :], bank(0)[0:DEC, :], ACT.Copy), "ktok")
            fs_act.done(act.activation(VTOKS, bank(1)[0:DEC, :], ACT.Copy), "vtok")
            act.wait_ge(gp_pe.sem, gp_pe.value("prev"))
            gp_act.done(act.activation(PREV[:, :, :, :].rearrange("p c b w -> p (c b w)"), bank(5, CONV_CH * DEC * (CONV_W - 1)), ACT.Copy), "prev")
            act.wait_ge(gp_pe.sem, gp_pe.value("tails"))
            for n, b in enumerate((6, 7, 2)):
                gp_act.done(act.activation(TAILS[:, n * 512:(n + 1) * 512], bank(b)[0:DEC + CONV_W - 1, :], ACT.Copy), f"tail{n}")
            with act.Fori(0, FOX_HEADS) as h:
                def chunk(first):
                    return PRJ[:, bass.ds(h + first, 1), 0:SEQ].rearrange("p a t -> p (a t)")

                def exponent(q):
                    await_step(act, fp_dve, f"neg{q}", h)
                    fp_act.done(act.activation(PROB[:, q, 0:(q + 1) * P], bank(SCORE_BANK[q], (q + 1) * P), ACT.Exp,
                                               bias=STAT[:, q, 1:2], accum_out=STAT[:, q, 2:3]), f"exp{q}")

                def turned(q):
                    await_step(act, fp_pe, f"turn{q}", h)
                    fp_act.done(act.activation(PTR[:, q % 2, 0:q + 1, :].rearrange("p k q -> p (k q)"),
                                               bank(2 + q % 2, (q + 1) * P), ACT.Copy), f"pt{q}")

                fp_act.done(act.activation(QS[:, :], chunk(AB_Q), ACT.Copy, scale=SCALE), "q")
                fp_act.done(act.activation(KS[:, :], chunk(AB_K), ACT.Copy), "k")
                fp_act.done(act.activation(VS[:, :], chunk(AB_V), ACT.Copy), "v")
                fp_act.done(act.activation(SELH[:, :], IDENT[:, bass.ds(h + ROW_NEGC, 1)].broadcast_to([P, P]), ACT.Copy), "sel")
                await_step(act, fp_pe, "ktok", h)
                hold(act, fk_stored, 16 * h + 16, 16)
                fp_act.done(act.activation(TA[:, 0:SEQ], bank(5), ACT.Copy), "ktok")
                for q in range(NBLK):
                    exponent(q)
                for q in range(NBLK):
                    turned(q)
                await_step(act, fp_pe, "pv3", h)
                fp_act.done(act.activation(MOH[:, bass.ds(h, 1), 0:SEQ].rearrange("p a t -> p (a t)"), bank(4), ACT.Copy), "hi")

            act.wait_ge(fk_stored, 16 * FOX_HEADS + 16)
            act.wait_ge(fv_stored, 16 * FOX_HEADS + 16)
            def channels(first, count):
                return PRJ[:, first:first + count, :]

            act.wait_ge(cv_dve.sem, cv_dve.value("w3", CONV_CH - 1))
            act.activation(channels(GQ, 2 * GDN_HEADS), channels(GQ, 2 * GDN_HEADS), ACT.Silu).then_inc(cv_act, 1)
            act.wait_ge(fs_dve.sem, fs_dve.value("sub"))
            sc = SC[:, :, :, :].rearrange("p b g h -> p (b g h)")
            fs_act.done(act.activation(sc, sc, ACT.Exp), "exp")
            act.wait_ge(fs_dve.sem, fs_dve.value("subn"))
            sn = SN[:, :, :].rearrange("p b h -> p (b h)")
            fs_act.done(act.activation(sn, sn, ACT.Exp), "expn")
            act.wait_ge(tails_stored, 64)
            act.wait_ge(cv_act, 1)
            ln_act.done(act.activation(SQH[:, 0:GDN_HEADS, :], channels(GQ, GDN_HEADS), ACT.Square), "sqq")
            ln_act.done(act.activation(SQH[:, GDN_HEADS:, :], channels(GK, GDN_HEADS), ACT.Square), "sqk")
            act.activation(channels(GV, 2 * GDN_HEADS), channels(GV, 2 * GDN_HEADS), ACT.Silu).then_inc(cv_act, 1)
            act.wait_ge(ln_pe.sem, ln_pe.value("sum"))
            for rows, c, scale, name in ((slice(0, 32), 1, float(P), "stdq"), (slice(32, NORM_ROWS), 0, 1.0, "stdk")):
                ln_act.done(act.activation(halves(TA[rows, :]), ACC[0][rows, :, 0:HALF], ACT.Sqrt, bias=EPSC[rows, c:c + 1], scale=scale), name)
            act.wait_ge(ln_dve.sem, ln_dve.value(f"mul{2 * GDN_HEADS - 1}"))
            act.wait_ge(tails_stored, 64)
            with act.Fori(0, NBLK) as c:
                def chunk_of(first):
                    return PRJ[:, first:first + GDN_HEADS, bass.ds(c * P, P)]

                await_turns(act, gl_dve, c)
                gl_act.done(act.activation(KTS[:, :, :], chunk_of(GK), ACT.Copy), "kts")
                gl_act.done(act.activation(VTS[:, :, :], chunk_of(GV), ACT.Copy), "vts")
                await_step(act, gl_dve, "gd", c)
                gl_act.done(act.activation(GAM[:, :, :], GAM[:, :, :], ACT.Exp), "gam")
                gl_act.done(act.activation(EG[:, :, :].rearrange("p h i -> p (h i)"), bank(0), ACT.Exp), "eg")
                gl_act.done(act.activation(KDC[:, :], KDC[:, :], ACT.Exp), "kdc")
                gl_act.done(act.activation(EGC[:, :], RT[:, bass.ds(c, 1), ROW_GC:ROW_GC + 4].rearrange("p a h -> p (a h)"), ACT.Exp), "egc")
                for n in range(1, LEVELS):
                    await_step(act, gl_pe, f"t{n}", c)
                    gl_act.done(act.activation(T1[:, :, :].rearrange("p h i -> p (h i)"), bank(6), ACT.Copy), f"t{n}")
                await_step(act, gl_pe, "u", c)
                gl_act.done(act.activation(VNEW[:, :, :].rearrange("p h i -> p (h i)"), bank(1), ACT.Copy), "u")
                await_step(act, gl_pe, "wt", c)
                gl_act.done(act.activation(WT[:, :, :].rearrange("p h i -> p (h i)"), bank(2), ACT.Copy), "wt")
                await_step(act, gl_pe, "o", c)
                gl_act.done(act.activation(chunk_of(GQ), bank(4).rearrange("p (h i) -> p h i", h=GDN_HEADS), ACT.Copy), "o")
                await_step(act, v_pe, "1folded", c)
                act.activation(OS[:, :, bass.ds(2 * c, 2)], bank(7, 2 * FOX_HEADS).rearrange("p (s h) -> p h s", s=2), ACT.Copy).then_inc(vo_copied, 1)
            act.wait_ge(fs_dve.sem, fs_dve.value("add"))
            fs_act.done(act.activation(MOH[:, 0:FOX_HEADS, SEQ:TOK], OS[:, :, :], ACT.Copy), "hi")
            act.wait_ge(gs_pe.sem, gs_pe.value("bc"))
            gs_act.done(act.activation(EGS[:, :, :].rearrange("p h b -> p (h b)"), bank(1)[:, NJ:2 * NJ], ACT.Exp), "egs")
            gs_act.done(act.activation(BEQ[:, :, :].rearrange("p n j -> p (n j)"), bank(1, 3 * NJ), ACT.Copy), "beq")
            act.wait_ge(gs_pe.sem, gs_pe.value("kt"))
            gs_act.done(act.activation(KTK[:, :], bank(2)[0:NJ, 0:P], ACT.Copy), "kt")
            act.wait_ge(gs_pe.sem, gs_pe.value("vt"))
            gs_act.done(act.activation(VTK[:, :], bank(3)[0:NJ, 0:P], ACT.Copy), "vt")
            act.wait_ge(gs_dve.sem, gs_dve.value("o3"))
            go_act.done(act.activation(SQO[:, :, :], channels(GQ, GDN_HEADS), ACT.Square), "sq")
            act.wait_ge(go_pe.sem, go_pe.value("sum"))
            go_act.done(act.activation(halves(TA[0:NORM_ROWS, :]), ACC[0][0:NORM_ROWS, :, 0:HALF], ACT.Sqrt,
                                       bias=EPSC[0:NORM_ROWS, 0:1], scale=1.0 / P), "std")
            act.wait_ge(go_dve.sem, go_dve.value("gate"))
            go_act.done(act.activation(MOH[:, FOX_HEADS:, :], NRM[:, :, :], ACT.Copy), "hi")
            act.wait_ge(gdn_stored, 1)
            norm_chunks(2)
            deviation(2)
            up(1)
            norm_chunks(3)
            deviation(3)
            up(2)
            norm_chunks(4)
            deviation(4)
            act.wait_ge(ret_consts_in, 64)

            def ret_turn(h, p):
                first, is_first, is_last = ret_first(h), isinstance(h, int) and h == 0, isinstance(h, int) and h == RET_HEADS
                g, o = h - 1, 1 - p

                def swap(n, name):
                    hold(act, tile_free, RTILE + first + n + 5)
                    act.activation(TB[0:64, :], TA[64:P, :], ACT.Copy)
                    rp_act.done(act.activation(TB[64:P, :], TA[0:64, :], ACT.Copy), name)

                def gate(v):
                    gated = RGATE[:, bass.ds(2 * g + v, 1), :].rearrange("p a t -> p (a t)")
                    await_step(act, rm_dve, f"ga{v}", g)
                    rm_act.done(act.activation(gated, gated, ACT.Silu), f"si{v}")
                    await_step(act, rm_dve, f"g{v}", g)
                    rm_act.done(act.activation(RMOH[:, bass.ds(2 * g + v, 1), :].rearrange("p a t -> p (a t)"), VBH[o][:, v, :], ACT.Copy), f"hi{v}")

                if not is_last:
                    swap(0, "q")
                if not is_first:
                    await_step(act, rm_pe, "v1", g)
                    for v in range(2):
                        rm_act.done(act.activation(VTK_R[:, :, v * P:(v + 1) * P], bank(5 + v).rearrange("p (n d) -> p n d", n=NBLK),
                                                   ACT.Copy), f"vt{v}")
                if not is_last:
                    swap(1, "k")
                if not is_first:
                    hold(act, rss_stored, 16 * g + 16, 16)
                    act.dma_start(SSR[:, :, :], state_ret[0][:, bass.ds(g, 1)].rearrange("b a k v -> k b (a v)")).then_inc(rss_in, 16)
                    await_step(act, rm_dve, "s3", g)
                    act.dma_start(rs_prompt[0, 0, bass.ds(g, 1)].rearrange("a k v -> (a k) v"), SALL[NBLK - 1][:, :]).then_inc(rsp_stored, 16)
                    await_step(act, rm_pe, "o", g)
                    await_step(act, rm_dve, "vsc", g)
                    for v in range(2):
                        rm_act.done(act.activation(VBH[o][:, v, 0:SEQ], bank(4 + v), ACT.Copy), f"o{v}")
                    await_step(act, rm_pe, "tok", g)
                    rm_act.done(act.activation(KVT[:, :], bank(7)[0:DEC, 0:3 * P], ACT.Copy), "tk")
                    for v, (squares, name) in enumerate(((SQ, "c0"), (SSQ, "c1"))):
                        await_step(act, rm_dve, name, g)
                        rm_act.done(act.activation(squares[:, :], VBH[o][:, v, :], ACT.Square), f"sq{v}")
                    await_step(act, rm_pe, "var", g)
                    rm_act.done(act.activation(halves(TB[:, :]), ACC[2][:, :, 0:HALF], ACT.Sqrt, bias=EPSC[:, 0:1],
                                               scale=1.0 / RET_DV), "std")
                    gate(0)
                    gate(1)
                    hold(act, states_stepped, g + 2)
                    act.dma_start(rs_sample[0][:, bass.ds(g, 1)].rearrange("b a k v -> k b (a v)"), SSR[:, :, :]).then_inc(rss_stored, 16)

            ret_turns(act, ret_turn)
            norm_chunks(5)
            deviation(5)
            up(3)
            norm_chunks(6)
            deviation(6)
            for n in range(NBLK):
                act.wait_ge(final_turned, n + 1)
                final_copied.done(act.activation(YTOK[:, n, :].rearrange("p (h c) -> p h c", h=2), ACC[n % 2][:, :, :], ACT.Copy), f"tok{n}")
            act.wait_ge(final_turned, NBLK + 1)
            final_copied.done(act.activation(YTOKS[:, :].rearrange("p (h c) -> p h c", h=2), ACC[2][0:DEC, :, :], ACT.Copy), "sample")

        @block.vector
        def _(dve):
            def clear_squares(r):
                if r >= 1:
                    dve.wait_ge(stat_done, r)
                dve.memset(SSQ[:, :], 0.0).then_inc(ssq_ready, 1)

            def norm_chunk(r, d):
                n = KD * r + d
                hold(dve, sq_ready, n + 1)
                hold(dve, ssq_ready, SSQ_STEPS * r + d + 1)
                dve.tensor_tensor(SSQ[:, :], SSQ[:, :], SQ[:, :], ALU.add).then_inc(ssq_ready, 1)
                hold(dve, xh_ready, n + 1)
                dve.scalar_tensor_tensor(out=XL[:, bass.ds(d, 1), :].rearrange("p a t -> p (a t)"),
                                         in0=X[:, bass.ds(d, 1), :].rearrange("p a t -> p (a t)"),
                                         scalar=PAR[:, bass.ds(PAR_NORM + KD * r + d, 1)],
                                         in1=XH[:, bass.ds(d, 1), :].rearrange("p a t -> p (a t)").bitcast(F32),
                                         op0=ALU.mult, op1=ALU.subtract).then_inc(xl_ready, 1)

            def update(name, scale, per_chunk=2):
                u0, r = unit_at[name], UPDATE[name]
                clear_squares(r)
                with dve.Fori(0, KD // 2) as i:
                    for s in range(2):
                        d = 2 * i + s
                        hold(dve, used, u0 + per_chunk * d + per_chunk + 2)
                        xd = X[:, bass.ds(d, 1), :].rearrange("p a (n t) -> p (a n) t", n=2)
                        dve.scalar_tensor_tensor(out=xd, in0=ACC[s][:, :, 0:HALF], scalar=scale, in1=xd,
                                                 op0=ALU.mult, op1=ALU.add).then_inc(tile_free, 1)
                        norm_chunk(r, d)

            def reciprocal(r):
                dve.wait_ge(std_ready, r + 1)
                dve.reciprocal(RSTD[:, :], RSTD[:, :]).then_inc(rstd_ready, 1)
                dve.wait_ge(rstd_ready, r + 1)

            def up(f):
                t0, u0 = tile_at[f"up{f}"], unit_at[f"up{f}"]
                with dve.Fori(0, KF // 2) as i:
                    for s in range(2):
                        t = t0 + 4 * i + 2 * s
                        n = KF * f + 2 * i + s
                        hold(dve, used, u0 + 4 * i + 2 * s + 3)
                        dve.tensor_tensor(halves(TA[:, :]), ACC[2 * s][:, :, 0:HALF], halves(RSTD[:, :]),
                                          ALU.mult).then_inc(tile_free, 1)
                        hold(dve, used, u0 + 4 * i + 2 * s + 4)
                        dve.tensor_tensor(halves(TB[:, :]), ACC[2 * s + 1][:, :, 0:HALF], halves(RSTD[:, :]),
                                          ALU.mult).then_inc(tile_free, 1)
                        hold(dve, act_ready, n + 1)
                        hold(dve, tile_free, t + 6)
                        dve.tensor_tensor(TH[:, :], TA[:, :], TB[:, :], ALU.mult).then_inc(hfull_ready, 1)
                        hold(dve, hh_ready, n + 1)
                        dve.tensor_tensor(HL[:, bass.ds(2 * i + s, 1), :].rearrange("p a t -> p (a t)"), TH[:, :],
                                          HH[:, bass.ds(2 * i + s, 1), :].rearrange("p a t -> p (a t)").bitcast(F32),
                                          ALU.subtract).then_inc(h_ready, 1)

            dve.sem_inc(tile_free, 4)
            dve.sem_inc(states_stepped, 1)
            for steps in OPENED["dve"]:
                dve.sem_inc(steps.sem, 1)
            dve.memset(ONES[:, :], 1.0).then_inc(ones_set, 1)
            dve.memset(EPSC[:, 0:1], EPS).then_inc(ones_set, 1)
            dve.memset(EPSC[:, 1:2], P * EPS).then_inc(ones_set, 1)
            dve.memset(EPSC[:, 2:3], 1.0).then_inc(ones_set, 1)
            dve.memset(ROWSEL[:, :], 0.0).then_inc(rowsel_set, 1)
            dve.wait_ge(rowsel_set, 1)
            dve.memset(ROWSEL[:, ROWSEL_ONE:ROWSEL_ONE + 1], 1.0).then_inc(rowsel_set, 1)
            dve.memset(COLS[:, 0:2], 0.0).then_inc(cols_clear, 1)
            dve.memset(COLS[:, 2:3], 1.0).then_inc(cols_clear, 1)
            dve.memset(COLS[:, 3:4], 0.0).then_inc(cols_clear, 1)
            dve.wait_ge(cols_clear, 3)
            dve.memset(COLS[ROW_GC:ROW_GC + 4, 2:3], -1.0).then_inc(cols_clear, 1)
            dve.memset(COLS[ROW_LOGF:ROW_LOGF + 4, 3:4], 1.0).then_inc(cols_clear, 1)
            dve.sem_inc(prod_done, 2)
            dve.sem_inc(sum_done, 1)
            dve.wait_ge(par_ready, 1)
            clear_squares(0)
            for d in range(KD + 1):
                if d >= 1:
                    norm_chunk(0, d - 1)
                if d == KD:
                    break
                dve.wait_ge(loaded_turned, d + 1)
                dve.tensor_copy(X[:, d, 0:SEQ], ACC[d % 4][:, 0, 0:SEQ]).then_inc(x_part, 1)
                dve.wait_ge(x_part, d + 1)
                dve.tensor_copy(X[:, d, SEQ:TOK], ACC[d % 4][:, 1, 0:DEC]).then_inc(tile_free, 1)
            reciprocal(0)
            up(0)
            update("down0", 0.5)
            reciprocal(1)
            def take(f, s):
                hold(dve, used, AB_UNIT + f + 3)
                dve.tensor_tensor(PRJ[:, bass.ds(f, 1), :].rearrange("p a (n t) -> p (a n) t", n=2),
                                  ACC[(s + 1) % 2][:, :, 0:HALF], halves(RSTD[:, :]), ALU.mult).then_inc(tile_free, 1)

            def key_scores(place, slot, n, b, scores):
                batch, of_slot, parity = n
                landed = 16 * KBATCH
                hold(dve, kpage_in[slot], landed * of_slot + landed, landed)
                hold(dve, qbr_ready, b + 1)
                hold(dve, sum_done, batch + 1)
                dve.tensor_tensor(PROD[place][:, :, :], KPAGES[place][:, slot, :, :],
                                  QBR[:, parity:parity + 1, :].broadcast_to([P, KBATCH, FOX_HEADS * P]), ALU.mult).then_inc(prod_done, 1)
                hold(dve, prod_done, batch + 3)
                dve.tensor_reduce(scores, PROD[place][:, :, :].rearrange("p g (h d) -> p g h d", h=FOX_HEADS),
                                  AX, ALU.add).then_inc(sum_done, 1)

            dve.memset(R[:, :], 0.0).then_inc(clear_r, 1)
            dve.wait_ge(clear_r, 1)
            dve.wait_ge(cols_in, 48)
            dve.wait_ge(cols_clear, 5)
            dve.wait_ge(used, GATE_UNIT + 3)
            dve.tensor_tensor(halves(TA[:, :]), ACC[0][:, :, 0:HALF], halves(RSTD[:, :]), ALU.mult).then_inc(tile_free, 1)

            dve.wait_ge(tile_free, GATE_TILE + 5)
            gate_dve.done(dve.tensor_scalar(TA[:, :], TA[:, :], COLS[:, 0:1], None, ALU.add), "z")
            dve.wait_ge(gate_dve.sem, gate_dve.value("z"))
            gate_dve.done(dve.scalar_tensor_tensor(out=TB[:, :], in0=TA[:, :], scalar=-1.0, in1=TA[:, :], op0=ALU.mult, op1=ALU.max), "az")
            take(0, 0)
            dve.wait_ge(gate_act.sem, gate_act.value("l"))
            dve.tensor_scalar(TH[:, :], TA[:, :], COLS[:, 2:3], 0.0, ALU.mult, ALU.min).then_inc(clear_r, 1)
            dve.wait_ge(clear_r, 2)
            gate_dve.done(dve.tensor_tensor(TH[:, :], TH[:, :], TB[:, :], ALU.subtract), "t")
            dve.wait_ge(gate_dve.sem, gate_dve.value("t"))
            gate_dve.done(dve.tensor_scalar(TA[:, :], TH[:, :], COLS[:, 3:4], None, ALU.mult), "g")
            dve.wait_ge(gate_dve.sem, gate_dve.value("g"))
            take(1, 1)
            lo, hi = ROW_LOGF, ROW_LOGF + 4
            gate_dve.done(dve.tensor_copy(R[lo:hi, :], TA[lo:hi, :]), "logf")
            gate_dve.done(dve.tensor_tensor_scan(SQ[lo:hi, 0:SEQ], ONES[lo:hi, 0:1].broadcast_to([4, SEQ]), TA[lo:hi, 0:SEQ],
                                                 0.0, ALU.mult, ALU.add), "c")
            dve.wait_ge(gate_dve.sem, gate_dve.value("c"))
            gate_dve.done(dve.tensor_scalar(R[ROW_NEGC:ROW_NEGC + 4, 0:SEQ], SQ[lo:hi, 0:SEQ], -1.0, None, ALU.mult), "negc")
            take(2, 2)
            lo, hi = ROW_GC, ROW_GC + 4
            for n in range(NBLK):
                gate_dve.done(dve.tensor_tensor_scan(R[lo:hi, n * P:(n + 1) * P], ONES[lo:hi, :], TA[lo:hi, n * P:(n + 1) * P],
                                                     0.0, ALU.mult, ALU.add), f"gc{n}")
            gate_dve.done(dve.tensor_copy(R[lo:hi, SEQ:TOK], TA[lo:hi, SEQ:TOK]), "gcs")
            take(3, 3)
            with dve.Fori(0, (AB_CH - 4) // 8) as i:
                for m in range(8):
                    take(8 * i + (m + 4), m)
                    g = KBATCH * (m % 4)
                    key_scores(0, m % 2, (8 * i + m, 4 * i + m // 2, m // 4), 2 * i + m // 4,
                               SC[:, bass.ds(2 * i + m // 4, 1), g:g + KBATCH, :].rearrange("p a g h -> p (a g) h"))
            dve.wait_ge(gate_pe.sem, gate_pe.value("rt"))
            gate_dve.done(dve.tensor_copy(RT[:, :, :].rearrange("p n c -> p (n c)"), bank(2)), "rt")
            gate_dve.done(dve.tensor_copy(RTS[:, :], bank(3)[0:DEC, 0:P]), "rts")

            def chain(ins, name):
                fs_dve.done(ins, name)
                dve.wait_ge(fs_dve.sem, fs_dve.value(name))

            def by_head(chunk):
                return PRJ[:, chunk:chunk + FOX_HEADS, SEQ:TOK].rearrange("p h b -> p b h")

            def over_pages(tile):
                return tile[:, :, None, :].broadcast_to([P, DEC, N_PAGES, FOX_HEADS])

            dve.wait_ge(fs_pe.sem, fs_pe.value("total"))
            chain(dve.memset(SUF[:, :, 15, :], 0.0), "suf15")
            total = bank(4).rearrange("p (b g h) -> p b g h", g=N_PAGES, h=FOX_HEADS)
            for g in range(14, -1, -1):
                chain(dve.tensor_tensor(SUF[:, :, g, :], total[:, :, g + 1, :], SUF[:, :, g + 1, :], ALU.add), f"suf{g}")
            suf = SUF[:, :, :, :].rearrange("p b g h -> p (b g h)")
            chain(dve.tensor_tensor(suf, bank(3), suf, ALU.add), "addlater")

            dve.wait_ge(gp_act.sem, gp_act.value("prev"))
            dve.wait_ge(gp_pe.sem, gp_pe.value("tails"))
            with dve.Fori(0, FOX_HEADS) as h:
                def keys(m):
                    key_scores(1, m, (2 * h + (4 * EARLY + m), h + 2 * EARLY, m), EARLY + m, SC[:, EARLY + m, bass.ds(KBATCH * h, KBATCH), :])

                def convolve(j):
                    c, tile = 3 * h + j, (SQ, SSQ, TH)[j]
                    source = PRJ[:, bass.ds(c + AB_CONV, 1), :].rearrange("p a t -> p (a t)")

                    def tap(w):
                        return PAR[:, bass.ds(c + PAR_CONV + CONV_CH * w, 1)]

                    cv_dve.done(dve.memset(tile[:, 0:CONV_W - 1], 0.0), "z")
                    for s in range(CONV_W - 1, 0, -1):
                        k = CONV_W - 1 - s
                        prev = PREV[:, bass.ds(c, 1), :, k:k + 1].rearrange("p a b w -> p (a b w)")
                        if k == 0:
                            cv_dve.done(dve.tensor_scalar(tile[:, s:SEQ], source[:, 0:SEQ - s], tap(k), None, ALU.mult), f"p{s}")
                            cv_dve.done(dve.tensor_scalar(tile[:, SEQ:TOK], prev, tap(k), None, ALU.mult), f"s{k}")
                            continue
                        await_step(dve, cv_dve, f"s{k - 1}", c)
                        cv_dve.done(dve.scalar_tensor_tensor(out=tile[:, s:SEQ], in0=source[:, 0:SEQ - s], scalar=tap(k),
                                                             in1=tile[:, s:SEQ], op0=ALU.mult, op1=ALU.add), f"p{s}")
                        cv_dve.done(dve.scalar_tensor_tensor(out=tile[:, SEQ:TOK], in0=prev, scalar=tap(k),
                                                             in1=tile[:, SEQ:TOK], op0=ALU.mult, op1=ALU.add), f"s{k}")
                    await_step(dve, cv_dve, f"s{CONV_W - 2}", c)
                    cv_dve.done(dve.scalar_tensor_tensor(out=source, in0=source, scalar=tap(CONV_W - 1), in1=tile[:, :],
                                                         op0=ALU.mult, op1=ALU.add), "w3")

                def row_max(q):
                    await_step(dve, fp_pe, f"score{q}", h)
                    fp_dve.done(dve.tensor_reduce(STAT[:, q, 0:1], bank(SCORE_BANK[q], (q + 1) * P), AX, ALU.max), f"max{q}")
                    await_step(dve, fp_dve, f"max{q}", h)
                    fp_dve.done(dve.tensor_scalar(STAT[:, q, 1:2], STAT[:, q, 0:1], -1.0, None, ALU.mult), f"neg{q}")

                def normalize(q):
                    await_step(dve, fp_act, f"exp{q}", h)
                    fp_dve.done(dve.reciprocal(STAT[:, q, 3:4], STAT[:, q, 2:3]), f"rinv{q}")
                    await_step(dve, fp_dve, f"rinv{q}", h)
                    p = PROB[:, q, 0:(q + 1) * P]
                    fp_dve.done(dve.tensor_scalar(p, p, STAT[:, q, 3:4], None, ALU.mult), f"norm{q}")

                await_step(dve, fp_pe, "vtok", h)
                hold(dve, fv_stored, 16 * h + 16, 16)
                fp_dve.done(dve.tensor_copy(TB[:, 0:SEQ], bank(6)), "vtok")
                for q in range(NBLK):
                    row_max(q)
                normalize(0)
                normalize(1)
                convolve(0)
                normalize(2)
                normalize(3)
                keys(0)
                convolve(1)
                keys(1)
                convolve(2)
                await_step(dve, fp_act, "hi", h)
                fp_dve.done(dve.tensor_tensor(MOL[:, bass.ds(h, 1), 0:SEQ].rearrange("p a t -> p (a t)"), bank(4),
                                              MOH[:, bass.ds(h, 1), 0:SEQ].rearrange("p a t -> p (a t)").bitcast(F32),
                                              ALU.subtract), "lo")

            chain(dve.tensor_tensor(QKS[:, :, :], by_head(AB_Q), by_head(AB_K), ALU.mult), "qk")
            dve.wait_ge(sum_done, 4 * DEC + 1)
            chain(dve.scalar_tensor_tensor(out=SC[:, :, :, :].rearrange("p b g h -> p (b g h)"),
                                           in0=SC[:, :, :, :].rearrange("p b g h -> p (b g h)"), scalar=SCALE, in1=suf,
                                           op0=ALU.mult, op1=ALU.add), "scale")
            dve.wait_ge(fs_pe.sem, fs_pe.value("snew"))
            cn = bank(4, NDH).rearrange("p (h b) -> p b h", b=DEC)[:, :, None, :].broadcast_to([P, DEC, N_PAGES, FOX_HEADS])
            chain(dve.tensor_tensor(SC[:, :, :, :], cn, SC[:, :, :, :], ALU.add), "addcn")
            chain(dve.tensor_scalar(SN[:, :, :].rearrange("p b h -> p (b h)"), bank(4)[:, NDH:2 * NDH], SCALE, None, ALU.mult), "sn")
            chain(dve.tensor_reduce(MX[:, :, :], SC[:, :, :, :].rearrange("p b g h -> p b h g"), AX, ALU.max), "mx")
            dve.wait_ge(fs_pe.sem, fs_pe.value("turn"))
            chain(dve.tensor_reduce(MXC[:, :], bank(5)[0:NDH, 0:P], AX, ALU.max), "mxc")
            chain(dve.tensor_scalar(DG[:, :], IDENT[0:NDH, 0:NDH], MXC[:, 0:1], None, ALU.mult), "dg")
            dve.wait_ge(fs_pe.sem, fs_pe.value("max"))
            chain(dve.tensor_tensor(MX[:, :, :], bank(6, NDH).rearrange("p (b h) -> p b h", h=FOX_HEADS), SN[:, :, :], ALU.max), "m")
            chain(dve.tensor_tensor(SC[:, :, :, :], SC[:, :, :, :], over_pages(MX), ALU.subtract), "sub")
            chain(dve.tensor_tensor(SN[:, :, :], SN[:, :, :], MX[:, :, :], ALU.subtract), "subn")
            dve.wait_ge(fs_act.sem, fs_act.value("expn"))
            chain(dve.tensor_reduce(DEN[:, :, :], SC[:, :, :, :].rearrange("p b g h -> p b h g"), AX, ALU.add), "dn")
            dve.wait_ge(fs_pe.sem, fs_pe.value("den"))
            chain(dve.tensor_tensor(DEN[:, :, :], bank(7, NDH).rearrange("p (b h) -> p b h", h=FOX_HEADS), SN[:, :, :], ALU.add), "den")
            chain(dve.reciprocal(DEN[:, :, :], DEN[:, :, :]), "rinv")
            chain(dve.tensor_tensor(SC[:, :, :, :], SC[:, :, :, :], over_pages(DEN), ALU.mult), "norm")
            chain(dve.tensor_tensor(SN[:, :, :], SN[:, :, :], DEN[:, :, :], ALU.mult), "normn")
            chain(dve.tensor_tensor(OT[:, :, :].rearrange("p h b -> p b h"), by_head(AB_V), SN[:, :, :], ALU.mult), "vn")
            dve.wait_ge(ln_act.sem, ln_act.value("stdk"))
            ln_dve.done(dve.reciprocal(TA[0:NORM_ROWS, :], TA[0:NORM_ROWS, :]), "inv")
            for j in range(2 * GDN_HEADS):
                dve.wait_ge(ln_pe.sem, ln_pe.value(f"b{j}"))
                x = halves(PRJ[:, GQ + j, :])
                ln_dve.done(dve.tensor_tensor(x, ACC[1 + j % 3][:, :, 0:HALF], x, ALU.mult), f"mul{j}")
            dve.wait_ge(tails_stored, 64)
            dve.wait_ge(ln_dve.sem, ln_dve.value(f"mul{2 * GDN_HEADS - 1}"))
            dve.wait_ge(lev_in, 16)
            dve.memset(STATE[:, :, :], 0.0).then_inc(state_clear, 1)
            dve.wait_ge(state_clear, 1)
            with dve.Fori(0, NBLK) as c:
                def flat(tile):
                    return tile[:, :, :].rearrange("p h i -> p (h i)")

                def heads_of(b):
                    return bank(b).rearrange("p (h i) -> p h i", h=GDN_HEADS)

                def column(row, h):
                    return RT[:, bass.ds(c, 1), row + h:row + h + 1].rearrange("p a h -> p (a h)")

                def same(a):
                    return a[:, None, :].broadcast_to(GCH)

                await_step(dve, gl_pe, "gcb", c)
                gl_dve.done(dve.tensor_copy(XI[:, :, :], same(IDENT)), "xi")
                gl_dve.done(dve.tensor_copy(XIT[:, :, :], same(IDENT)), "xit")
                for h in range(GDN_HEADS):
                    ins = dve.tensor_scalar(GAM[:, h, :], bank(0)[:, h * P:(h + 1) * P], column(ROW_GC, h), 0.0, ALU.subtract, ALU.min)
                gl_dve.done(ins, "dt")
                gl_dve.done(dve.tensor_tensor(KDC[:, :], heads_of(0)[:, :, P - 1:P].rearrange("p h a -> p (h a)"),
                                              RT[:, bass.ds(c, 1), ROW_GC:ROW_GC + 4].rearrange("p a h -> p (a h)"), ALU.subtract), "gd")
                await_step(dve, gl_act, "gam", c)
                gl_dve.done(dve.tensor_tensor(GAM[:, :, :], GAM[:, :, :], same(INCL), ALU.mult), "gamm")
                await_step(dve, gl_pe, "bb", c)
                await_step(dve, gl_act, "kts", c)
                gl_dve.done(dve.tensor_tensor(KBT[:, :, :], heads_of(1), KTS[:, :, :], ALU.mult), "kbt")
                await_step(dve, gl_act, "eg", c)
                gl_dve.done(dve.tensor_tensor(QET[:, :, :], PRJ[:, GQ:GQ + GDN_HEADS, bass.ds(c * P, P)], EG[:, :, :], ALU.mult), "qet")
                await_step(dve, gl_pe, "a", c)
                await_step(dve, gl_dve, "gamm", c)
                gl_dve.done(dve.tensor_tensor(AT[:, :, :], heads_of(4), GAM[:, :, :], ALU.mult), "at")
                await_step(dve, gl_pe, "qk", c)
                gl_dve.done(dve.tensor_tensor(ATTN[:, :, :], heads_of(5), GAM[:, :, :], ALU.mult), "attn")
                await_step(dve, gl_act, "egc", c)
                gl_dve.done(dve.tensor_tensor(BEGE[:, :], RT[:, bass.ds(c, 1), ROW_BETA:ROW_BETA + 4].rearrange("p a h -> p (a h)"),
                                              EGC[:, :], ALU.mult), "bege")
                def by_token(tile, b, factor, name):
                    for h in range(GDN_HEADS):
                        ins = dve.tensor_scalar(tile[:, h, :], bank(b)[:, h * P:(h + 1) * P], factor(h), None, ALU.mult)
                    gl_dve.done(ins, name)

                def blocks(n):
                    gl_dve.done(dve.tensor_tensor(ATS[:, :, :], AT[:, :, :], same(LEV[:, n, :]), ALU.mult), f"ats{n}")

                await_step(dve, gl_dve, "at", c)
                blocks(0)
                await_step(dve, gl_dve, "ats0", c)
                gl_dve.done(dve.tensor_tensor(flat(XIT), flat(XIT), flat(ATS), ALU.subtract), "xt0")
                await_step(dve, gl_pe, "t0", c)
                await_step(dve, gl_dve, "xt0", c)
                blocks(1)
                gl_dve.done(dve.tensor_tensor(flat(XI), flat(XI), bank(6), ALU.subtract), "x0")
                await_step(dve, gl_dve, "bege", c)
                for n in range(1, LEVELS):
                    if n == 1:
                        by_token(VB, 3, lambda h: column(ROW_BETA, h), "vb")
                    elif n == 2:
                        by_token(KBE, 2, lambda h: BEGE[:, h:h + 1], "kbe")
                    elif n == 3:
                        by_token(KDE, 2, lambda h: KDC[:, h:h + 1], "kd")
                    await_step(dve, gl_pe, f"t{n}", c)
                    if n < LEVELS - 1:
                        blocks(n + 1)
                        await_step(dve, gl_pe, f"x{n}", c)
                        gl_dve.done(dve.tensor_tensor(flat(XI), flat(XI), bank(5), ALU.subtract), f"x{n}")
                    await_step(dve, gl_pe, f"xt{n}", c)
                    gl_dve.done(dve.tensor_tensor(flat(XIT), flat(XIT), bank(0), ALU.subtract), f"xt{n}")
                await_step(dve, gl_pe, "ws", c)
                await_step(dve, gl_act, "u", c)
                gl_dve.done(dve.tensor_tensor(flat(VNEW), flat(VNEW), bank(3), ALU.subtract), "vn")
                await_step(dve, gl_pe, "s", c)
                for h in range(GDN_HEADS):
                    ins = dve.scalar_tensor_tensor(out=STATE[:, h, :], in0=STATE[:, h, :], scalar=EG[:, h, P - 1:P],
                                                   in1=bank(5)[:, h * P:(h + 1) * P], op0=ALU.mult, op1=ALU.add)
                gl_dve.done(ins, "s")

            dve.wait_ge(vo_copied, NBLK + 1)
            chain(dve.tensor_tensor(OS[:, :, :], OS[:, :, :], OT[:, :, :], ALU.add), "add")
            dve.wait_ge(fs_act.sem, fs_act.value("hi"))
            chain(dve.tensor_tensor(MOL[:, 0:FOX_HEADS, SEQ:TOK], OS[:, :, :],
                                    MOH[:, 0:FOX_HEADS, SEQ:TOK].bitcast(F32), ALU.subtract), "lo")
            dve.wait_ge(gl_act.sem, gl_act.value("o", NBLK - 1))
            dve.wait_ge(gl_dve.sem, gl_dve.value("s", NBLK - 1))

            def new_tokens(chunk):
                return PRJ[:, chunk:chunk + GDN_HEADS, SEQ:TOK]

            def grid(a):
                return a.rearrange("p (h b) -> p h b", h=GDN_HEADS)

            def chain_g(ins, name):
                gs_dve.done(ins, name)
                dve.wait_ge(gs_dve.sem, gs_dve.value(name))

            kq = KQ[:, :, :].rearrange("p (h b) n -> p h b n", h=GDN_HEADS)
            chain_g(dve.tensor_copy(kq[:, :, :, 0], new_tokens(GK)), "kq0")
            chain_g(dve.tensor_copy(kq[:, :, :, 1], new_tokens(GQ)), "kq1")
            chain_g(dve.tensor_copy(KC[:, :, :], new_tokens(GK)), "kc")
            chain_g(dve.tensor_tensor(QKP[:, :, :], new_tokens(GK), new_tokens(GQ), ALU.mult), "qkp")
            dve.wait_ge(gs_act.sem, gs_act.value("beq"))
            read = bank(0, 2 * NJ).rearrange("p (h b n) -> p h b n", h=GDN_HEADS, n=2)
            chain_g(dve.tensor_tensor(W1[:, :, :], read[:, :, :, 0], EGS[:, :, :], ALU.mult), "a1")
            chain_g(dve.tensor_tensor(W1[:, :, :], new_tokens(GV), W1[:, :, :], ALU.subtract), "a2")
            chain_g(dve.tensor_tensor(VN2[:, :, :], W1[:, :, :], grid(BEQ[:, 0, :]), ALU.mult), "a3")
            chain_g(dve.tensor_tensor(W1[:, :, :], read[:, :, :, 1], EGS[:, :, :], ALU.mult), "o1")
            chain_g(dve.tensor_tensor(W2[:, :, :], VN2[:, :, :], grid(BEQ[:, 2, :]), ALU.mult), "o2")
            chain_g(dve.tensor_tensor(new_tokens(GQ), W1[:, :, :], W2[:, :, :], ALU.add), "o3")
            dve.wait_ge(gs_act.sem, gs_act.value("vt"))
            def own_rows(h):
                if h >= 2:
                    dve.wait_ge(gs_pe.sem, gs_pe.value(f"up{h - 2}"))
                gs_dve.done(dve.tensor_tensor(VBD[:, h % 2, :, :], VTK[:, None, :].broadcast_to([NJ, DEC, P]),
                                              IDENT[0:NJ, h * DEC:(h + 1) * DEC][:, :, None].broadcast_to([NJ, DEC, P]), ALU.mult), f"bd{h}")

            own_rows(0)
            own_rows(1)
            for h in range(GDN_HEADS):
                dve.wait_ge(gs_pe.sem, gs_pe.value(f"up{h}"))
                for b in range(DEC):
                    ins = dve.scalar_tensor_tensor(out=SS[:, h * DEC + b, :], in0=SS[:, h * DEC + b, :], scalar=EGS[:, h, b:b + 1],
                                                   in1=ACC[2 + h % 2][:, b // 4, (b % 4) * P:(b % 4 + 1) * P], op0=ALU.mult, op1=ALU.add)
                gs_dve.done(ins, f"s{h}")
                if h + 2 < GDN_HEADS:
                    own_rows(h + 2)

            dve.wait_ge(go_act.sem, go_act.value("std"))
            go_dve.done(dve.reciprocal(TA[0:NORM_ROWS, :], TA[0:NORM_ROWS, :]), "inv")
            for j in range(GDN_HEADS):
                dve.wait_ge(go_pe.sem, go_pe.value(f"b{j}"))
                go_dve.done(dve.scalar_tensor_tensor(out=halves(NRM[:, j, :]), in0=ACC[2 + j % 2][:, :, 0:HALF], scalar=PAR[:, PAR_GDN:PAR_GDN + 1],
                                                     in1=halves(PRJ[:, GQ + j, :]), op0=ALU.mult, op1=ALU.mult), f"norm{j}")
            dve.wait_ge(go_dve.sem, go_dve.value(f"norm{GDN_HEADS - 1}"))
            dve.wait_ge(cv_act, 2)
            go_dve.done(dve.tensor_tensor(NRM[:, :, :], NRM[:, :, :], PRJ[:, AB_Z:AB_Z + GDN_HEADS, :], ALU.mult), "gate")
            dve.wait_ge(go_act.sem, go_act.value("hi"))
            go_dve.done(dve.tensor_tensor(MOL[:, FOX_HEADS:, :], NRM[:, :, :], MOH[:, FOX_HEADS:, :].bitcast(F32), ALU.subtract), "lo")
            dve.wait_ge(gdn_stored, 1)
            update("ab_out", 1.0, 1)
            reciprocal(2)
            up(1)
            update("down1", 0.5)
            reciprocal(3)
            up(2)
            update("down2", 0.5)
            reciprocal(4)
            dve.wait_ge(ret_consts_in, 64)

            def ret_turn(h, p):
                first, is_first, is_last = ret_first(h), isinstance(h, int) and h == 0, isinstance(h, int) and h == RET_HEADS
                g, o = h - 1, 1 - p
                K_SCALE = float(P) ** -0.5

                def scaled(n, out):
                    hold(dve, used, RU + first + n + 3)
                    dve.tensor_tensor(halves(out), ACC[n % 2][:, :, 0:HALF], halves(RSTD[:, :]), ALU.mult).then_inc(tile_free, 1)

                def rotate(out, factor, name):
                    rp_dve.done(dve.scalar_tensor_tensor(out=out[:, :], in0=TA[:, :], scalar=factor, in1=ROPE[:, 0, :],
                                                         op0=ALU.mult, op1=ALU.mult), f"{name}c")
                    await_step(dve, rp_act, name, h)
                    rp_dve.done(dve.scalar_tensor_tensor(out=TB[:, :], in0=TB[:, :], scalar=factor, in1=ROPE[:, 1, :],
                                                         op0=ALU.mult, op1=ALU.mult), f"{name}s")
                    await_step(dve, rp_dve, f"{name}s", h)
                    rp_dve.done(dve.tensor_tensor(out[:, :], out[:, :], TB[:, :], ALU.add), name)

                def decay(kind):
                    return DECS[:, kind, bass.ds(g, 1)]

                def by_chunk(tile):
                    return tile[:, 0:SEQ].rearrange("p (n i) -> p n i", n=NBLK)

                def of_head(table):
                    return table[:, bass.ds(g, 1), :].broadcast_to([P, NBLK, P])

                def block_rows(n):
                    rm_dve.done(dve.tensor_tensor(KBLK, KVT[:, None, 0:P].broadcast_to([DEC, DEC // 2, P]),
                                                  IDENT[0:DEC, DEC // 2 * n:DEC // 2 * (n + 1)][:, :, None].broadcast_to([DEC, DEC // 2, P]),
                                                  ALU.mult), f"kb{n}")

                def state_update(n):
                    await_step(dve, rm_pe, f"r{n}", g)
                    s = SSR[:, 2 * n:2 * n + 2, :].rearrange("p b v -> p (b v)")
                    return rm_dve.done(dve.scalar_tensor_tensor(out=s, in0=s, scalar=decay(2), in1=bank(6 + n % 2), op0=ALU.mult, op1=ALU.add), f"u{n}")

                def gate_tile(v, n):
                    hold(dve, used, RU + first + n + 3)
                    rm_dve.done(dve.tensor_tensor(RGATE[:, bass.ds(2 * g + v, 1), :].rearrange("p a (n t) -> p (a n) t", n=2),
                                                  ACC[n % 2][:, :, 0:HALF], halves(RSTD[:, :]), ALU.mult), f"ga{v}")
                    await_step(dve, rm_dve, f"ga{v}", g)
                    dve.sem_inc(tile_free, 1)

                def gate(v):
                    low, gated = (t[:, bass.ds(2 * g + v, 1), :].rearrange("p a t -> p (a t)") for t in (RMOL, RGATE))
                    await_step(dve, rm_act, f"si{v}", g)
                    rm_dve.done(dve.tensor_tensor(VBH[o][:, v, :], gated, VBH[o][:, v, :], ALU.mult), f"g{v}")
                    await_step(dve, rm_act, f"hi{v}", g)
                    rm_dve.done(dve.tensor_tensor(low, VBH[o][:, v, :],
                                                  RMOH[:, bass.ds(2 * g + v, 1), :].rearrange("p a t -> p (a t)").bitcast(F32),
                                                  ALU.subtract), f"lo{v}")

                if not is_last:
                    scaled(0, TA[:, :])
                    hold(dve, tile_free, RTILE + first + 5)
                    rotate(QB[p], 1.0, "q")
                if not is_first:
                    await_step(dve, rm_pe, "a", g)
                    rm_dve.done(dve.tensor_scalar(KD_[:, :, :].rearrange("p n d -> p (n d)"), bank(4), decay(0), None, ALU.mult), "kd")
                    rm_dve.done(dve.tensor_tensor(by_chunk(ATT), bank(7).rearrange("p (n i) -> p n i", n=NBLK), of_head(DMAT), ALU.mult), "att")
                    rm_dve.done(dve.tensor_tensor(by_chunk(QB[o]), by_chunk(QB[o]), of_head(QDEC), ALU.mult), "qd")
                    rm_dve.done(dve.tensor_scalar(QSD[:, :], QB[o][:, SEQ:TOK], decay(2), None, ALU.mult), "qsd")
                    rm_dve.done(dve.tensor_tensor(QKR[:, :], QB[o][:, SEQ:TOK], KB[o][:, SEQ:TOK], ALU.mult), "qkp")
                    rm_dve.done(dve.tensor_copy(VSC[:, :, :], VBH[o][:, :, SEQ:TOK]), "vsc")
                if not is_last:
                    scaled(1, TA[:, :])
                    hold(dve, tile_free, RTILE + first + 6)
                    rotate(KB[p], K_SCALE, "k")
                if not is_first:
                    await_step(dve, rm_pe, "kv", g)
                    for n in range(NBLK):
                        kv = bank(6 + n // 2)[:, (n % 2) * RET_DV:(n % 2 + 1) * RET_DV]
                        if n == 0:
                            rm_dve.done(dve.tensor_copy(SALL[0][:, :], kv), "s0")
                            continue
                        await_step(dve, rm_dve, f"s{n - 1}", g)
                        if n == NBLK - 1:
                            hold(dve, rsp_stored, 16 * g + 16, 16)
                        rm_dve.done(dve.scalar_tensor_tensor(out=SALL[n][:, :], in0=SALL[n - 1][:, :], scalar=decay(1), in1=kv,
                                                             op0=ALU.mult, op1=ALU.add), f"s{n}")
                if not is_last:
                    scaled(2, VBH[p][:, 0, :])
                if not is_first:
                    await_step(dve, rm_pe, "cross", g)
                    read = bank(6)[:, 0:2 * DEC].rearrange("p (v b) -> p v b", v=2)
                    qk = bank(6)[:, 2 * DEC:3 * DEC][:, None, :].broadcast_to([P, 2, DEC])
                    rm_dve.done(dve.tensor_tensor(WSC[:, :, :], qk, VSC[:, :, :], ALU.mult), "ov")
                    await_step(dve, rm_dve, "ov", g)
                    rm_dve.done(dve.tensor_tensor(VBH[o][:, :, SEQ:TOK], read, WSC[:, :, :], ALU.add), "os")
                if not is_last:
                    scaled(3, VBH[p][:, 1, :])
                if not is_first:
                    await_step(dve, rm_pe, "mean", g)
                    for v in range(2):
                        out = halves(VBH[o][:, v, :])
                        rm_dve.done(dve.scalar_tensor_tensor(out=out, in0=ACC[2][:, :, 0:HALF], scalar=-1.0 / RET_DV, in1=out,
                                                             op0=ALU.mult, op1=ALU.add), f"c{v}")
                    await_step(dve, rm_act, "tk", g)
                    block_rows(0)
                    gate_tile(0, 0 if is_last else 4)
                    await_step(dve, rm_act, "std", g)
                    rm_dve.done(dve.reciprocal(TB[:, :], TB[:, :]), "inv")
                    await_step(dve, rm_dve, "inv", g)
                    for v in range(2):
                        rm_dve.done(dve.scalar_tensor_tensor(out=VBH[o][:, v, :], in0=VBH[o][:, v, :],
                                                             scalar=PAR[:, bass.ds(2 * g + PAR_RET + v, 1)], in1=TB[:, :],
                                                             op0=ALU.mult, op1=ALU.mult), f"n{v}")
                    state_update(0)
                    state_update(1)
                    block_rows(1)
                    await_step(dve, rm_dve, "n0", g)
                    gate(0)
                    gate_tile(1, 1 if is_last else 5)
                    state_update(2)
                    state_update(3)
                    await_step(dve, rm_dve, "u3", g)
                    dve.sem_inc(states_stepped, 1)
                    gate(1)

            ret_turns(dve, ret_turn)
            update("ret_out", 1.0)
            reciprocal(5)
            up(3)
            update("down3", 0.5)
            reciprocal(6)
            for d in range(KD):
                dve.scalar_tensor_tensor(out=YF[:, d, :], in0=X[:, d, :], scalar=PAR[:, PAR_FINAL + d:PAR_FINAL + d + 1],
                                         in1=RSTD[:, :], op0=ALU.mult, op1=ALU.mult).then_inc(y_ready, 1)


_INS = ["x_prompt", "x_sample", "cache_fox_k", "cache_fox_v", "cache_fox_logf", "page_table", "state_gdn_conv",
        "state_gdn_S", "state_ret_S", "norm_g", "final_norm_g", "ffn_w_gu", "ffn_w_down", "ab_w_in", "ab_w_out",
        "fox_b_f", "gdn_conv_w", "gdn_A_log", "gdn_dt_bias", "gdn_norm_g", "c_w_in", "c_w_out", "ret_norm_g"]
_OUTS = [(1, 512, 1024), (8, 1, 1024), (1, 1, 512, 4, 128), (1, 1, 512, 4, 128), (1, 1, 512, 4), (1, 8, 1, 4, 128),
         (1, 8, 1, 4, 128), (1, 8, 1, 4), (1, 1, 3, 1536), (1, 1, 4, 128, 128), (1, 8, 3, 1536), (1, 8, 4, 128, 128),
         (1, 1, 8, 128, 256), (1, 8, 8, 128, 256)]


def kernel(**inputs):
    import concourse.bacc as _bacc
    from concourse.bass_utils import run_bass_kernel_spmd as _run

    nc = _bacc.Bacc("TRN2", target_bir_lowering=False, num_devices=1)
    arrays, args = {}, []
    for name in _INS + ["shape_constants"]:
        a = shape_constants() if name == "shape_constants" else np.ascontiguousarray(inputs[name])
        arrays[f"in_{name}"] = a
        args.append(nc.dram_tensor(f"in_{name}", a.shape, mybir.dt.from_np(a.dtype), kind="ExternalInput").ap())
    for i, shape in enumerate(_OUTS):
        args.append(nc.dram_tensor(f"out_{i}", shape, F32, kind="ExternalOutput").ap())
    trunk_program(nc, *args)
    r = _run(nc, [arrays], core_ids=[0])
    return tuple(r.results[0][f"out_{i}"] for i in range(len(_OUTS)))
```
